# Optimizing a Trainium2 kernel written in Bass

```python
import jax
import jax.numpy as jnp
from jax import lax
import numpy as np

D_MODEL = 1024
BATCH = 1
SEQ = 256
DEPTH = 1

D_MIX = D_MODEL
ATTN_HEAD_DIM = 64
ATTN_HEADS = (D_MIX // 2) // ATTN_HEAD_DIM
ATTN_WIDTH = ATTN_HEADS * ATTN_HEAD_DIM
DILATED_PATTERNS = ((128, 1), (512, 4), (2048, 16))
ALIBI_MAX_BIAS = 8.0
HGRN_KEY_DIM = 128
HGRN_VAL_DIM = 128
HGRN_HEADS = (D_MIX - ATTN_WIDTH) // HGRN_VAL_DIM
HGRN_WIDTH = HGRN_HEADS * HGRN_VAL_DIM
HGRN_FDIM = HGRN_HEADS * HGRN_KEY_DIM
HGRN_CHUNK = 64
IN_SPLITS = (ATTN_WIDTH, ATTN_WIDTH, ATTN_WIDTH, HGRN_FDIM, HGRN_FDIM, HGRN_FDIM, HGRN_WIDTH, HGRN_WIDTH)
D_IN = 3 * ATTN_WIDTH + 3 * HGRN_FDIM + 2 * HGRN_WIDTH
N_EXPERTS = 16
CAPACITY_FACTOR = 2
D_FF_EXPERT = D_MODEL
NORM_EPS = 1e-6
NEG_INF = -1e30


def rms_norm(x, w):
    xf = x.astype(jnp.float32)
    y = xf * lax.rsqrt(jnp.mean(xf * xf, axis=-1, keepdims=True) + NORM_EPS)
    return (y * w.astype(jnp.float32)).astype(x.dtype)

def alibi_slopes(n_heads):
    return jnp.exp2(-ALIBI_MAX_BIAS * jnp.arange(1, n_heads + 1, dtype=jnp.float32) / n_heads)

def dilated_window_attention(q, k, v, window, dilation, slopes):
    B, S, H, Dh = q.shape
    half = window // (2 * dilation)
    blk = half
    span = dilation * blk
    Sp = -(-S // span) * span
    L = Sp // dilation
    nb = L // blk

    def to_sub(t):
        t = jnp.pad(t, ((0, 0), (0, Sp - S), (0, 0), (0, 0)))
        return t.reshape(B, L, dilation, H, Dh).transpose(0, 2, 1, 3, 4)

    def windows(t):
        t = jnp.pad(t, ((0, 0), (0, 0), (blk, blk), (0, 0), (0, 0))).reshape(B, dilation, nb + 2, blk, H, Dh)
        return jnp.concatenate([t[:, :, :-2], t[:, :, 1:-1], t[:, :, 2:]], axis=3)

    qs = to_sub(q).reshape(B, dilation, nb, blk, H, Dh)
    ks = windows(to_sub(k))
    vs = windows(to_sub(v))

    qi = jnp.arange(blk)
    kj = jnp.arange(3 * blk)
    delta = kj[None, :] - blk - qi[:, None]
    band = jnp.abs(delta) <= half
    l_k = jnp.arange(nb)[:, None] * blk - blk + kj[None, :]
    pos_k = l_k[None] * dilation + jnp.arange(dilation)[:, None, None]
    key_ok = (l_k[None] >= 0) & (pos_k < S)
    mask = band[None, None, None] & key_ok[:, :, None, None, :]
    bias = -slopes[:, None, None] * (dilation * jnp.abs(delta)).astype(jnp.float32)[None]

    s = jnp.einsum('brnqhd,brnkhd->brnhqk', qs, ks)
    s = jnp.where(mask, s + bias, NEG_INF)
    m = jnp.max(s, axis=-1, keepdims=True)
    e = jnp.exp(s - m)
    den = jnp.sum(e, axis=-1)
    num = jnp.einsum('brnhqk,brnkhd->brnqhd', e, vs)

    def back_stat(t):
        t = t.transpose(0, 1, 2, 4, 3).reshape(B, dilation, L, H)
        return t.transpose(0, 2, 1, 3).reshape(B, Sp, H)[:, :S]

    num = num.reshape(B, dilation, L, H, Dh).transpose(0, 2, 1, 3, 4).reshape(B, Sp, H, Dh)[:, :S]
    return back_stat(m[..., 0]), back_stat(den), num

def dilated_attention_mixer(q, k, v, q_norm_w, k_norm_w):
    B, S, _ = q.shape
    shp = (B, S, ATTN_HEADS, ATTN_HEAD_DIM)
    qh = rms_norm(q.reshape(shp), q_norm_w).astype(jnp.float32) * (ATTN_HEAD_DIM ** -0.5)
    kh = rms_norm(k.reshape(shp), k_norm_w).astype(jnp.float32)
    vh = v.reshape(shp).astype(jnp.float32)
    slopes = alibi_slopes(ATTN_HEADS)
    ms, dens, nums = [], [], []
    for window, dilation in DILATED_PATTERNS:
        m, den, num = dilated_window_attention(qh, kh, vh, window, dilation, slopes)
        ms.append(m)
        dens.append(den)
        nums.append(num)
    m_all = jnp.stack(ms)
    scale = jnp.exp(m_all - jnp.max(m_all, axis=0, keepdims=True))
    numer = jnp.sum(scale[..., None] * jnp.stack(nums), axis=0)
    denom = jnp.sum(scale * jnp.stack(dens), axis=0)
    return (numer / denom[..., None]).reshape(B, S, ATTN_WIDTH)

def chunked_gated_recurrence(q, k, v, log_f):
    B, S, H, Dk = q.shape
    Dv = v.shape[-1]
    C = HGRN_CHUNK
    n = S // C

    def to_chunks(t):
        return t.reshape(B, n, C, H, t.shape[-1]).transpose(1, 0, 3, 2, 4)

    incl = jnp.tril(jnp.ones((C, C), dtype=bool))[:, :, None]

    def step(state, inp):
        qb, kb, vb, gb = inp
        b = jnp.cumsum(gb, axis=2)
        o_inter = jnp.einsum('bhck,bhkv->bhcv', qb * jnp.exp(b), state)
        diff = b[:, :, :, None, :] - b[:, :, None, :, :]
        decay = jnp.exp(jnp.where(incl, diff, -jnp.inf))
        a = jnp.einsum('bhtk,bhsk,bhtsk->bhts', qb, kb, decay)
        o_intra = jnp.einsum('bhts,bhsv->bhtv', a, vb)
        b_last = b[:, :, -1:, :]
        k_dec = kb * jnp.exp(b_last - b)
        state = jnp.exp(b_last[:, :, 0, :])[..., None] * state + jnp.einsum('bhsk,bhsv->bhkv', k_dec, vb)
        return state, o_inter + o_intra

    init = jnp.zeros((B, H, Dk, Dv), jnp.float32)
    _, out = lax.scan(step, init, (to_chunks(q), to_chunks(k), to_chunks(v), to_chunks(log_f)))
    return out.transpose(1, 0, 3, 2, 4).reshape(B, S, H, Dv)

def hgrn2_mixer(q, f_fwd, f_bwd, i, g, lb_fwd, lb_bwd, out_norm_w):
    B, S, _ = q.shape

    def heads(t, d):
        return t.reshape(B, S, HGRN_HEADS, d).astype(jnp.float32)

    qh = jax.nn.silu(heads(q, HGRN_KEY_DIM))
    vh = heads(i, HGRN_VAL_DIM)

    def gates(f_raw, lb):
        lb = lb.reshape(HGRN_HEADS, HGRN_KEY_DIM)
        z = heads(f_raw, HGRN_KEY_DIM)
        f = lb + (1.0 - lb) * jax.nn.sigmoid(z)
        return (1.0 - lb) * jax.nn.sigmoid(-z), jnp.log(f)

    k_f, lf_f = gates(f_fwd, lb_fwd)
    k_b, lf_b = gates(f_bwd, lb_bwd)
    o_f = chunked_gated_recurrence(qh, k_f, vh, lf_f)
    flip = lambda t: jnp.flip(t, axis=1)
    o_b = flip(chunked_gated_recurrence(flip(qh), flip(k_b), flip(vh), flip(lf_b)))
    o = rms_norm(o_f + o_b, out_norm_w) * jax.nn.silu(heads(g, HGRN_VAL_DIM))
    return o.reshape(B, S, HGRN_WIDTH)

def expert_choice_moe(h, w_router, w_gate, w_up, w_down):
    B, S, D = h.shape
    cap = max(1, CAPACITY_FACTOR * S // N_EXPERTS)
    logits = jnp.einsum('bsd,de->bse', h, w_router).astype(jnp.float32)
    aff = jax.nn.softmax(logits, axis=-1)
    gate, idx = lax.top_k(aff.transpose(0, 2, 1), cap)
    xin = jax.vmap(lambda hb, ib: hb[ib])(h, idx)
    hid = jax.nn.silu(jnp.einsum('becd,edf->becf', xin, w_gate)) * jnp.einsum('becd,edf->becf', xin, w_up)
    y = jnp.einsum('becf,efd->becd', hid, w_down) * gate[..., None].astype(h.dtype)
    bidx = jnp.arange(B)[:, None, None]
    return jnp.zeros_like(h).at[bidx, idx].add(y)

def first_inputs(seed: int = 0) -> dict:
    key = jax.random.key(seed)
    ks = jax.random.split(key, 16)
    f32 = jnp.float32
    nrm = lambda k, shape, fan_in: jax.random.normal(k, shape, f32) * (fan_in ** -0.5)
    gain = lambda k, shape: 1.0 + 0.02 * jax.random.normal(k, shape, f32)
    return {
        "x": jax.random.normal(ks[0], (BATCH, SEQ, D_MODEL), f32),
        "norm1_w": gain(ks[1], (DEPTH, D_MODEL)),
        "w_in": nrm(ks[2], (DEPTH, D_MODEL, D_IN), D_MODEL),
        "attn_q_norm_w": gain(ks[3], (DEPTH, ATTN_HEAD_DIM)),
        "attn_k_norm_w": gain(ks[4], (DEPTH, ATTN_HEAD_DIM)),
        "hgrn_lb_fwd": 1.0 + 0.1 * jax.random.normal(ks[5], (DEPTH + 1, HGRN_FDIM), f32),
        "hgrn_lb_bwd": 1.0 + 0.1 * jax.random.normal(ks[6], (DEPTH + 1, HGRN_FDIM), f32),
        "hgrn_out_norm_w": gain(ks[7], (DEPTH, HGRN_VAL_DIM)),
        "w_out": nrm(ks[8], (DEPTH, D_MIX, D_MODEL), D_MIX),
        "norm2_w": gain(ks[9], (DEPTH, D_MODEL)),
        "w_router": nrm(ks[10], (DEPTH, D_MODEL, N_EXPERTS), D_MODEL),
        "w_expert_gate": nrm(ks[11], (DEPTH, N_EXPERTS, D_MODEL, D_FF_EXPERT), D_MODEL),
        "w_expert_up": nrm(ks[12], (DEPTH, N_EXPERTS, D_MODEL, D_FF_EXPERT), D_MODEL),
        "w_expert_down": nrm(ks[13], (DEPTH, N_EXPERTS, D_FF_EXPERT, D_MODEL), D_FF_EXPERT),
    }

def first_block(x, norm1_w, w_in, attn_q_norm_w, attn_k_norm_w, hgrn_lb_fwd, hgrn_lb_bwd,
              hgrn_out_norm_w, w_out, norm2_w, w_router, w_expert_gate, w_expert_up, w_expert_down):
    lb_f_all = jnp.cumsum(jax.nn.softmax(hgrn_lb_fwd.astype(jnp.float32), axis=0), axis=0)
    lb_b_all = jnp.cumsum(jax.nn.softmax(hgrn_lb_bwd.astype(jnp.float32), axis=0), axis=0)
    split_at = np.cumsum(IN_SPLITS)[:-1].tolist()
    for l in range(DEPTH):
        h = rms_norm(x, norm1_w[l])
        proj = jnp.einsum('bsd,de->bse', h, w_in[l])
        aq, ak, av, hq, hf_f, hf_b, hi, hg = jnp.split(proj, split_at, axis=-1)
        a_out = dilated_attention_mixer(aq, ak, av, attn_q_norm_w[l], attn_k_norm_w[l])
        b_out = hgrn2_mixer(hq, hf_f, hf_b, hi, hg, lb_f_all[l], lb_b_all[l], hgrn_out_norm_w[l])
        mixed = jnp.concatenate([a_out.astype(x.dtype), b_out.astype(x.dtype)], axis=-1)
        x = x + jnp.einsum('bsm,md->bsd', mixed, w_out[l])
        x = x + expert_choice_moe(rms_norm(x, norm2_w[l]), w_router[l], w_expert_gate[l],
                                  w_expert_up[l], w_expert_down[l])
    return x


HEAD_DIM = 64
D_RWKV = D_MODEL // 2
RWKV_HEADS = D_RWKV // HEAD_DIM
DECAY_LORA = 64
ICL_LORA = 64
GATE_LORA = 128
RWKV_GN_EPS = 64e-5
D_MOBA = D_MODEL // 2
MOBA_HEADS = D_MOBA // HEAD_DIM
MOBA_BLOCK = 256
MOBA_TOPK = 3
MOBA_Q_CHUNK = 32
D_SSM = D_MODEL // 2
SSM_GROUP = 16
SSM_GROUPS = D_SSM // SSM_GROUP
SSM_STATE = 64
N_BRANCHES = 3
N_EXPERT_GROUPS = 4
EXPERTS_PER_GROUP = 8
N_EXPERTS_2 = N_EXPERT_GROUPS * EXPERTS_PER_GROUP
EXPERT_TOPK = 2
D_EXPERT = D_MODEL // 4
MOE_BLOCK = 512
LN_EPS = 1e-5
DEEPNORM_ALPHA = (2 * DEPTH) ** 0.25
DEEPNORM_BETA = (8 * DEPTH) ** -0.25
NEG_INF_2 = -1e30
RWKV_COLS = 3 * D_RWKV + DECAY_LORA + ICL_LORA + GATE_LORA
MOBA_COLS = 3 * D_MOBA
OFF_MOBA = RWKV_COLS
OFF_SSM = OFF_MOBA + MOBA_COLS
OFF_GATE = OFF_SSM + D_SSM
D_IN_PROJ = OFF_GATE + N_BRANCHES * D_MODEL


def layer_norm(x, w, b):
    xf = x.astype(jnp.float32)
    mu = jnp.mean(xf, -1, keepdims=True)
    var = jnp.mean(jnp.square(xf - mu), -1, keepdims=True)
    y = (xf - mu) * lax.rsqrt(var + LN_EPS) * w.astype(jnp.float32) + b.astype(jnp.float32)
    return y.astype(x.dtype)

def wkv7_scan(r, w, k, v, a, b):
    Bsz, L, H, N = r.shape

    def step(S, inp):
        r_t, w_t, k_t, v_t, a_t, b_t = inp
        sa = jnp.einsum('bhij,bhj->bhi', S, a_t)
        S = S * w_t[:, :, None, :] + sa[..., None] * b_t[:, :, None, :] + v_t[..., None] * k_t[:, :, None, :]
        return S, jnp.einsum('bhij,bhj->bhi', S, r_t)

    xs = tuple(jnp.moveaxis(t, 1, 0) for t in (r, w, k, v, a, b))
    S0 = jnp.zeros((Bsz, H, N, N), jnp.float32)
    _, y = lax.scan(step, S0, xs)
    return jnp.moveaxis(y, 0, 1)

def rwkv7_mixer(z, mu, w0, w2, a0, a2, g2, k_k, k_a, r_k, ln_w, ln_b):
    f32 = jnp.float32
    Bsz, L, _ = z.shape
    z = z.astype(f32)
    z_prev = jnp.pad(z, ((0, 0), (1, 0), (0, 0)))[:, :-1]
    z = z + (z_prev - z) * mu.astype(f32)
    cuts = np.cumsum([D_RWKV, D_RWKV, D_RWKV, DECAY_LORA, ICL_LORA]).tolist()
    r, k, v, xw, xa, xg = jnp.split(z, cuts, axis=-1)
    w_log = -jax.nn.softplus(-(w0.astype(f32) + jnp.tanh(xw) @ w2.astype(f32))) - 0.5
    decay = jnp.exp(-jnp.exp(w_log))
    a = jax.nn.sigmoid(a0.astype(f32) + xa @ a2.astype(f32))
    g = jax.nn.sigmoid(xg) @ g2.astype(f32)

    def heads(t):
        return t.reshape(Bsz, L, RWKV_HEADS, HEAD_DIM)

    kk = heads(k * k_k.astype(f32))
    kk = kk * lax.rsqrt(jnp.maximum(jnp.sum(kk * kk, -1, keepdims=True), 1e-24))
    k = k * (1.0 + (a - 1.0) * k_a.astype(f32))
    rh, kh, vh, ah = heads(r), heads(k), heads(v), heads(a)
    y = wkv7_scan(rh, heads(decay), kh, vh, -kk, kk * ah)
    mean = jnp.mean(y, -1, keepdims=True)
    var = jnp.mean(jnp.square(y - mean), -1, keepdims=True)
    y = ((y - mean) * lax.rsqrt(var + RWKV_GN_EPS)).reshape(Bsz, L, D_RWKV)
    y = y * ln_w.astype(f32) + ln_b.astype(f32)
    bonus = jnp.sum(rh * kh * r_k.astype(f32), -1, keepdims=True) * vh
    return (y + bonus.reshape(Bsz, L, D_RWKV)) * g

def alibi_slopes_2(n_heads):
    return 2.0 ** (-8.0 * jnp.arange(1, n_heads + 1, dtype=jnp.float32) / n_heads)

def moba_attention(q, k, v):
    f32 = jnp.float32
    Bsz, L, H, Dh = q.shape
    n_blk = -(-L // MOBA_BLOCK)
    Lp = n_blk * MOBA_BLOCK
    k_sel = min(MOBA_TOPK, n_blk)
    pad = ((0, 0), (0, Lp - L), (0, 0), (0, 0))
    q = jnp.pad(q, pad) * (Dh ** -0.5)
    kbt = jnp.pad(k, pad).reshape(Bsz, n_blk, MOBA_BLOCK, H, Dh).transpose(0, 3, 1, 2, 4)
    vbt = jnp.pad(v, pad).reshape(Bsz, n_blk, MOBA_BLOCK, H, Dh).transpose(0, 3, 1, 2, 4)
    kmean = jnp.mean(kbt.astype(f32), axis=3)
    n_chunk = Lp // MOBA_Q_CHUNK
    qc = q.reshape(Bsz, n_chunk, MOBA_Q_CHUNK, H, Dh).transpose(1, 0, 3, 2, 4)
    slopes = alibi_slopes_2(H)
    bi = jnp.arange(Bsz)[:, None, None, None]
    hi = jnp.arange(H)[None, :, None, None]
    blk_ids = jnp.arange(n_blk)
    offs = jnp.arange(MOBA_BLOCK)

    def one_chunk(args):
        c, qb = args
        q0 = c * MOBA_Q_CHUNK
        blk = q0 // MOBA_BLOCK
        tpos = q0 + jnp.arange(MOBA_Q_CHUNK)
        gate = jnp.einsum('bhqd,bhnd->bhqn', qb.astype(f32), kmean)
        gate = jnp.where(blk_ids < blk, gate, -jnp.inf)
        _, idx = lax.top_k(gate, k_sel)
        valid = idx < blk
        kg = kbt[bi, hi, idx]
        vg = vbt[bi, hi, idx]
        s_sel = jnp.einsum('bhqd,bhqknd->bhqkn', qb, kg, preferred_element_type=f32)
        spos = idx[..., None] * MOBA_BLOCK + offs
        s_sel = s_sel - slopes[:, None, None, None] * (tpos[:, None, None] - spos).astype(f32)
        s_sel = jnp.where(valid[..., None], s_sel, NEG_INF_2)
        k_own = lax.dynamic_index_in_dim(kbt, blk, axis=2, keepdims=False)
        v_own = lax.dynamic_index_in_dim(vbt, blk, axis=2, keepdims=False)
        s_own = jnp.einsum('bhqd,bhnd->bhqn', qb, k_own, preferred_element_type=f32)
        dist = tpos[:, None] - (blk * MOBA_BLOCK + offs)[None, :]
        s_own = jnp.where(dist >= 0, s_own - slopes[:, None, None] * dist.astype(f32), NEG_INF_2)
        s = jnp.concatenate([s_sel.reshape(Bsz, H, MOBA_Q_CHUNK, k_sel * MOBA_BLOCK), s_own], -1)
        p = jax.nn.softmax(s, axis=-1)
        p_sel = p[..., :k_sel * MOBA_BLOCK].reshape(Bsz, H, MOBA_Q_CHUNK, k_sel, MOBA_BLOCK).astype(vg.dtype)
        p_own = p[..., k_sel * MOBA_BLOCK:].astype(v_own.dtype)
        return (jnp.einsum('bhqkn,bhqknd->bhqd', p_sel, vg)
                + jnp.einsum('bhqn,bhnd->bhqd', p_own, v_own))

    out = lax.map(one_chunk, (jnp.arange(n_chunk), qc))
    return out.transpose(1, 0, 3, 2, 4).reshape(Bsz, Lp, H * Dh)[:, :L]

def _complex_affine_combine(e1, e2):
    ar1, ai1, br1, bi1 = e1
    ar2, ai2, br2, bi2 = e2
    return (ar2 * ar1 - ai2 * ai1, ar2 * ai1 + ai2 * ar1,
            ar2 * br1 - ai2 * bi1 + br2, ar2 * bi1 + ai2 * br1 + bi2)

def s5_mixer(u, a_re, a_im, b_re, b_im, c_re, c_im, d, log_dt, glu_w, glu_b):
    f32 = jnp.float32
    Bsz, L, _ = u.shape
    u = u.astype(f32)
    a_re = a_re.astype(f32)
    a_im = a_im.astype(f32)
    dt = jnp.exp(log_dt.astype(f32))[:, None]
    mag = jnp.exp(a_re * dt)
    lam_re = mag * jnp.cos(a_im * dt)
    lam_im = mag * jnp.sin(a_im * dt)
    den = a_re * a_re + a_im * a_im
    nr = lam_re - 1.0
    coef_re = (nr * a_re + lam_im * a_im) / den
    coef_im = (lam_im * a_re - nr * a_im) / den
    b_re = b_re.astype(f32)
    b_im = b_im.astype(f32)
    bb_re = coef_re[..., None] * b_re - coef_im[..., None] * b_im
    bb_im = coef_re[..., None] * b_im + coef_im[..., None] * b_re
    ug = u.reshape(Bsz, L, SSM_GROUPS, SSM_GROUP)
    bu_re = jnp.einsum('blgh,gph->blgp', ug, bb_re)
    bu_im = jnp.einsum('blgh,gph->blgp', ug, bb_im)
    lr = jnp.broadcast_to(lam_re, bu_re.shape)
    li = jnp.broadcast_to(lam_im, bu_re.shape)
    _, _, h_re, h_im = lax.associative_scan(_complex_affine_combine, (lr, li, bu_re, bu_im), axis=1)
    y = (jnp.einsum('blgp,ghp->blgh', h_re, c_re.astype(f32))
         - jnp.einsum('blgp,ghp->blgh', h_im, c_im.astype(f32)))
    y = y.reshape(Bsz, L, D_SSM) + d.astype(f32) * u
    y = jax.nn.gelu(y)
    zg = y @ glu_w.astype(f32) + glu_b.astype(f32)
    return zg[..., :D_SSM] * jax.nn.sigmoid(zg[..., D_SSM:])

def hybrid_mixer(x, w_in, rwkv_mu, rwkv_w0, rwkv_w2, rwkv_a0, rwkv_a2, rwkv_g2, rwkv_k_k, rwkv_k_a,
                 rwkv_r_k, rwkv_ln_w, rwkv_ln_b, ssm_a_re, ssm_a_im, ssm_b_re, ssm_b_im, ssm_c_re,
                 ssm_c_im, ssm_d, ssm_log_dt, ssm_glu_w, ssm_glu_b, w_up_rwkv, w_up_moba, w_up_ssm,
                 gate_b, w_out):
    Bsz, L, _ = x.shape
    proj = x @ w_in
    y_a = rwkv7_mixer(proj[..., :OFF_MOBA], rwkv_mu, rwkv_w0, rwkv_w2, rwkv_a0, rwkv_a2, rwkv_g2,
                      rwkv_k_k, rwkv_k_a, rwkv_r_k, rwkv_ln_w, rwkv_ln_b).astype(x.dtype)
    q, k, v = jnp.split(proj[..., OFF_MOBA:OFF_SSM], 3, axis=-1)

    def heads(t):
        return t.reshape(Bsz, L, MOBA_HEADS, HEAD_DIM)

    y_b = moba_attention(heads(q), heads(k), heads(v))
    y_c = s5_mixer(proj[..., OFF_SSM:OFF_GATE], ssm_a_re, ssm_a_im, ssm_b_re, ssm_b_im, ssm_c_re,
                   ssm_c_im, ssm_d, ssm_log_dt, ssm_glu_w, ssm_glu_b).astype(x.dtype)
    gates = jax.nn.sigmoid(proj[..., OFF_GATE:] + gate_b).reshape(Bsz, L, N_BRANCHES, D_MODEL)
    merged = (gates[..., 0, :] * (y_a @ w_up_rwkv)
              + gates[..., 1, :] * (y_b @ w_up_moba)
              + gates[..., 2, :] * (y_c @ w_up_ssm))
    return merged @ w_out

def hier_moe(x, router_group_w, router_group_b, router_expert_w, router_expert_b,
             expert_w_gate, expert_w_up, expert_w_down):
    f32 = jnp.float32
    Bsz, L, D = x.shape
    T = Bsz * L
    TK = T * EXPERT_TOPK
    xt = x.reshape(T, D)
    xf = xt.astype(f32)
    g_logits = xf @ router_group_w.astype(f32) + router_group_b.astype(f32)
    g_sel = jnp.argmax(g_logits, axis=-1)
    p_group = jnp.take_along_axis(jax.nn.softmax(g_logits, -1), g_sel[:, None], axis=-1)
    e_logits = (xf @ router_expert_w.astype(f32) + router_expert_b.astype(f32)).reshape(
        T, N_EXPERT_GROUPS, EXPERTS_PER_GROUP)
    e_logits = jnp.take_along_axis(e_logits, g_sel[:, None, None], axis=1)[:, 0]
    top_logit, top_local = lax.top_k(e_logits, EXPERT_TOPK)
    weight = p_group * jax.nn.softmax(top_logit, axis=-1)
    expert = g_sel[:, None] * EXPERTS_PER_GROUP + top_local
    flat_e = expert.reshape(TK)
    order = jnp.argsort(flat_e)
    e_sorted = flat_e[order]
    tok_sorted = order // EXPERT_TOPK
    counts = jnp.bincount(flat_e, length=N_EXPERTS_2)
    starts = jnp.cumsum(counts) - counts
    padded = (counts + MOE_BLOCK - 1) // MOE_BLOCK * MOE_BLOCK
    p_ends = jnp.cumsum(padded)
    p_starts = p_ends - padded
    dest = p_starts[e_sorted] + jnp.arange(TK) - starts[e_sorted]
    n_blocks = -(-TK // MOE_BLOCK) + N_EXPERTS_2
    buf = jnp.zeros((n_blocks * MOE_BLOCK, D), x.dtype).at[dest].set(xt[tok_sorted])
    blk_e = jnp.minimum(jnp.searchsorted(p_ends, jnp.arange(n_blocks) * MOE_BLOCK, side='right'),
                        N_EXPERTS_2 - 1)
    xb = buf.reshape(n_blocks, MOE_BLOCK, D)
    hid = (jax.nn.silu(jnp.einsum('nbd,ndf->nbf', xb, expert_w_gate[blk_e]))
           * jnp.einsum('nbd,ndf->nbf', xb, expert_w_up[blk_e]))
    yb = jnp.einsum('nbf,nfd->nbd', hid, expert_w_down[blk_e]).reshape(n_blocks * MOE_BLOCK, D)
    w_sorted = weight.reshape(TK)[order].astype(x.dtype)
    y = jnp.zeros((T, D), x.dtype).at[tok_sorted].add(yb[dest] * w_sorted[:, None])
    return y.reshape(Bsz, L, D)

def second_inputs(seed: int = 0) -> dict:
    key = jax.random.key(seed)
    keys = iter(jax.random.split(key, 48))
    f32 = jnp.float32

    def nrm(shape, scale):
        return scale * jax.random.normal(next(keys), shape, f32)

    def near(shape, center, spread):
        return center + spread * jax.random.normal(next(keys), shape, f32)

    Ld = DEPTH
    ratio = jnp.arange(D_RWKV, dtype=f32) / (D_RWKV - 1)
    w0_base = -7.0 + 5.0 * ratio ** 0.85 + 0.5
    a_im_base = jnp.pi * jnp.arange(SSM_STATE, dtype=f32)
    return {
        'x': nrm((BATCH, SEQ, D_MODEL), 1.0),
        'w_in': nrm((Ld, D_MODEL, D_IN_PROJ), D_MODEL ** -0.5),
        'rwkv_mu': jax.random.uniform(next(keys), (Ld, RWKV_COLS), f32),
        'rwkv_w0': w0_base + nrm((Ld, D_RWKV), 0.1),
        'rwkv_w2': nrm((Ld, DECAY_LORA, D_RWKV), 0.5 * DECAY_LORA ** -0.5),
        'rwkv_a0': nrm((Ld, D_RWKV), 0.1),
        'rwkv_a2': nrm((Ld, ICL_LORA, D_RWKV), ICL_LORA ** -0.5),
        'rwkv_g2': nrm((Ld, GATE_LORA, D_RWKV), GATE_LORA ** -0.5),
        'rwkv_k_k': near((Ld, D_RWKV), 0.85, 0.05),
        'rwkv_k_a': near((Ld, D_RWKV), 1.0, 0.05),
        'rwkv_r_k': nrm((Ld, RWKV_HEADS, HEAD_DIM), 0.1),
        'rwkv_ln_w': near((Ld, D_RWKV), 1.0, 0.05),
        'rwkv_ln_b': nrm((Ld, D_RWKV), 0.02),
        'ssm_a_re': near((Ld, SSM_GROUPS, SSM_STATE), -0.5, 0.01),
        'ssm_a_im': jnp.broadcast_to(a_im_base, (Ld, SSM_GROUPS, SSM_STATE)) + nrm((Ld, SSM_GROUPS, SSM_STATE), 0.01),
        'ssm_b_re': nrm((Ld, SSM_GROUPS, SSM_STATE, SSM_GROUP), (2 * SSM_GROUP) ** -0.5),
        'ssm_b_im': nrm((Ld, SSM_GROUPS, SSM_STATE, SSM_GROUP), (2 * SSM_GROUP) ** -0.5),
        'ssm_c_re': nrm((Ld, SSM_GROUPS, SSM_GROUP, SSM_STATE), 0.5),
        'ssm_c_im': nrm((Ld, SSM_GROUPS, SSM_GROUP, SSM_STATE), 0.5),
        'ssm_d': nrm((Ld, D_SSM), 1.0),
        'ssm_log_dt': jax.random.uniform(next(keys), (Ld, SSM_GROUPS), f32,
                                         minval=float(np.log(1e-3)), maxval=float(np.log(1e-1))),
        'ssm_glu_w': nrm((Ld, D_SSM, 2 * D_SSM), D_SSM ** -0.5),
        'ssm_glu_b': nrm((Ld, 2 * D_SSM), 0.02),
        'w_up_rwkv': nrm((Ld, D_RWKV, D_MODEL), D_RWKV ** -0.5),
        'w_up_moba': nrm((Ld, D_MOBA, D_MODEL), D_MOBA ** -0.5),
        'w_up_ssm': nrm((Ld, D_SSM, D_MODEL), D_SSM ** -0.5),
        'gate_b': nrm((Ld, N_BRANCHES * D_MODEL), 0.1),
        'w_out': nrm((Ld, D_MODEL, D_MODEL), DEEPNORM_BETA * D_MODEL ** -0.5),
        'ln1_w': near((Ld, D_MODEL), 1.0, 0.05),
        'ln1_b': nrm((Ld, D_MODEL), 0.02),
        'router_group_w': nrm((Ld, D_MODEL, N_EXPERT_GROUPS), D_MODEL ** -0.5),
        'router_group_b': nrm((Ld, N_EXPERT_GROUPS), 0.01),
        'router_expert_w': nrm((Ld, D_MODEL, N_EXPERTS_2), D_MODEL ** -0.5),
        'router_expert_b': nrm((Ld, N_EXPERTS_2), 0.01),
        'expert_w_gate': nrm((Ld, N_EXPERTS_2, D_MODEL, D_EXPERT), D_MODEL ** -0.5),
        'expert_w_up': nrm((Ld, N_EXPERTS_2, D_MODEL, D_EXPERT), D_MODEL ** -0.5),
        'expert_w_down': nrm((Ld, N_EXPERTS_2, D_EXPERT, D_MODEL), DEEPNORM_BETA * D_EXPERT ** -0.5),
        'ln2_w': near((Ld, D_MODEL), 1.0, 0.05),
        'ln2_b': nrm((Ld, D_MODEL), 0.02),
    }

def second_block(x, w_in, rwkv_mu, rwkv_w0, rwkv_w2, rwkv_a0, rwkv_a2, rwkv_g2, rwkv_k_k, rwkv_k_a,
              rwkv_r_k, rwkv_ln_w, rwkv_ln_b, ssm_a_re, ssm_a_im, ssm_b_re, ssm_b_im, ssm_c_re,
              ssm_c_im, ssm_d, ssm_log_dt, ssm_glu_w, ssm_glu_b, w_up_rwkv, w_up_moba, w_up_ssm,
              gate_b, w_out, ln1_w, ln1_b, router_group_w, router_group_b, router_expert_w,
              router_expert_b, expert_w_gate, expert_w_up, expert_w_down, ln2_w, ln2_b):
    for l in range(DEPTH):
        h = hybrid_mixer(x, w_in[l], rwkv_mu[l], rwkv_w0[l], rwkv_w2[l], rwkv_a0[l], rwkv_a2[l],
                         rwkv_g2[l], rwkv_k_k[l], rwkv_k_a[l], rwkv_r_k[l], rwkv_ln_w[l], rwkv_ln_b[l],
                         ssm_a_re[l], ssm_a_im[l], ssm_b_re[l], ssm_b_im[l], ssm_c_re[l], ssm_c_im[l],
                         ssm_d[l], ssm_log_dt[l], ssm_glu_w[l], ssm_glu_b[l], w_up_rwkv[l],
                         w_up_moba[l], w_up_ssm[l], gate_b[l], w_out[l])
        x = layer_norm(DEEPNORM_ALPHA * x + h, ln1_w[l], ln1_b[l])
        h = hier_moe(x, router_group_w[l], router_group_b[l], router_expert_w[l], router_expert_b[l],
                     expert_w_gate[l], expert_w_up[l], expert_w_down[l])
        x = layer_norm(DEEPNORM_ALPHA * x + h, ln2_w[l], ln2_b[l])
    return x


def setup_inputs(seed=0):
    out = dict(first_inputs(seed))
    for name, value in second_inputs(seed + 1).items():
        if name != "x":
            out[name + "_2"] = value
    return out


def reference(
    x, norm1_w, w_in, attn_q_norm_w, attn_k_norm_w, hgrn_lb_fwd, hgrn_lb_bwd, hgrn_out_norm_w,
    w_out, norm2_w, w_router, w_expert_gate, w_expert_up, w_expert_down, w_in_2, rwkv_mu_2,
    rwkv_w0_2, rwkv_w2_2, rwkv_a0_2, rwkv_a2_2, rwkv_g2_2, rwkv_k_k_2, rwkv_k_a_2, rwkv_r_k_2,
    rwkv_ln_w_2, rwkv_ln_b_2, ssm_a_re_2, ssm_a_im_2, ssm_b_re_2, ssm_b_im_2, ssm_c_re_2,
    ssm_c_im_2, ssm_d_2, ssm_log_dt_2, ssm_glu_w_2, ssm_glu_b_2, w_up_rwkv_2, w_up_moba_2,
    w_up_ssm_2, gate_b_2, w_out_2, ln1_w_2, ln1_b_2, router_group_w_2, router_group_b_2,
    router_expert_w_2, router_expert_b_2, expert_w_gate_2, expert_w_up_2, expert_w_down_2,
    ln2_w_2, ln2_b_2,
):
    x = first_block(
        x, norm1_w, w_in, attn_q_norm_w, attn_k_norm_w, hgrn_lb_fwd, hgrn_lb_bwd,
        hgrn_out_norm_w, w_out, norm2_w, w_router, w_expert_gate, w_expert_up, w_expert_down,
    )
    return second_block(
        x, w_in_2, rwkv_mu_2, rwkv_w0_2, rwkv_w2_2, rwkv_a0_2, rwkv_a2_2, rwkv_g2_2, rwkv_k_k_2,
        rwkv_k_a_2, rwkv_r_k_2, rwkv_ln_w_2, rwkv_ln_b_2, ssm_a_re_2, ssm_a_im_2, ssm_b_re_2,
        ssm_b_im_2, ssm_c_re_2, ssm_c_im_2, ssm_d_2, ssm_log_dt_2, ssm_glu_w_2, ssm_glu_b_2,
        w_up_rwkv_2, w_up_moba_2, w_up_ssm_2, gate_b_2, w_out_2, ln1_w_2, ln1_b_2,
        router_group_w_2, router_group_b_2, router_expert_w_2, router_expert_b_2,
        expert_w_gate_2, expert_w_up_2, expert_w_down_2, ln2_w_2, ln2_b_2,
    )


_drawn_inputs = setup_inputs


def setup_inputs(seed=0):
    import zlib

    import numpy as np

    out = dict(_drawn_inputs(seed))
    spreads = {}
    factors = {'attn_q_norm_w': 5.498,
     'attn_k_norm_w': 5.786,
     'hgrn_lb_fwd': 4.572,
     'hgrn_lb_bwd': 6.532,
     'hgrn_out_norm_w': 3.288,
     'norm2_w': 2.838,
     'rwkv_w2_2': 5.016,
     'rwkv_a0_2': 8.0,
     'rwkv_k_k_2': 37.032,
     'rwkv_k_a_2': 5.346,
     'rwkv_ln_w_2': 34.56,
     'rwkv_ln_b_2': 64.0,
     'ssm_a_re_2': 200.0,
     'ssm_glu_b_2': 58.331,
     'gate_b_2': 4.498,
     'router_group_b_2': 19.154,
     'router_expert_b_2': 17.732,
     'ln2_b_2': 2.735,
     'ssm_a_im_2': 53.736,
     'ssm_b_re_2': 57.872,
     'ssm_b_im_2': 64.0,
     'ssm_c_re_2': 64.0,
     'ssm_c_im_2': 64.0,
     'ssm_log_dt_2': 46.176}
    for name, (base, spread) in spreads.items():
        noise = np.random.default_rng([zlib.crc32(name.encode()), seed]).standard_normal(out[name].shape)
        drawn = base * np.exp(spread * noise) if base else spread * noise
        out[name] = jnp.asarray(drawn.astype(out[name].dtype))
    for name, factor in factors.items():
        out[name] = (out[name] * factor).astype(out[name].dtype)
    return out
```

```python
from contextlib import ExitStack

import numpy as np

import concourse.bass as bass
from concourse import mybir

F32 = mybir.dt.float32
ALU = mybir.AluOpType
ACT = mybir.ActivationFunctionType
AXX = mybir.AxisListType.X

P = 128
SEQ = 256
NT = SEQ // P
DM = 1024
KD = DM // P
HEADS, HD = 8, 64
HW = HEADS * HD
GH = 4
E1, CAP, FF1 = 16, 32, 1024
E2, FF2 = 32, 256
NG, EPG = 4, 8
CH = 64
NCH = SEQ // CH
ST = 16
SLOTS, UNIT = 6, 4096
RMS_EPS, LN_EPS, GN_EPS = 1e-6, 1e-5, 64e-5
DEEPNORM_ALPHA = 2 ** 0.25
LOW = 5


def shape_constants():
    parts, at = [], {}

    def put(name, a):
        a = np.asarray(a, np.float32).reshape(P, -1)
        at[name] = (sum(x.shape[1] for x in parts), a.shape[1])
        parts.append(a)

    i = np.arange(P)
    put("ident", np.eye(P))
    q = (np.arange(NT)[None, :, None] * P + i[:, None, None])
    k = np.arange(SEQ)[None, None, :]
    dist = np.abs(q - k)
    put("dist", dist)
    times = (dist <= 64).astype(int) + (dist % 4 == 0) + (dist % 16 == 0)
    put("dilated", np.where(times > 0, np.log(np.maximum(times, 1)), -1e30))
    put("causal", np.where(k <= q, 0.0, -1e30))
    s, t = (i % 32)[:, None], np.arange(32)[None, :]
    put("sibling", np.stack([((s >> l + 1) == (t >> l + 1)) & ((s >> l) != (t >> l)) for l in range(LOW)], 1))
    put("eye32", s == t)
    tri = (i[:, None] <= i[None, :]) & (i[:, None] // CH == i[None, :] // CH)
    put("cumsum", tri)
    put("chunk_sum", i[:, None] // CH == np.arange(2)[None, :])
    r, c = (i % CH)[:, None], np.arange(CH)[None, :]
    put("before_upto", np.concatenate([r < c, r <= c], 1))
    put("after", r > c)
    put("eye64", r == c)
    put("lower", np.stack([((r >> m + 1) == (c >> m + 1)) & ((r >> m) % 2 == 1) & ((c >> m) % 2 == 0)
                           for m in range(6)], 1))
    put("upper", np.stack([((r >> m + 1) == (c >> m + 1)) & ((c >> m) % 2 == 1) & ((r >> m) % 2 == 0)
                           for m in range(6)], 1))
    put("slots", np.broadcast_to(np.arange(1, CAP + 1), (P, CAP)))
    return np.ascontiguousarray(np.concatenate(parts, 1)), at


COLUMN_VECTORS = [("norm1_w", 8), ("norm2_w", 8), ("q_w", 1), ("k_w", 1), ("lb", 16), ("mu_lora", 2),
                  ("a_re", ST), ("a_im", ST), ("log_dt", ST), ("ssm_d", 4), ("glu_b", 8), ("gate_b", 24)]
ROW_VECTORS = [("out_norm_w", 128), ("router_b", 36), ("mu", 1536), ("w0", HW), ("a0", HW), ("k_k", HW),
               ("k_a", HW), ("r_k", HW), ("gn_w", HW), ("gn_b", HW), ("ln1_w", DM), ("ln1_b", DM),
               ("ln2_w", DM), ("ln2_b", DM)]


SHARED = {
    "b2_turned": ("n1_turned", 4), "pu_product": ("p1_product", 16), "ssm_b_turned": ("da_turned", 4),
    "ssm_driven": ("da_scores", 8), "ssm_emitted": ("da_probs_turned", 8), "pg_product": ("da_weighed", 8),
    "pr_product": ("hg_level_used", 8), "rw_lora_out": ("hg_o", 2), "rw_cum": ("hg_turned", 2),
    "rw_turned": ("o1_product", 4), "rw_products": ("n2_turned", 4), "rw_W": ("r_logits", 1),
    "rw_DW": ("r_aff_turned", 1), "rw_WD": ("r_slots_turned", 1), "rw_xv": ("r_gathered", 8),
    "rw_x1": ("r_gated_turned", 1), "b2_T": ("n1_ms", 1), "pu_out0": ("n1_rows", 2), "ssm_bT": ("n1_T", 4),
    "ssm_rotated": ("p1_out0", 8), "ssm_scanned": ("da_ms", 1), "ssm_y": ("da_rows", 2),
    "ssm_gelu_inner": ("da_T", 4), "ssm_gelu": ("da_biased", 8), "pg_out0": ("da_max", 8),
    "glu_out": ("da_probs", 8), "pr_out0": ("da_out", 4), "rw_lora": ("hg_lb_less_max", 1),
    "rw_pre": ("hg_q_used", 1), "rw_decay": ("hg_level", 8), "rw_ms": ("hg_score", 1),
    "rw_bonus": ("hg_ms", 1), "rw_cum_before": ("hg_rows", 1), "rw_scaled": ("hg_out", 2),
    "rw_T": ("o1_out0", 4), "rw_products_out": ("n2_ms", 1), "rw_inv": ("n2_rows", 2),
    "rw_xv_out": ("n2_T", 4), "rw_state": ("r_max", 1), "rw_x": ("r_aff", 1), "rw_y": ("r_slots", 1),
    "rw_gn_ms": ("r_chosen", 1), "rw_y_rows": ("r_gated", 1), "rw_out": ("r_xin", 8),
    "pu_out1": ("n1_squares", 2), "ssm_gelu_sigmoid": ("n1_sd", 1), "pg_out1": ("p1_out1", 8),
    "glu_sigmoid": ("da_sd", 1), "pr_out1": ("da_exp", 8), "rw_lora_act": ("da_probsT", 8),
    "rw_gate": ("hg_lb_exp", 1), "rw_post": ("hg_sigmoids", 3), "rw_sd": ("hg_k_pairs", 5),
    "rw_exp": ("hg_score_copied", 4), "rw_W_out": ("hg_o_copied", 1), "rw_u_out": ("hg_gate", 1),
    "rw_y2_out": ("hg_sd", 1), "rw_gn_sd": ("n2_squares", 2), "pm_out1": ("n2_sd", 1),
    "mb_exp": ("r_exp", 1), "mb_probsT": ("r_gated_T", 1),
}


class Stage:

    def __init__(self, tensor=None, vector=None, scalar=None, gpsimd=None, sync=None, done=None, held=(),
                 mag=None, v=None, y=None):
        self.tensor, self.vector, self.scalar, self.gpsimd, self.sync = tensor, vector, scalar, gpsimd, sync
        self.done, self.held, self.mag, self.v, self.y = done, held, mag, v, y


class Columns:

    def __init__(self, tensor, start, end):
        self.tensor, self.free_list, self.held, self.log = tensor, [(start, end)], {}, {}

    def take(self, name, n, top=False):
        order = list(enumerate(self.free_list))
        for j, (a, b) in reversed(order) if top else order:
            if b - a >= n:
                a = b - n if top else a
                self.free_list[j] = (self.free_list[j][0], a) if top else (a + n, b)
                self.held[name] = self.log[name] = (a, a + n)
                return self.tensor[:, a:a + n]
        raise MemoryError(f"{name} {n} {self.free_list} {self.held}")

    def release(self, *names):
        for name in names:
            self.free_list.append(self.held.pop(name))
        merged = []
        for a, b in sorted(self.free_list):
            if merged and merged[-1][1] == a:
                merged[-1] = (merged[-1][0], b)
            elif a < b:
                merged.append((a, b))
        self.free_list = merged


def along(ap, extra, where):
    dims = [list(x) for x in ap.ap]
    dims.insert(where, [0, extra])
    return bass.AP(tensor=ap.tensor, offset=ap.offset, ap=dims)


def two_blocks(nc, D, const_at, stop=99):
    ctx = ExitStack()
    sems = {}

    def inc(name):
        while name in SHARED:
            name = SHARED[name][0]
        if name not in sems:
            sems[name] = ctx.enter_context(nc.semaphore(name))
        return sems[name]

    def count(name, n):
        base, first = 0, name
        while name in SHARED:
            base += SHARED[name][1]
            name = SHARED[name][0]
        return inc(first), n + base

    with ctx:
        TOTAL = 52800
        arena = ctx.enter_context(nc.sbuf_tensor("arena", [P, TOTAL], F32))
        psum = ctx.enter_context(nc.psum_tensor("psum", [P, 8, 512], F32))
        ring = [arena[:, s * UNIT:(s + 1) * UNIT] for s in range(SLOTS)]
        cols = Columns(arena, SLOTS * UNIT, TOTAL)

        n_const = sum(n for _, n in const_at.values())
        const_sb = cols.take("const", n_const)

        def const(name):
            a, n = const_at[name]
            return const_sb[:, a:a + n]

        n_vec = sum(n for _, n in COLUMN_VECTORS)
        vec_sb = cols.take("vec", n_vec)
        vec, a = {}, 0
        for name, n in COLUMN_VECTORS:
            vec[name] = vec_sb[:, a:a + n]
            a += n
        row_at, a = {}, 0
        for name, n in ROW_VECTORS:
            row_at[name] = (a, n)
            a += n

        def row_source(first, last):
            a, b = row_at[first][0], sum(row_at[last])
            return bass.AP(tensor=D["rows"].tensor, offset=a, ap=[[0, P], [1, b - a]])

        rows_a = cols.take("rows_a", 164)
        row = {"out_norm_w": rows_a[:, 0:128], "router_b": rows_a[:, 128:164]}
        w_router = cols.take("w_router", KD * E1)
        small = cols.take("small", 1200)
        small_used = [0]

        def tiny(n):
            small_used[0] += n
            assert small_used[0] <= 1200, small_used
            return small[:, small_used[0] - n:small_used[0]]

        ident = const("ident")
        x_sb = cols.take("x", NT * DM).rearrange("p (t d) -> p t d", t=NT)

        def bank(b, n=512):
            return psum[:, b, 0:n]

        def banks(b, n):
            return psum[:, b:b + n, :].rearrange("p b n -> p (b n)")

        class Chain:

            def __init__(self, eng, name):
                self.eng, self.name, self.n = eng, name, 0

            def __call__(self, ins):
                self.n += 1
                ins.then_inc(inc(self.name), 1)
                self.eng.wait_ge(*count(self.name, self.n))


        def column_unit(w, c0, n):
            return (w[:, c0:c0 + n].rearrange("(k p) n -> p k n", p=P), w.shape[0] // P, n)

        first_units = [column_unit(D["w_in"], 512 * j, 512) for j in range(8)]
        first_units += [column_unit(D["w_out"], 512 * j, 512) for j in range(2)]
        UNITS_E1 = 6 * E1
        U_E1 = len(first_units)
        U_B2 = U_E1 + UNITS_E1
        OFF_SSM, OFF_MOBA, OFF_GATE = 3328, 1792, 3840
        b2 = [column_unit(D["w_in_2"], OFF_SSM, 512), column_unit(D["ssm_glu_w_2"], 0, 1024)]
        b2 += [column_unit(D["w_in_2"], 512 * j, 512) for j in range(3)]
        b2 += [column_unit(D["w_in_2"], 1536, 256)]
        b2 += [column_unit(D["w_in_2"], OFF_MOBA + 512 * j, 512) for j in range(3)]
        b2 += [column_unit(D["w_in_2"], OFF_GATE + 512 * j, 512) for j in range(6)]
        b2 += [column_unit(D[w], 0, 1024) for w in ("w_up_rwkv_2", "w_up_moba_2", "w_up_ssm_2")]
        b2 += [column_unit(D["w_out_2"], 512 * j, 512) for j in range(2)]
        U_SSM, U_GLU, U_RWKV, U_LORA, U_MOBA, U_GATE, U_UP, U_OUT2 = (U_B2 + x for x in (0, 1, 2, 5, 6, 9, 15, 18))
        U_END = U_B2 + len(b2)

        def slot(u, k, n):
            return ring[u % SLOTS][:, 0:k * n].rearrange("p (k n) -> p k n", k=k)

        def unit_ready(eng, u):
            eng.wait_ge(*count(f"slot_loaded{u % SLOTS}", 16 * (u // SLOTS + 1)))

        def load_unit(sp, u, unit):
            src, k, n = unit
            if u >= SLOTS:
                sp.wait_ge(*count("units_used", u - SLOTS + 1))
            sp.dma_start(slot(u, k, n), src).then_inc(inc(f"slot_loaded{u % SLOTS}"), 16)

        def load_inputs(sp):
            sp.dma_start(x_sb, D["x"].rearrange("(t p) d -> p t d", p=P)).then_inc(inc("x_loaded"), 16)
            sp.dma_start(const_sb, D["consts"]).then_inc(inc("const_loaded"), 16)
            sp.dma_start(vec_sb, D["vectors"]).then_inc(inc("const_loaded"), 16)
            sp.dma_start(rows_a, row_source("out_norm_w", "router_b")).then_inc(inc("const_loaded"), 16)
            sp.dma_start(w_router.rearrange("p (k e) -> p k e", k=KD), D["w_router"].rearrange("k p e -> p k e"))\
              .then_inc(inc("router_loaded"), 16)
            for u, unit in enumerate(first_units):
                load_unit(sp, u, unit)

        def rms_rows(tag, src, ready, out, scratch):
            ss, sd, rs = tiny(2), tiny(2), tiny(2)

            def scalar(act):
                act.wait_ge(*count(*ready))
                for t in range(NT):
                    act.activation(scratch, src[:, t], ACT.Square, accum_out=ss[:, t:t + 1])\
                       .then_inc(inc(tag + "_squares"), 1)
                    act.wait_ge(*count(tag + "_squares", t + 1))
                act.wait_ge(*count(tag + "_ms", 1))
                act.activation(sd, rs, ACT.Sqrt).then_inc(inc(tag + "_sd"), 1)

            def vector(dve):
                dve.wait_ge(*count(tag + "_squares", NT))
                dve.tensor_scalar(rs, ss, 1.0 / DM, RMS_EPS, ALU.mult, ALU.add).then_inc(inc(tag + "_ms"), 1)
                dve.wait_ge(*count(tag + "_sd", 1))
                dve.wait_ge(*count(*ready))
                vchain(dve)(dve.reciprocal(rs, sd))
                for t in range(NT):
                    dve.tensor_scalar(out[:, t], src[:, t], rs[:, t:t + 1], None, ALU.mult)\
                       .then_inc(inc(tag + "_rows"), 1)

            return Stage(scalar=scalar, vector=vector)

        def transpose_rows(tag, src, out, ready, weight=None):
            def tensor(pe):
                pe.wait_ge(*count("const_loaded", 48))
                pe.wait_ge(*count(*ready))
                for j in range(KD // 2):
                    for k in (2 * j, 2 * j + 1):
                        for t in range(NT):
                            mm = pe.transpose(bank(j)[:, (k % 2) * SEQ + t * P:(k % 2) * SEQ + (t + 1) * P],
                                              src[:, t, k * P:(k + 1) * P], ident)
                    mm.then_inc(inc(tag + "_turned"), 1)

            def vector(dve):
                dve.wait_ge(*count("const_loaded", 48))
                for j in range(KD // 2):
                    dve.wait_ge(*count(tag + "_turned", j + 1))
                    for k in (2 * j, 2 * j + 1):
                        src_ps = bank(j)[:, (k % 2) * SEQ:(k % 2 + 1) * SEQ]
                        if weight is None:
                            ins = dve.tensor_copy(out[:, k], src_ps)
                        else:
                            ins = dve.tensor_scalar(out[:, k], src_ps, weight[:, k:k + 1], None, ALU.mult)
                    ins.then_inc(inc(tag + "_T"), 1)

            return Stage(tensor=tensor, vector=vector)

        the_chain = {}

        def vchain(dve):
            if "v" not in the_chain:
                the_chain["v"] = Chain(dve, "vector_step")
            return the_chain["v"]

        def achain(act):
            if "a" not in the_chain:
                the_chain["a"] = Chain(act, "scalar_step")
            return the_chain["a"]

        def gchain(pool):
            if "g" not in the_chain:
                the_chain["g"] = Chain(pool, "gpsimd_step")
            return the_chain["g"]

        def project(tag, lhs, ready, jobs, lanes=2, v_copy=None, a_copy=None):
            v_copy = v_copy or (lambda dve, out, src: dve.tensor_copy(out, src))
            a_copy = a_copy or (lambda act, out, src: act.activation(out, src, ACT.Copy))

            def tensor(pe):
                pe.wait_ge(*count(*ready))
                finished = 0
                for j, (u, kind, sub, n, kt, out) in enumerate(jobs):
                    w = slot(u, kt, n)
                    unit_ready(pe, u)
                    if j >= 4:
                        pe.wait_ge(*count(f"{tag}_out{j % lanes}", (j - 4) // lanes + 1))
                    b = bank(j % 4)
                    blocks = [(b[:, 0:n], None)] if kind == "tok" else \
                        [(b[:, e * SEQ:(e + 1) * SEQ], (2 * sub + e) * P) for e in range(2)]
                    for o, c in blocks:
                        for k in range(kt):
                            if kind == "tok":
                                mm = pe.matmul(o, lhs[:, k, sub * P:(sub + 1) * P], w[:, k, :],
                                               start=(k == 0), stop=(k == kt - 1))
                            else:
                                mm = pe.matmul(o, w[:, k, c:c + P], lhs[:, k, :],
                                               start=(k == 0), stop=(k == kt - 1))
                            if finished:
                                mm.then_inc(inc("units_used"), 1)
                                finished = 0
                    mm.then_inc(inc(tag + "_product"), 1)
                    finished = j + 1 == len(jobs) or jobs[j + 1][0] != u
                pe.wait_ge(*count(tag + "_product", len(jobs)))
                pe.sem_inc(inc("units_used"), 1)

            def copies(eng, lane, copy):
                for j, (u, kind, sub, n, kt, out) in enumerate(jobs):
                    if j % lanes == lane:
                        eng.wait_ge(*count(tag + "_product", j + 1))
                        src = bank(j % 4)[:, 0:n] if kind == "tok" else \
                            bank(j % 4).rearrange("p (e s) -> p e s", e=2)
                        copy(eng, out, src).then_inc(inc(f"{tag}_out{lane}"), 1)

            return Stage(tensor=tensor, vector=lambda dve: copies(dve, 0, v_copy),
                         scalar=lambda act: copies(act, 1, a_copy),
                         done=[(f"{tag}_out{n}", (len(jobs) + lanes - 1 - n) // lanes) for n in range(lanes)])

        hT = cols.take("hT", KD * SEQ).rearrange("p (k s) -> p k s", k=KD)
        xn = cols.take("xn", NT * DM).rearrange("p (t d) -> p t d", t=NT)
        scratch = cols.take("scratch", DM)
        norm1 = rms_rows("n1", x_sb, ("x_loaded", 16), xn, scratch)
        turn1 = transpose_rows("n1", xn, hT, ("n1_rows", NT), vec["norm1_w"])
        qkv = cols.take("qkv", NT * 3 * HW).rearrange("p (t c) -> p t c", t=NT)
        hgT = cols.take("hgT", 3 * GH * SEQ).rearrange("p (c s) -> p c s", s=SEQ)
        ig = cols.take("ig", NT * 2 * HW).rearrange("p (t c) -> p t c", t=NT)
        jobs = [(u, "tok", t, 512, KD, qkv[:, t, 512 * u:512 * u + 512]) for u in range(3) for t in range(NT)]
        jobs += [(u, "T", s, 512, KD, hgT[:, 4 * (u - 3) + 2 * s:4 * (u - 3) + 2 * s + 2]) for u in range(3, 6) for s in range(2)]
        jobs += [(u, "tok", t, 512, KD, ig[:, t, 512 * (u - 6):512 * (u - 5)]) for u in range(6, 8) for t in range(NT)]
        proj1 = project("p1", hT, ("n1_T", KD // 2), jobs)
        cols.release("xn", "scratch")
        mixT = cols.take("mixT", KD * SEQ).rearrange("p (k s) -> p k s", k=KD)

        def attention(tag, src, inputs_done, out, mask, norm):
            qkT = cols.take(tag + "qkT", 8 * SEQ).rearrange("p (c s) -> p c s", s=SEQ)
            sc = [cols.take(f"{tag}sc{j}", 512).rearrange("p (t s) -> p t s", t=NT) for j in range(2)]
            pT = [cols.take(f"{tag}pT{j}", 512).rearrange("p (t s) -> p t s", t=NT) for j in range(2)]
            den, rden, nmax = tiny(2 * HEADS), tiny(2 * HEADS), tiny(2 * HEADS)
            qk = src[:, :, 0:2 * HW]
            if norm:
                sq = cols.take(tag + "sq", NT * 2 * HW)
                ms, sd = tiny(32), tiny(32)

            def prepare(dve):
                step = vchain(dve)
                for sem, n in inputs_done:
                    dve.wait_ge(*count(sem, n))
                if norm:
                    sqv = sq.rearrange("p (t c) -> p t c", t=NT)
                    step(dve.tensor_tensor(sqv, qk, qk, ALU.mult))
                    step(dve.tensor_reduce(ms, sq.rearrange("p (h d) -> p h d", d=HD), AXX, ALU.add))
                    dve.tensor_scalar(ms, ms, 1.0 / HD, RMS_EPS, ALU.mult, ALU.add).then_inc(inc(tag + "_ms"), 1)
                    dve.wait_ge(*count(tag + "_sd", 1))
                    step(dve.reciprocal(sd, sd))
                    for t in range(NT):
                        v = qk[:, t].rearrange("p (h d) -> p h d", d=HD)
                        last = dve.tensor_tensor(v, v, along(sd[:, 16 * t:16 * t + 16], HD, 2), ALU.mult)
                        last.then_inc(inc(tag + "_rows"), 1)
                else:
                    dve.sem_inc(inc(tag + "_rows"), NT)
                for j in range(4):
                    dve.wait_ge(*count(tag + "_turned", j + 1))
                    o, i = qkT[:, 2 * j:2 * j + 2], bank(j).rearrange("p (e s) -> p e s", e=2)
                    if norm:
                        w = vec["q_w"] if j < 2 else vec["k_w"]
                        ins = dve.tensor_scalar(o, i, w, HD ** -0.5 if j < 2 else 1.0, ALU.mult, ALU.mult)
                    else:
                        ins = dve.tensor_scalar(o, i, HD ** -0.5 if j < 2 else 1.0, None, ALU.mult)
                    ins.then_inc(inc(tag + "_T"), 1)

            def products(pe):
                pe.wait_ge(*count(tag + "_rows", NT))
                for sem, n in inputs_done:
                    pe.wait_ge(*count(sem, n))
                for j in range(4):
                    for c in (2 * j, 2 * j + 1):
                        for t in range(NT):
                            mm = pe.transpose(bank(j)[:, (c % 2) * SEQ + t * P:(c % 2) * SEQ + (t + 1) * P],
                                              src[:, t, c * P:(c + 1) * P], ident)
                    mm.then_inc(inc(tag + "_turned"), 1)
                pe.wait_ge(*count(tag + "_T", 4))

                def scores(h):
                    if h >= 2:
                        pe.wait_ge(*count(tag + "_biased", h - 1))
                    r = slice(64 * (h % 2), 64 * (h % 2) + 64)
                    for t in range(NT):
                        mm = pe.matmul(bank(4 + h % 2)[:, t * SEQ:(t + 1) * SEQ],
                                       qkT[r, h // 2, t * P:(t + 1) * P], qkT[r, 4 + h // 2, :],
                                       start=True, stop=True)
                    mm.then_inc(inc(tag + "_scores"), 1)

                def weigh(h):
                    pe.wait_ge(*count(tag + "_probs", h + 1))
                    if h >= 1:
                        pe.wait_ge(*count(tag + "_probsT", h))
                    for t in range(NT):
                        for k in range(NT):
                            mm = pe.transpose(bank(6)[:, k * SEQ + t * P:k * SEQ + (t + 1) * P],
                                              sc[h % 2][:, t, k * P:(k + 1) * P], ident)
                    mm.then_inc(inc(tag + "_probs_turned"), 1)
                    pe.wait_ge(*count(tag + "_probsT", h + 1))
                    if h % 2 == 0 and h >= 4:
                        pe.wait_ge(*count(tag + "_out", h // 2 - 1))
                    o = bank(7)[64 * (h % 2):64 * (h % 2) + 64, (h // 2 % 2) * SEQ:(h // 2 % 2 + 1) * SEQ]
                    for k in range(NT):
                        mm = pe.matmul(o, src[:, k, 2 * HW + h * HD:2 * HW + (h + 1) * HD], pT[h % 2][:, k],
                                       start=(k == 0), stop=(k == NT - 1))
                    mm.then_inc(inc(tag + "_weighed"), 1)

                scores(0)
                for h in range(HEADS):
                    if h + 1 < HEADS:
                        scores(h + 1)
                    weigh(h)

            def softmax(dve):
                step = vchain(dve)

                def bias(h):
                    dve.wait_ge(*count(tag + "_scores", h + 1))
                    if h >= 2:
                        dve.wait_ge(*count(tag + "_probs_turned", h - 1))
                    s = sc[h % 2]
                    slope = 2.0 ** -(h + 1)
                    dve.scalar_tensor_tensor(s, dist, -slope, bank(4 + h % 2).rearrange("p (t s) -> p t s", t=NT),
                                             ALU.mult, ALU.add).then_inc(inc(tag + "_biased"), 1)
                    dve.wait_ge(*count(tag + "_biased", h + 1))
                    step(dve.tensor_tensor(s, s, mask, ALU.add))
                    dve.tensor_reduce(nmax[:, 2 * h:2 * h + 2], s, AXX, ALU.max, negate=True)\
                       .then_inc(inc(tag + "_max"), 1)

                def divide(h):
                    dve.wait_ge(*count(tag + "_exp", h + 1))
                    step(dve.reciprocal(rden[:, 2 * h:2 * h + 2], den[:, 2 * h:2 * h + 2]))
                    dve.tensor_tensor(sc[h % 2], sc[h % 2], along(rden[:, 2 * h:2 * h + 2], SEQ, 2), ALU.mult)\
                       .then_inc(inc(tag + "_probs"), 1)

                bias(0)
                for h in range(HEADS):
                    if h + 1 < HEADS:
                        bias(h + 1)
                    divide(h)
                    if h % 2:
                        dve.wait_ge(*count(tag + "_weighed", h + 1))
                        dve.tensor_copy(out[:, h // 2], bank(7)[:, (h // 2 % 2) * SEQ:(h // 2 % 2 + 1) * SEQ])\
                           .then_inc(inc(tag + "_out"), 1)

            def exps(act):
                if norm:
                    act.wait_ge(*count(tag + "_ms", 1))
                    act.activation(sd, ms, ACT.Sqrt).then_inc(inc(tag + "_sd"), 1)

                def turned(h):
                    act.wait_ge(*count(tag + "_probs_turned", h + 1))
                    if h >= 2:
                        act.wait_ge(*count(tag + "_weighed", h - 1))
                    act.activation(pT[h % 2].rearrange("p t s -> p (t s)"), bank(6), ACT.Copy)\
                       .then_inc(inc(tag + "_probsT"), 1)

                for h in range(HEADS):
                    act.wait_ge(*count(tag + "_max", h + 1))
                    for t in range(NT):
                        ins = act.activation(sc[h % 2][:, t], sc[h % 2][:, t], ACT.Exp,
                                             bias=nmax[:, 2 * h + t:2 * h + t + 1],
                                             accum_out=den[:, 2 * h + t:2 * h + t + 1])
                    ins.then_inc(inc(tag + "_exp"), 1)
                    if h >= 1:
                        turned(h - 1)
                turned(HEADS - 1)

            cols.release(tag + "qkT", tag + "sc0", tag + "sc1", tag + "pT0", tag + "pT1")
            if norm:
                cols.release(tag + "sq")

            def vector(dve):
                prepare(dve)
                softmax(dve)

            return Stage(tensor=products, vector=vector, scalar=exps)

        dist = const("dist").rearrange("p (t s) -> p t s", t=NT)
        attention1 = attention("da", qkv, proj1.done, mixT[:, 0:4], const("dilated").rearrange("p (t s) -> p t s", t=NT), True)

        def hgrn():
            cols.release("qkv", "hT")
            names = []

            def take(name, n):
                names.append("hg_" + name)
                return cols.take("hg_" + name, n)

            q2 = take("q2", 2048).rearrange("p (d s) -> p d s", d=2)
            k2 = take("k2", 2048).rearrange("p (d s) -> p d s", d=2)
            totals = [take(f"total{l}", 2048 >> l).rearrange("p (d s) -> p d s", d=2) for l in range(8)]
            qs = take("qs", 1024)
            kd = take("kd", 1024)
            low = take("low", LOW * 256)
            near = take("near", 256)
            o_sb = take("o", 1024).rearrange("p (t c) -> p t c", t=NT)
            sig = take("sig", 1024)
            score = hgT[:, 4:12].rearrange("p c s -> p (c s)").rearrange("p (h s t) -> p h s t", h=GH, s=NT)
            far, sig_q, e_lb, lb_sum = tiny(8), None, tiny(16), tiny(8)
            lb, rest = tiny(8), tiny(8)
            ms, sd = tiny(8), tiny(8)
            q_raw, f_raw = hgT[:, 0:4].rearrange("p c s -> p (c s)"), hgT[:, 4:12].rearrange("p c s -> p (c s)")
            k_pairs = hgT[:, 4:8].rearrange("p c s -> p (c s)")
            lbv = vec["lb"].rearrange("p (d r k) -> p d r k", d=2, r=2)
            e_view = e_lb.rearrange("p (d r k) -> p d r k", d=2, r=2)
            score_ps = banks(4, 4).rearrange("p (h s t) -> p h s t", h=GH, s=NT)
            eye, siblings = const("eye32"), const("sibling").rearrange("p (l t) -> p l t", l=LOW)
            g_in = ig[:, :, HW:2 * HW]

            def pair(ap2, n, t0, size):
                dims = [list(ap2.ap[0])]
                if size // (2 * n) > 1:
                    dims.append([2 * n, size // (2 * n)])
                dims.append([n + 1024, 2])
                if n > 1:
                    dims.append([1, n])
                return bass.AP(tensor=ap2.tensor, offset=ap2.offset + t0, ap=dims)

            def scalar(act):
                for sem, n in proj1.done:
                    act.wait_ge(*count(sem, n))
                act.wait_ge(*count("hg_lb_less_max", 1))
                act.activation(e_lb, e_lb, ACT.Exp).then_inc(inc("hg_lb_exp"), 1)
                act.activation(sig, q_raw, ACT.Sigmoid).then_inc(inc("hg_sigmoids"), 1)
                act.activation(totals[0].rearrange("p d s -> p (d s)"), f_raw, ACT.Sigmoid).then_inc(inc("hg_sigmoids"), 1)
                act.activation(k2.rearrange("p d s -> p (d s)"), f_raw, ACT.Sigmoid, scale=-1.0).then_inc(inc("hg_sigmoids"), 1)
                for l in range(LOW):
                    act.wait_ge(*count("hg_level", l + 1))
                    act.activation(k_pairs, pair(k2, 1 << l, 0, GH * SEQ), ACT.Copy).then_inc(inc("hg_k_pairs"), 1)
                act.wait_ge(*count("hg_level_used", 8))
                for h in range(GH):
                    act.activation(score[:, h], score_ps[:, h], ACT.Copy).then_inc(inc("hg_score_copied"), 1)
                act.wait_ge(*count("hg_o", NT))
                act.activation(o_sb, banks(0, 2).rearrange("p (t c) -> p t c", t=NT), ACT.Copy).then_inc(inc("hg_o_copied"), 1)
                act.wait_ge(*count("hg_q_used", 1))
                act.activation(sig.rearrange("p (t c) -> p t c", t=NT), g_in, ACT.Sigmoid).then_inc(inc("hg_gate"), 1)
                act.wait_ge(*count("hg_ms", 1))
                act.activation(sd, ms, ACT.Sqrt).then_inc(inc("hg_sd"), 1)

            def vector(dve):
                step = vchain(dve)
                fv = far.rearrange("p (d k) -> p d k", d=2)
                step(dve.tensor_tensor(fv, lbv[:, :, 0], lbv[:, :, 1], ALU.max))
                dve.tensor_tensor(e_view[:, :, 0], lbv[:, :, 0], fv, ALU.subtract)
                dve.tensor_tensor(e_view[:, :, 1], lbv[:, :, 1], fv, ALU.subtract).then_inc(inc("hg_lb_less_max"), 1)
                dve.wait_ge(*count("hg_lb_exp", 1))
                sv = lb_sum.rearrange("p (d k) -> p d k", d=2)
                step(dve.tensor_tensor(sv, e_view[:, :, 0], e_view[:, :, 1], ALU.add))
                step(dve.reciprocal(lb_sum, lb_sum))
                dve.tensor_tensor(lb.rearrange("p (d k) -> p d k", d=2), e_view[:, :, 0], sv, ALU.mult)
                step(dve.tensor_tensor(rest.rearrange("p (d k) -> p d k", d=2), e_view[:, :, 1], sv, ALU.mult))
                dve.wait_ge(*count("hg_sigmoids", 3))
                for sem, n in proj1.done:
                    dve.wait_ge(*count(sem, n))
                for j in range(8):
                    g = totals[0][:, j // 4, (j % 4) * SEQ:(j % 4 + 1) * SEQ]
                    k = k2[:, j // 4, (j % 4) * SEQ:(j % 4 + 1) * SEQ]
                    dve.tensor_scalar(g, g, rest[:, j:j + 1], lb[:, j:j + 1], ALU.mult, ALU.add)
                    last = dve.tensor_scalar(k, k, rest[:, j:j + 1], None, ALU.mult)
                step(last)
                step(dve.tensor_tensor(qs, q_raw, sig, ALU.mult))
                dve.tensor_tensor(q2[:, 0], qs, totals[0][:, 1], ALU.mult).then_inc(inc("hg_q_used"), 1)
                dve.tensor_tensor(q2[:, 1], qs, totals[0][:, 0], ALU.mult)
                dve.tensor_tensor(kd, k2[:, 0], k2[:, 1], ALU.add).then_inc(inc("hg_level"), 1)
                dve.wait_ge(*count("hg_level", 1))
                for l in range(7):
                    n = 1 << l
                    t_f, t_b = (totals[l][:, d].rearrange("p (j u) -> p j u", u=2) for d in range(2))
                    dve.tensor_tensor(totals[l + 1][:, 0], t_f[:, :, 0], t_f[:, :, 1], ALU.mult)
                    dve.tensor_tensor(totals[l + 1][:, 1], t_b[:, :, 0], t_b[:, :, 1], ALU.mult)
                    dve.wait_ge(*count("hg_level_used", l + 1))
                    for arr, lower, upper in ((q2, t_b[:, :, 1], t_f[:, :, 0]), (k2, t_f[:, :, 1], t_b[:, :, 0])):
                        for u, other in ((0, lower), (1, upper)):
                            v = arr[:, u].rearrange("p (j u i) -> p j u i", u=2, i=n)[:, :, u]
                            last = dve.tensor_tensor(v, v, along(other, n, 2), ALU.mult)
                    last.then_inc(inc("hg_level"), 1)
                    dve.wait_ge(*count("hg_level", l + 2))
                lowv = low.rearrange("p (l e t) -> p l e t", l=LOW, e=8)
                step(dve.tensor_tensor(lowv, banks(0, 3)[:, 0:LOW * 256].rearrange("p (l e t) -> p l e t", l=LOW, e=8),
                                       along(siblings, 8, 2), ALU.mult))
                step(dve.tensor_reduce(near, low.rearrange("p (l e) -> p e l", l=LOW), AXX, ALU.add))
                dve.wait_ge(*count("hg_score_copied", GH))
                nearv = near.rearrange("p (h s t) -> p h s t", h=GH, s=NT)
                spots = [(slice(32 * b, 32 * b + 32), s, s * P + 32 * b) for b in range(4) for s in range(NT)]
                for r, s, c in spots:
                    last = dve.tensor_tensor(score[r, :, s, c:c + 32], score[r, :, s, c:c + 32], along(eye[r], GH, 1), ALU.mult)
                step(last)
                for r, s, c in spots:
                    last = dve.tensor_tensor(score[r, :, s, c:c + 32], score[r, :, s, c:c + 32], nearv[r, :, s], ALU.add)
                last.then_inc(inc("hg_score"), 1)
                dve.wait_ge(*count("hg_o_copied", 1))
                o_heads = o_sb.rearrange("p t (h v) -> p (t h) v", v=P)
                sq = score.rearrange("p h s t -> p (h s t)")[:, 0:1024]
                step(dve.tensor_tensor(sq.rearrange("p (t c) -> p t c", t=NT), o_sb, o_sb, ALU.mult))
                step(dve.tensor_reduce(ms, sq.rearrange("p (h v) -> p h v", v=P), AXX, ALU.add))
                dve.tensor_scalar(ms, ms, 1.0 / P, RMS_EPS, ALU.mult, ALU.add).then_inc(inc("hg_ms"), 1)
                dve.wait_ge(*count("hg_sd", 1))
                step(dve.reciprocal(sd, sd))
                step(dve.tensor_tensor(o_heads, o_heads, along(sd, P, 2), ALU.mult))
                step(dve.tensor_tensor(o_heads, o_heads, along(row["out_norm_w"], 8, 1), ALU.mult))
                step(dve.tensor_tensor(o_sb, o_sb, g_in, ALU.mult))
                dve.wait_ge(*count("hg_gate", 1))
                dve.tensor_tensor(o_sb, o_sb, sig.rearrange("p (t c) -> p t c", t=NT), ALU.mult).then_inc(inc("hg_rows"), 1)
                for j in range(2):
                    dve.wait_ge(*count("hg_turned", j + 1))
                    dve.tensor_copy(mixT[:, 4 + 2 * j:6 + 2 * j], bank(2 + j).rearrange("p (e s) -> p e s", e=2))\
                       .then_inc(inc("hg_out"), 1)

            def tensor(pe):
                for l in range(8):
                    n = 1 << l
                    pe.wait_ge(*count("hg_level", l + 1))
                    if l < LOW:
                        pe.wait_ge(*count("hg_k_pairs", l + 1))
                    if l == 0:
                        pe.wait_ge(*count("da_out", 4))
                    for h in range(GH):
                        if l < LOW:
                            for s in range(NT):
                                for b in range(4):
                                    t0 = h * SEQ + s * P + 32 * b
                                    r = slice(32 * b, 32 * b + 32)
                                    c = l * 256 + h * 64 + s * 32
                                    mm = pe.matmul(banks(0, 3)[r, c:c + 32], k_pairs[:, t0:t0 + 32], pair(q2, n, t0, 32),
                                                   start=True, stop=True)
                                    if l == 0:
                                        mm = pe.matmul(score_ps[r, h, s, s * P + 32 * b:s * P + 32 * b + 32],
                                                       kd[:, t0:t0 + 32], qs[:, t0:t0 + 32], start=True, stop=True)
                        else:
                            for j in range(SEQ // (2 * n)):
                                a, z = 2 * j * n, (2 * j + 1) * n
                                for s0, t0, copy in ((a, z, 0), (z, a, 1)):
                                    mm = pe.matmul(score_ps[s0 % P:s0 % P + n, h, s0 // P, t0:t0 + n],
                                                   k2[:, copy, h * SEQ + s0:h * SEQ + s0 + n],
                                                   q2[:, 1 - copy, h * SEQ + t0:h * SEQ + t0 + n], start=True, stop=True)
                    mm.then_inc(inc("hg_level_used"), 1)
                pe.wait_ge(*count("hg_score", 1))
                for t in range(NT):
                    for h in range(GH):
                        for s in range(NT):
                            mm = pe.matmul(bank(t)[:, h * P:(h + 1) * P], score[:, h, s, t * P:(t + 1) * P],
                                           ig[:, s, h * P:(h + 1) * P], start=(s == 0), stop=(s == NT - 1))
                    mm.then_inc(inc("hg_o"), 1)
                pe.wait_ge(*count("hg_rows", 1))
                for j in range(2):
                    for c in (2 * j, 2 * j + 1):
                        for t in range(NT):
                            mm = pe.transpose(bank(2 + j)[:, (c % 2) * SEQ + t * P:(c % 2) * SEQ + (t + 1) * P],
                                              o_sb[:, t, c * P:(c + 1) * P], ident)
                    mm.then_inc(inc("hg_turned"), 1)

            cols.release("hgT", "ig", *names)
            return Stage(tensor=tensor, vector=vector, scalar=scalar)

        hgrn2 = hgrn()

        jobs = [(8 + c, "tok", t, 512, KD, x_sb[:, t, 512 * c:512 * (c + 1)]) for c in range(2) for t in range(NT)]
        out_proj1 = project("o1", mixT, ("hg_out", 2), jobs, lanes=1,
                            v_copy=lambda dve, out, src: dve.tensor_tensor(out, out, src, ALU.add))
        cols.release("mixT")
        h2 = cols.take("h2", NT * DM, top=True).rearrange("p (t d) -> p t d", t=NT)
        scratch2 = cols.take("scratch2", DM, top=True)
        norm2 = rms_rows("n2", x_sb, ("o1_out0", 4), h2, scratch2)
        h2T = cols.take("h2T", KD * SEQ, top=True).rearrange("p (k s) -> p k s", k=KD)
        turn2 = transpose_rows("n2", h2, h2T, ("n2_rows", NT), vec["norm2_w"])
        chosen = cols.take("chosen", NT * E1 * CAP, top=True)
        gated = cols.take("gated", NT * E1 * CAP, top=True)
        gated_T = cols.take("gated_T", 4 * SEQ).rearrange("p (g s) -> p g s", g=4)
        xin = cols.take("xin", (E1 + 1) * KD * CAP).rearrange("p (e k c) -> p e k c", e=E1 + 1, k=KD)

        def route():
            aff = tiny(NT * E1).rearrange("p (t e) -> p t e", t=NT)
            nmax, total = tiny(NT), tiny(NT)
            work, best, picked = cols.take("r_work", SEQ), tiny(8), cols.take("r_picked", SEQ)
            place, ones_row = cols.take("r_count", SEQ), cols.take("r_ones", SEQ)
            slot_of = tiny(NT * E1)
            logits = bank(4, NT * E1).rearrange("p (t e) -> p t e", t=NT)
            c3 = chosen.rearrange("p (a c) -> p a c", c=CAP)
            g3 = gated.rearrange("p (a c) -> p a c", c=CAP)
            by_tile = chosen.rearrange("p (t c) -> p t c", t=NT)
            gated_by_tile = gated.rearrange("p (t c) -> p t c", t=NT)

            def tensor(pe):
                pe.wait_ge(*count("router_loaded", 16))
                pe.wait_ge(*count("n2_T", KD // 2))
                wr = w_router.rearrange("p (k e) -> p k e", k=KD)
                for t in range(NT):
                    for k in range(KD):
                        mm = pe.matmul(logits[:, t], h2T[:, k, t * P:(t + 1) * P], wr[:, k],
                                       start=(k == 0), stop=(k == KD - 1))
                mm.then_inc(inc("r_logits"), 1)
                pe.wait_ge(*count("r_aff", 1))
                for t in range(NT):
                    mm = pe.transpose(bank(5)[0:E1, t * P:(t + 1) * P], aff[:, t], ident)
                mm.then_inc(inc("r_aff_turned"), 1)
                pe.wait_ge(*count("r_slots", 1))
                for t in range(NT):
                    mm = pe.transpose(bank(6)[:, t * E1:(t + 1) * E1], place[0:E1, t * P:(t + 1) * P], ident[0:E1, 0:E1])
                mm.then_inc(inc("r_slots_turned"), 1)
                pe.wait_ge(*count("r_chosen", 1))
                for k in range(KD):
                    if k >= 2:
                        pe.wait_ge(*count("r_xin", k - 1))
                    for t in range(NT):
                        mm = pe.matmul(bank(2 + k % 2), h2[:, t, k * P:(k + 1) * P], by_tile[:, t],
                                       start=(t == 0), stop=(t == NT - 1))
                    mm.then_inc(inc("r_gathered"), 1)
                pe.wait_ge(*count("r_gated", 1))
                for g in range(4):
                    for t in range(NT):
                        mm = pe.transpose(bank(g // 2)[:, (g % 2) * SEQ + t * P:(g % 2) * SEQ + (t + 1) * P],
                                          gated_by_tile[:, t, g * P:(g + 1) * P], ident)
                mm.then_inc(inc("r_gated_turned"), 1)

            def scalar(act):
                act.wait_ge(*count("r_max", 1))
                for t in range(NT):
                    ins = act.activation(aff[:, t], logits[:, t], ACT.Exp, bias=nmax[:, t:t + 1],
                                         accum_out=total[:, t:t + 1])
                ins.then_inc(inc("r_exp"), 1)
                act.wait_ge(*count("r_gated_turned", 1))
                act.activation(gated_T.rearrange("p g s -> p (g s)"), banks(0, 2), ACT.Copy).then_inc(inc("r_gated_T"), 1)

            def vector(dve):
                step = vchain(dve)
                dve.memset(xin[:, E1], 0.0)
                dve.memset(ones_row, 1.0)
                dve.wait_ge(*count("r_logits", 1))
                dve.tensor_reduce(nmax, logits, AXX, ALU.max, negate=True).then_inc(inc("r_max"), 1)
                dve.wait_ge(*count("r_exp", 1))
                step(dve.reciprocal(total, total))
                dve.tensor_tensor(aff, aff, along(total, E1, 2), ALU.mult).then_inc(inc("r_aff"), 1)
                dve.wait_ge(*count("r_aff_turned", 1))
                w = work[0:E1]
                step(dve.tensor_copy(w, bank(5)[0:E1, 0:SEQ]))
                for _ in range(CAP // 8):
                    step(dve.max(best[0:E1], w))
                    step(dve.match_replace(w, best[0:E1], w, -1.0))
                step(dve.tensor_scalar(picked[0:E1], w, -0.5, None, ALU.is_lt))
                step(dve.tensor_tensor_scan(place[0:E1], ones_row[0:E1], picked[0:E1], 0.0, ALU.mult, ALU.add))
                dve.tensor_tensor(place[0:E1], place[0:E1], picked[0:E1], ALU.mult).then_inc(inc("r_slots"), 1)
                dve.wait_ge(*count("r_slots_turned", 1))
                step(dve.tensor_copy(slot_of, bank(6)[:, 0:NT * E1]))
                dve.tensor_tensor(c3, along(slot_of, CAP, 2), along(const("slots"), NT * E1, 1), ALU.is_equal)\
                   .then_inc(inc("r_chosen"), 1)
                dve.wait_ge(*count("r_chosen", 1))
                dve.tensor_tensor(g3, c3, along(aff.rearrange("p t e -> p (t e)"), CAP, 2), ALU.mult)\
                   .then_inc(inc("r_gated"), 1)
                for k in range(KD):
                    dve.wait_ge(*count("r_gathered", k + 1))
                    dve.tensor_scalar(xin[:, 0:E1, k], bank(2 + k % 2).rearrange("p (e c) -> p e c", c=CAP),
                                      vec["norm2_w"][:, k:k + 1], None, ALU.mult).then_inc(inc("r_xin"), 1)

            cols.release("r_work", "r_picked", "r_count", "r_ones")
            return Stage(tensor=tensor, vector=vector, scalar=scalar)

        routing = route()

        def experts1():
            xcur = cols.take("e1_x", KD * CAP).rearrange("p (k c) -> p k c", k=KD)
            gcur = cols.take("e1_g", SEQ)
            hid = cols.take("e1_hid", 512)
            hid_T = cols.take("e1_hid_T", 256)
            y_sb = cols.take("e1_y", DM)
            hid_T4 = hid_T.rearrange("p (c n m) -> p c n m", c=4, n=2)
            gate_ps, up_ps, turned_ps, y_ps = bank(0)[0:64], bank(1)[0:64], bank(2), banks(3, 2)
            weights = [("w_expert_gate", 0), ("w_expert_gate", 1), ("w_expert_up", 0), ("w_expert_up", 1),
                       ("w_expert_down", 0), ("w_expert_down", 1)]

            def ready(eng, e4, j, g):
                u = U_E1 + 6 * e4 + j
                eng.wait_ge(*count(f"slot_loaded{u % SLOTS}", g * 64 + 16 * (u // SLOTS + 1)))

            def w_slot(e4, j):
                return slot(U_E1 + 6 * e4 + j, KD, 512)

            def sync(sp):
                with sp.Fori(0, E1 // 4) as g:
                    for e4 in range(4):
                        for j, (name, half) in enumerate(weights):
                            u = U_E1 + 6 * e4 + j
                            sp.wait_ge(*count("units_used", g * 24 + (u - SLOTS + 1)))
                            src = D[name][bass.ds(g * 4 + e4, 1), :, 512 * half:512 * half + 512]
                            sp.dma_start(w_slot(e4, j), src.rearrange("o (k p) n -> p (o k) n", p=P))\
                              .then_inc(inc(f"slot_loaded{u % SLOTS}"), 16)

            def tensor(pe):
                pe.wait_ge(*count("r_xin", KD))
                pe.wait_ge(*count("r_gated_T", 1))
                pe.sem_inc(inc("e1_combined"), 1)
                with pe.Fori(0, E1 // 4) as g:
                    for e4 in range(4):
                        pe.wait_ge(*count("e1_x", g * 4 + (e4 + 1)))
                        for which, (ps, sem) in enumerate(((gate_ps, "e1_gate"), (up_ps, "e1_up"))):
                            for n in range(2):
                                ready(pe, e4, 2 * which + n, g)
                            for k in range(KD):
                                for n in range(2):
                                    mm = pe.matmul(ps[32 * n:32 * n + 32], xcur[:, k], w_slot(e4, 2 * which + n)[:, k],
                                                   start=(k == 0), stop=(k == KD - 1))
                                    if k == 0 and n == 0 and (which or e4):
                                        mm.then_inc(inc("units_used"), 1)
                                    if k == KD - 1 and n == 0:
                                        mm.then_inc(inc("units_used"), 1)
                            mm.then_inc(inc(sem), 1)
                        pe.wait_ge(*count("e1_hid", g * 4 + (e4 + 1)))
                        for c in range(4):
                            mm = pe.matmul(turned_ps[:, 64 * c:64 * c + 64], hid[0:64, P * c:P * c + P], ident[0:64, 0:64],
                                           start=True, stop=True)
                            if c == 0:
                                mm.then_inc(inc("units_used"), 1)
                        mm.then_inc(inc("e1_turned"), 1)
                        pe.wait_ge(*count("e1_hid_T", g * 4 + (e4 + 1)))
                        for n in range(2):
                            ready(pe, e4, 4 + n, g)
                            for k in range(KD):
                                mm = pe.matmul(y_ps[32 * e4:32 * e4 + 32, 512 * n:512 * n + 512],
                                               hid_T4[:, k % 4, k // 4], w_slot(e4, 4 + n)[:, k],
                                               start=(k == 0), stop=(k == KD - 1))
                            mm.then_inc(inc("units_used" if n == 0 else "e1_down"), 1)
                    pe.wait_ge(*count("e1_y", g + 1))
                    pe.wait_ge(*count("e1_gated", g + 1))
                    for j in range(4):
                        if j < 2:
                            pe.wait_ge(*count("e1_added", g * 4 + 1))
                        else:
                            pe.wait_ge(*count("e1_added", g * 4 + j))
                        if j == 0:
                            pe.sem_inc(inc("units_used"), 1)
                        pe.matmul(bank(5 + j % 2), gcur[:, (j // 2) * P:(j // 2 + 1) * P],
                                  y_sb[:, 512 * (j % 2):512 * (j % 2) + 512], start=True, stop=True)\
                          .then_inc(inc("e1_combined"), 1)

            def scalar(act):
                with act.Fori(0, E1 // 4) as g:
                    for e4 in range(4):
                        act.wait_ge(*count("e1_gate", g * 4 + (e4 + 1)))
                        act.activation(hid[0:64], gate_ps, ACT.Sigmoid).then_inc(inc("e1_sigmoid"), 1)
                        act.wait_ge(*count("e1_turned", g * 4 + (e4 + 1)))
                        act.activation(hid_T, turned_ps[:, 0:256], ACT.Copy).then_inc(inc("e1_hid_T"), 1)
                    act.wait_ge(*count("e1_down", g * 4 + 4))
                    act.activation(y_sb, y_ps, ACT.Copy).then_inc(inc("e1_y"), 1)

            def vector(dve):
                xin_e = xin.rearrange("p e k c -> p e (k c)")
                flat = xcur.rearrange("p k c -> p (k c)")
                dve.wait_ge(*count("r_xin", KD))
                dve.tensor_copy(flat, xin_e[:, 0]).then_inc(inc("e1_x"), 1)
                dve.wait_ge(*count("r_gated_T", 1))
                dve.sem_inc(inc("e1_added"), 1)
                with dve.Fori(0, E1 // 4) as g:
                    dve.wait_ge(*count("e1_combined", g * 4 + 1))
                    dve.tensor_copy(gcur, gated_T[:, bass.ds(g, 1), :].rearrange("p o s -> p (o s)")).then_inc(inc("e1_gated"), 1)
                    for e4 in range(4):
                        dve.wait_ge(*count("e1_sigmoid", g * 4 + (e4 + 1)))
                        dve.tensor_tensor(hid[0:64], hid[0:64], gate_ps, ALU.mult).then_inc(inc("e1_silu"), 1)
                        dve.wait_ge(*count("e1_silu", g * 4 + (e4 + 1)))
                        dve.wait_ge(*count("e1_up", g * 4 + (e4 + 1)))
                        dve.tensor_tensor(hid[0:64], hid[0:64], up_ps, ALU.mult).then_inc(inc("e1_hid"), 1)
                        dve.tensor_copy(flat, xin_e[:, bass.ds(g * 4 + (e4 + 1), 1)].rearrange("p o s -> p (o s)"))\
                           .then_inc(inc("e1_x"), 1)
                    for j in range(4):
                        dve.wait_ge(*count("e1_combined", g * 4 + (j + 2)))
                        part = x_sb[:, j // 2, 512 * (j % 2):512 * (j % 2) + 512]
                        dve.tensor_tensor(part, part, bank(5 + j % 2), ALU.add).then_inc(inc("e1_added"), 1)

            return Stage(tensor=tensor, vector=vector, scalar=scalar, sync=sync,
                         held=("e1_x", "e1_g", "e1_hid", "e1_hid_T", "e1_y", "gated_T", "xin"))

        moe1 = experts1()
        cols.release("h2", "h2T", "scratch2", "chosen", "gated")
        def ssm_setup():
            names = ("dt", "x", "y", "p", "em1", "mag", "half", "turns", "s", "c", "sin", "cosm1", "cos", "lre1",
                     "lim", "den", "t0", "t1", "cre", "cim", "en_c", "en_s", "sq_c", "sq_s")
            v = {n: tiny(ST) for n in names}
            a_re, a_im = vec["a_re"], vec["a_im"]
            two_pi = 2 * np.pi
            hi = float(np.float32(6.28125))
            lo = float(two_pi - hi)
            magic = float(1.5 * 2 ** 23)

            def scalar(act):
                act.wait_ge(*count("const_loaded", 48))
                act.activation(v["dt"], vec["log_dt"], ACT.Exp).then_inc(inc("ssm_dt"), 1)
                act.wait_ge(*count("ssm_half", 1))
                act.activation(v["s"], v["half"], ACT.Sin)
                act.activation(v["c"], v["t0"], ACT.Sin).then_inc(inc("ssm_sines"), 1)

            def vector(dve):
                step = vchain(dve)
                dve.wait_ge(*count("const_loaded", 48))
                dve.wait_ge(*count("ssm_dt", 1))
                step(dve.tensor_tensor(v["x"], a_re, v["dt"], ALU.mult))
                step(dve.tensor_scalar(v["x"], v["x"], 88.0, -100.0, ALU.min, ALU.max))
                step(dve.tensor_scalar(v["y"], v["x"], 1.0 / 128, None, ALU.mult))
                step(dve.tensor_scalar(v["p"], v["y"], 1.0 / 8, 1.0, ALU.mult, ALU.add))
                for n in range(7, 1, -1):
                    step(dve.tensor_tensor(v["p"], v["p"], v["y"], ALU.mult))
                    step(dve.tensor_scalar(v["p"], v["p"], 1.0 / n, 1.0, ALU.mult, ALU.add))
                step(dve.tensor_tensor(v["em1"], v["p"], v["y"], ALU.mult))
                for _ in range(7):
                    step(dve.scalar_tensor_tensor(v["em1"], v["em1"], 2.0, v["em1"], ALU.add, ALU.mult))
                step(dve.tensor_scalar(v["mag"], v["em1"], 1.0, None, ALU.add))
                step(dve.tensor_tensor(v["y"], a_im, v["dt"], ALU.mult))
                step(dve.tensor_scalar(v["turns"], v["y"], 1 / two_pi, magic, ALU.mult, ALU.add))
                step(dve.tensor_scalar(v["turns"], v["turns"], magic, None, ALU.subtract))
                step(dve.scalar_tensor_tensor(v["y"], v["turns"], -hi, v["y"], ALU.mult, ALU.add))
                step(dve.scalar_tensor_tensor(v["y"], v["turns"], -lo, v["y"], ALU.mult, ALU.add))
                step(dve.tensor_scalar(v["half"], v["y"], 0.5, 1.5707963, ALU.mult, ALU.min))
                step(dve.tensor_scalar(v["half"], v["half"], -1.5707963, None, ALU.max))
                step(dve.tensor_scalar(v["t1"], v["half"], -1.0, None, ALU.mult))
                step(dve.tensor_tensor(v["t1"], v["t1"], v["half"], ALU.max))
                dve.tensor_scalar(v["t0"], v["t1"], -1.0, float(np.pi / 2), ALU.mult, ALU.add).then_inc(inc("ssm_half"), 1)
                dve.wait_ge(*count("ssm_sines", 1))
                dve.scalar_tensor_tensor(v["sin"], v["s"], 2.0, v["c"], ALU.mult, ALU.mult)
                step(dve.scalar_tensor_tensor(v["cosm1"], v["s"], -2.0, v["s"], ALU.mult, ALU.mult))
                step(dve.tensor_scalar(v["cos"], v["cosm1"], 1.0, None, ALU.add))
                step(dve.tensor_tensor(v["lre1"], v["em1"], v["cos"], ALU.mult))
                step(dve.tensor_tensor(v["lre1"], v["lre1"], v["cosm1"], ALU.add))
                step(dve.tensor_tensor(v["lim"], v["mag"], v["sin"], ALU.mult))
                step(dve.tensor_tensor(v["den"], a_re, a_re, ALU.mult))
                step(dve.tensor_tensor(v["t1"], a_im, a_im, ALU.mult))
                step(dve.tensor_tensor(v["den"], v["den"], v["t1"], ALU.add))
                step(dve.reciprocal(v["den"], v["den"]))
                step(dve.tensor_tensor(v["cre"], v["lre1"], a_re, ALU.mult))
                step(dve.tensor_tensor(v["t1"], v["lim"], a_im, ALU.mult))
                step(dve.tensor_tensor(v["cre"], v["cre"], v["t1"], ALU.add))
                step(dve.tensor_tensor(v["cre"], v["cre"], v["den"], ALU.mult))
                step(dve.tensor_tensor(v["cim"], v["lim"], a_re, ALU.mult))
                step(dve.tensor_tensor(v["t1"], v["lre1"], a_im, ALU.mult))
                step(dve.tensor_tensor(v["cim"], v["cim"], v["t1"], ALU.subtract))
                dve.tensor_tensor(v["cim"], v["cim"], v["den"], ALU.mult).then_inc(inc("ssm_params"), 1)

            return Stage(vector=vector, scalar=scalar, mag=v["mag"], v=v)

        ssm_par = ssm_setup()

        def ssm_tables():
            v = ssm_par.v
            cos3, sin3 = ssm_cos, ssm_sin

            def scalar(act):
                act.wait_ge(*count("r_xin", KD))
                act.wait_ge(*count("r_gated_turned", 1))
                act.dma_start(bc_sb, D["ssm_bc"]).then_inc(inc("ssm_bc_loaded"), 16)

            def gpsimd(pool):
                step = gchain(pool)
                pool.wait_ge(*count("ssm_params", 1))
                pool.wait_ge(*count("r_xin", KD))
                pool.wait_ge(*count("r_gated_turned", 1))
                pool.wait_ge(*count("ssm_bc_loaded", 16))
                mul = lambda o, a, b: step(pool.tensor_tensor(o, a, b, ALU.mult))
                b_re, b_im, c_re, c_im = (bc_sb[:, 512 * j:512 * j + 512] for j in range(4))
                r3 = lambda a: a.rearrange("p (s c) -> p s c", s=ST)
                t3 = ssm_tmp[:, 0:512]
                cre, cim = (along(v[n], 32, 2) for n in ("cre", "cim"))
                mul(r3(bb_re), r3(b_re), cre)
                mul(r3(t3), r3(b_im), cim)
                step(pool.tensor_tensor(bb_re, bb_re, t3, ALU.subtract))
                mul(r3(bb_im), r3(b_im), cre)
                mul(r3(t3), r3(b_re), cim)
                step(pool.tensor_tensor(bb_im, bb_im, t3, ALU.add))
                step(pool.tensor_scalar(b_re, c_re, -1.0, None, ALU.mult))
                step(pool.tensor_scalar(b_im, c_im, -1.0, None, ALU.mult))
                step(pool.memset(cos3[:, :, 0:1], 1.0))
                step(pool.memset(sin3[:, :, 0:1], 0.0))
                step(pool.tensor_copy(v["en_c"], v["cos"]))
                step(pool.tensor_copy(v["en_s"], v["sin"]))
                for m in range(8):
                    n = 1 << m
                    for a in range(0, n, 64):
                        w = min(n, 64)
                        ec, es = along(v["en_c"], w, 2), along(v["en_s"], w, 2)
                        c0, s0 = cos3[:, :, a:a + w], sin3[:, :, a:a + w]
                        c1, s1 = cos3[:, :, n + a:n + a + w], sin3[:, :, n + a:n + a + w]
                        tmp = ssm_tmp[:, 0:ST * w].rearrange("p (s c) -> p s c", s=ST)
                        mul(c1, c0, ec)
                        mul(tmp, s0, es)
                        step(pool.tensor_tensor(c1, c1, tmp, ALU.subtract))
                        mul(s1, s0, ec)
                        mul(tmp, c0, es)
                        step(pool.tensor_tensor(s1, s1, tmp, ALU.add))
                    mul(v["sq_c"], v["en_c"], v["en_c"])
                    mul(v["sq_s"], v["en_s"], v["en_s"])
                    mul(v["en_s"], v["en_s"], v["en_c"])
                    step(pool.tensor_tensor(v["en_c"], v["sq_c"], v["sq_s"], ALU.subtract))
                    step(pool.tensor_tensor(v["en_s"], v["en_s"], v["en_s"], ALU.add))
                pool.sem_inc(inc("ssm_tables"), 1)

            return Stage(gpsimd=gpsimd, scalar=scalar)

        bc_sb = cols.take("bc", 2048, top=True)
        bb = cols.take("bb", 1024, top=True)
        bb_re, bb_im = bb[:, 0:512], bb[:, 512:1024]
        ssm_cos = cols.take("ssm_cos", ST * SEQ, top=True).rearrange("p (s c) -> p s c", s=ST)
        ssm_sin = cols.take("ssm_sin", ST * SEQ, top=True).rearrange("p (s c) -> p s c", s=ST)
        ssm_tmp = cols.take("ssm_tmp", 1024, top=True)
        ssm_tab = ssm_tables()
        cols.release(*moe1.held, "ssm_tmp")

        def load_block2(sp):
            for n, unit in enumerate(b2):
                load_unit(sp, U_B2 + n, unit)

        x1T = cols.take("x1T", KD * SEQ).rearrange("p (k s) -> p k s", k=KD)
        turn3 = transpose_rows("b2", x_sb, x1T, ("e1_added", E1 + 1))
        uT = cols.take("uT", 4 * SEQ, top=True).rearrange("p (c s) -> p c s", c=4)
        proj_u = project("pu", x1T, ("b2_T", KD // 2),
                         [(U_SSM, "T", s, 512, KD, uT[:, 2 * s:2 * s + 2]) for s in range(2)])

        def ssm():
            bT = cols.take("bT", 1024, top=True).rearrange("p (r q s) -> p r q s", r=2, q=4)
            xs = [cols.take(f"ssm_x{j}", 1024, top=True).rearrange("p (r s) -> p r s", r=2) for j in range(2)]
            ts = cols.take("ssm_t", 1024, top=True).rearrange("p (r s) -> p r s", r=2)
            pr = cols.take("ssm_p", 2048, top=True).rearrange("p (r s) -> p r s", r=4)
            yT = bb.rearrange("p (c s) -> p c s", c=4)
            c_re, nc_re, nc_im = bc_sb[:, 1024:1536], bc_sb[:, 0:512], bc_sb[:, 512:1024]
            flat_cos, flat_sin = (a.rearrange("p s c -> p (s c)") for a in (ssm_cos, ssm_sin))
            mag = ssm_par.mag
            HB = ST // 2

            def tensor(pe):
                pe.wait_ge(*count("ssm_tables", 1))
                pe.wait_ge(*count("pu_out0", 1))
                pe.wait_ge(*count("pu_out1", 1))
                for r, src in enumerate((bb_re, bb_im)):
                    for q in range(4):
                        mm = pe.transpose(bank(r)[:, q * P:(q + 1) * P], src[:, q * P:(q + 1) * P], ident)
                    mm.then_inc(inc("ssm_b_turned"), 1)
                pe.wait_ge(*count("ssm_bT", 1))

                def drive(s):
                    if s >= 2:
                        pe.wait_ge(*count("ssm_rotated", s - 1))
                    for r in range(2):
                        for i in range(2):
                            tile = 2 * s + i
                            rows = slice(32 * (tile % 4), 32 * (tile % 4) + 32)
                            mm = pe.matmul(bank(2 * (s % 2) + i)[:, r * SEQ:(r + 1) * SEQ], bT[rows, r, tile // 4],
                                           uT[rows, tile // 4], start=True, stop=True)
                    mm.then_inc(inc("ssm_driven"), 1)

                def emit(s):
                    pe.wait_ge(*count("ssm_products", s + 1))
                    q = s // 2
                    if s % 2 == 0 and q >= 2:
                        pe.wait_ge(*count("ssm_y", q - 1))
                    for i in range(2):
                        tile = 2 * s + i
                        o = bank(4 + q % 2)[32 * (tile % 4):32 * (tile % 4) + 32, 0:SEQ]
                        for n, c in enumerate((c_re, nc_re, nc_im, nc_im)):
                            mm = pe.matmul(o, c[:, 32 * tile:32 * tile + 32], pr[:, n, i * SEQ:(i + 1) * SEQ],
                                           start=(n == 0), stop=(n == 3))
                    mm.then_inc(inc("ssm_emitted"), 1)

                drive(0)
                for s in range(HB):
                    if s + 1 < HB:
                        drive(s + 1)
                    emit(s)

            def vector(dve):
                step = vchain(dve)
                dve.wait_ge(*count("ssm_tables", 1))
                dve.wait_ge(*count("ssm_b_turned", 2))
                dve.tensor_copy(bT.rearrange("p r q s -> p (r q s)"), banks(0, 2)).then_inc(inc("ssm_bT"), 1)

                def finish(q):
                    dve.wait_ge(*count("ssm_emitted", 2 * q + 2))
                    dve.scalar_tensor_tensor(yT[:, q], uT[:, q], vec["ssm_d"][:, q:q + 1], bank(4 + q % 2)[:, 0:SEQ],
                                             ALU.mult, ALU.add).then_inc(inc("ssm_y"), 1)

                for s in range(HB):
                    c, sn = flat_cos[:, 512 * s:512 * s + 512], flat_sin[:, 512 * s:512 * s + 512]
                    driven = banks(2 * (s % 2), 2).rearrange("p (i r s) -> p i r s", i=2, r=2)
                    re, im, x = driven[:, :, 0], driven[:, :, 1], xs[s % 2].rearrange("p r (i s) -> p r i s", i=2)
                    c, sn = (a.rearrange("p (i s) -> p i s", i=2) for a in (c, sn))
                    ts_ = ts.rearrange("p r (i s) -> p r i s", i=2)
                    dve.wait_ge(*count("ssm_driven", s + 1))
                    if s >= 2:
                        dve.wait_ge(*count("ssm_products", s - 1))
                    dve.tensor_tensor(x[:, 0], re, c, ALU.mult)
                    dve.tensor_tensor(ts_[:, 0], im, sn, ALU.mult)
                    dve.tensor_tensor(x[:, 1], im, c, ALU.mult)
                    dve.tensor_tensor(ts_[:, 1], re, sn, ALU.mult).then_inc(inc("ssm_rotated"), 1)
                    dve.wait_ge(*count("ssm_rotated", s + 1))
                    dve.tensor_tensor(x[:, 0], x[:, 0], ts_[:, 0], ALU.add)
                    step(dve.tensor_tensor(x[:, 1], x[:, 1], ts_[:, 1], ALU.subtract))
                    for r in range(2):
                        for i in range(2):
                            tile = 2 * s + i
                            part = x[:, r, i]
                            last = dve.tensor_tensor_scan(part, mag[:, tile:tile + 1].broadcast_to([P, SEQ]), part,
                                                          0.0, ALU.mult, ALU.add)
                    last.then_inc(inc("ssm_scanned"), 1)
                    if s % 2 and s >= 3:
                        finish(s // 2 - 1)
                finish(3)
                y = yT.rearrange("p c s -> p (c s)")
                inner = ts.rearrange("p r s -> p (r s)")
                dve.wait_ge(*count("ssm_y", 4))
                step(dve.tensor_tensor(inner, y, y, ALU.mult))
                step(dve.tensor_scalar(inner, inner, 0.044715, 1.0, ALU.mult, ALU.add))
                dve.tensor_tensor(inner, inner, y, ALU.mult).then_inc(inc("ssm_gelu_inner"), 1)
                dve.wait_ge(*count("ssm_gelu_sigmoid", 1))
                dve.tensor_tensor(y, y, inner, ALU.mult).then_inc(inc("ssm_gelu"), 1)

            def scalar(act):
                inner = ts.rearrange("p r s -> p (r s)")
                act.wait_ge(*count("ssm_gelu_inner", 1))
                act.activation(inner, inner, ACT.Sigmoid, scale=float(2 * np.sqrt(2 / np.pi))).then_inc(inc("ssm_gelu_sigmoid"), 1)

            def gpsimd(pool):
                for s in range(HB):
                    c, sn = flat_cos[:, 512 * s:512 * s + 512], flat_sin[:, 512 * s:512 * s + 512]
                    x = xs[s % 2]
                    pool.wait_ge(*count("ssm_scanned", s + 1))
                    if s >= 1:
                        pool.wait_ge(*count("ssm_emitted", s))
                    pool.tensor_tensor(pr[:, 0], x[:, 0], c, ALU.mult)
                    pool.tensor_tensor(pr[:, 1], x[:, 1], sn, ALU.mult)
                    pool.tensor_tensor(pr[:, 2], x[:, 0], sn, ALU.mult)
                    pool.tensor_tensor(pr[:, 3], x[:, 1], c, ALU.mult).then_inc(inc("ssm_products"), 1)

            cols.release("bc", "ssm_cos", "ssm_sin", "ssm_x0", "ssm_x1", "ssm_t", "ssm_p", "bT", "uT")
            return Stage(tensor=tensor, vector=vector, scalar=scalar, gpsimd=gpsimd, y=yT)

        ssm_scan = ssm()
        zg = cols.take("zg", 2048, top=True).rearrange("p (c s) -> p c s", c=8)
        glu_proj = project("pg", ssm_scan.y, ("ssm_gelu", 1),
                           [(U_GLU, "T", s, 1024, 4, zg[:, 2 * s:2 * s + 2]) for s in range(4)])
        ycT = cols.take("ycT", 1024).rearrange("p (c s) -> p c s", c=4)

        def glu_gate():
            def scalar(act):
                for sem, n in glu_proj.done:
                    act.wait_ge(*count(sem, n))
                for c in range(4):
                    ins = act.activation(zg[:, 4 + c], zg[:, 4 + c], ACT.Sigmoid, bias=vec["glu_b"][:, 4 + c:5 + c])
                ins.then_inc(inc("glu_sigmoid"), 1)

            def vector(dve):
                for sem, n in glu_proj.done:
                    dve.wait_ge(*count(sem, n))
                dve.wait_ge(*count("glu_sigmoid", 1))
                for c in range(4):
                    ins = dve.scalar_tensor_tensor(ycT[:, c], zg[:, c], vec["glu_b"][:, c:c + 1], zg[:, 4 + c],
                                                   ALU.add, ALU.mult)
                ins.then_inc(inc("glu_out"), 1)

            return Stage(vector=vector, scalar=scalar)

        glu = glu_gate()
        cols.release("bb", "zg")
        rkv = cols.take("rkv", NT * 3 * HW).rearrange("p (t c) -> p t c", t=NT)
        lora_z = cols.take("lora_z", 2 * (SEQ + 1), top=True).rearrange("p (e s) -> p e s", e=2)
        jobs = [(U_RWKV + c, "tok", t, 512, KD, rkv[:, t, 512 * c:512 * (c + 1)]) for c in range(3) for t in range(NT)]
        jobs += [(U_LORA, "T", 0, 256, KD, lora_z[:, :, 1:SEQ + 1])]
        proj_rkv = project("pr", x1T, ("glu_out", 1), jobs)

        def rwkv():
            take = lambda n, w, top=False: cols.take("rw_" + n, w, top)
            tok = lambda n, top=False: take(n, 1024, top).rearrange("p (t c) -> p t c", t=NT)
            rv = {n: take(n, HW) for n in ("gn_w", "gn_b")}
            gg, aa, kk = tok("g"), tok("a"), tok("kk")
            prev = take("prev", 3072, True).rearrange("p (t c) -> p t c", t=NT)
            mu = take("mu", 1536, True)
            rv |= {n: take(n, HW, True) for n in ("w0", "a0", "k_k", "k_a", "r_k")}
            wa, wg = take("wa", HW, True), take("wg", HW, True)
            lz = take("lz", 2 * SEQ, True).rearrange("p (e s) -> p e s", e=2)
            cols.release("rw_prev")
            ld, e1 = tok("ld", True), tok("e1", True)
            flat = lambda a: a.rearrange("p t c -> p (t c)")
            heads = lambda a: a.rearrange("p t (h d) -> p t h d", d=HD)
            r_, k_, v_ = (rkv[:, :, 512 * j:512 * j + 512] for j in range(3))
            ms, sd, bonus, pc = tiny(16), tiny(16), tiny(16), tiny(16)
            cols.release("rw_mu", "rw_w0", "rw_a0", "rw_wa", "rw_wg", "rw_lz", "lora_z")
            e2 = tok("e2", True)
            cols.release("rw_ld", "rw_e1", "rw_e2", "rw_k_k", "rw_k_a", "rw_r_k")
            arT = take("arT", 2048).rearrange("p (q c w s) -> p q c w s", q=4, c=NCH, w=2)
            bT, kT = (take(n, 1024).rearrange("p (q s) -> p q s", q=4) for n in ("bT", "kT"))
            mB, mK = (take(n, 2048).rearrange("p (t g s) -> p t g s", t=NT, g=HEADS) for n in ("mB", "mK"))
            cols.release("rw_kk")
            L = take("L", 1024).rearrange("p (t g s) -> p t g s", t=NT, g=HEADS)
            cols.release("rw_bT", "rw_kT")
            D_, DT, Ws, Cs = (take(n, 1024).rearrange("p (t g s) -> p t g s", t=NT, g=HEADS) for n in ("D", "DT", "W", "C"))
            cols.release("rw_D", "rw_W", "rw_C", "rw_L")
            xv = tok("xv")
            x_s, u_s = take("x", HW), take("u", HW)
            state = take("state", 256).rearrange("p (q i) -> p q i", q=4)
            y_sb = tok("y")
            ysq = xv
            flat4 = lambda a: a.rearrange("p t g s -> p (t g) s")
            both, after, eye = const("before_upto"), const("after"), const("eye64")
            lower = const("lower").rearrange("p (m s) -> p m s", m=6)
            upper = const("upper").rearrange("p (m s) -> p m s", m=6)
            all_heads = [(h % 2, h // 2, (h % 2) * 4 + h // 2, h) for h in range(HEADS)]

            def rows_of(par):
                return slice(64 * par, 64 * par + 64)

            def scalar(act):
                act.wait_ge(*count("glu_out", 1))
                for n, tile in [("mu", mu)] + [(n, rv[n]) for n in ("w0", "a0", "k_k", "k_a", "r_k", "gn_w", "gn_b")]:
                    act.dma_start(tile, row_source(n, n)).then_inc(inc("rw_rows_loaded"), 16)
                act.dma_start(wa, D["lora_wa"]).then_inc(inc("rw_lora_loaded"), 16)
                act.dma_start(wg, D["lora_g"]).then_inc(inc("rw_lora_loaded"), 16)
                proj_rkv.scalar(act)
                for sem, n in proj_rkv.done:
                    act.wait_ge(*count(sem, n))
                for t in range(NT):
                    act.dma_start(prev[1:P, t], rkv[0:P - 1, t]).then_inc(inc("rw_shifted"), 16)
                act.dma_start(prev[0:1, 1], rkv[P - 1:P, 0]).then_inc(inc("rw_shifted"), 16)
                act.wait_ge(*count("rw_lora", 1))
                act.activation(lz[0:64, 0], lz[0:64, 0], ACT.Tanh)
                act.activation(lz[:, 1], lz[:, 1], ACT.Sigmoid).then_inc(inc("rw_lora_act"), 1)
                act.wait_ge(*count("rw_lora_out", 3))
                act.activation(flat(gg), banks(4, 2), ACT.Copy).then_inc(inc("rw_gate"), 1)
                for n, a in enumerate((ld, aa)):
                    act.wait_ge(*count("rw_pre", n + 1))
                    act.activation(flat(a), flat(a), ACT.Sigmoid).then_inc(inc("rw_post"), 1)
                act.wait_ge(*count("rw_ms", 1))
                act.activation(sd, ms, ACT.Sqrt).then_inc(inc("rw_sd"), 1)
                act.wait_ge(*count("rw_cum", 1))
                act.wait_ge(*count("rw_bonus", 1))
                act.activation(flat(e1), banks(0, 2), ACT.Exp).then_inc(inc("rw_exp"), 1)
                act.activation(flat(e2), banks(0, 2), ACT.Exp, scale=-1.0).then_inc(inc("rw_exp"), 1)
                act.activation(pc, bank(2)[:, 0:16], ACT.Exp).then_inc(inc("rw_exp"), 1)
                act.wait_ge(*count("rw_cum_before", 1))
                act.activation(flat(ld), flat(ld), ACT.Exp).then_inc(inc("rw_exp"), 1)
                for m in range(1, 6):
                    act.wait_ge(*count("rw_W", m))
                    act.activation(Ws.rearrange("p t g s -> p (t g s)"), banks(0, 2), ACT.Copy).then_inc(inc("rw_W_out"), 1)
                for c in range(NCH):
                    R, t = rows_of(c % 2), c // 2
                    act.wait_ge(*count("rw_u", c + 1))
                    act.activation(u_s[R], bank(2)[R], ACT.Copy).then_inc(inc("rw_u_out"), 1)
                    act.wait_ge(*count("rw_y2", c + 1))
                    act.activation(y_sb[R, t], bank(6)[R], ACT.Copy).then_inc(inc("rw_y2_out"), 1)
                for n in range(2):
                    act.wait_ge(*count("rw_gn_ms", 1))
                act.activation(sd, ms, ACT.Sqrt).then_inc(inc("rw_gn_sd"), 1)

            def tensor(pe):
                pe.wait_ge(*count("rw_lora_act", 1))
                pe.wait_ge(*count("rw_lora_loaded", 32))
                for n, (lhs, rhs) in enumerate(((lz[0:64, 0], wa[0:64]), (lz[64:128, 0], wa[64:128]), (lz[:, 1], wg))):
                    for t in range(NT):
                        mm = pe.matmul(bank(2 * n + t), lhs[:, t * P:(t + 1) * P], rhs, start=True, stop=True)
                    mm.then_inc(inc("rw_lora_out"), 1)
                pe.wait_ge(*count("rw_decay", 1))
                for t in range(NT):
                    pe.matmul(bank(t), const("cumsum"), ld[:, t], start=True, stop=True)
                    for q in range(4):
                        mm = pe.matmul(bank(2)[:, 4 * q + 2 * t:4 * q + 2 * t + 2], ld[:, t, q * P:(q + 1) * P],
                                       const("chunk_sum"), start=True, stop=True)
                mm.then_inc(inc("rw_cum"), 1)
                pe.wait_ge(*count("rw_scaled", 1))
                for j in range(8):
                    src, half = (kk, r_, aa, k_)[j // 2], j % 2
                    if j >= 4:
                        pe.wait_ge(*count("rw_T", j - 3))
                    for q in (2 * half, 2 * half + 1):
                        for t in range(NT):
                            mm = pe.transpose(bank(3 + j % 4)[:, (q % 2) * SEQ + t * P:(q % 2) * SEQ + (t + 1) * P],
                                              src[:, t, q * P:(q + 1) * P], ident)
                    mm.then_inc(inc("rw_turned"), 1)
                pe.wait_ge(*count("rw_T", 8))
                for j in range(10):
                    if j >= 6:
                        pe.wait_ge(*count("rw_products_out", j - 5))
                    b = bank(j % 6)
                    if j < 8:
                        src, t, par = (bT, kT)[j // 4], j // 2 % 2, j % 2
                        for hh in range(4):
                            for c2 in range(2):
                                c = 2 * t + c2
                                mm = pe.matmul(b[rows_of(c2), hh * P:(hh + 1) * P], src[rows_of(par), hh, c * CH:(c + 1) * CH],
                                               arT[rows_of(par), hh, c].rearrange("p w s -> p (w s)"), start=True, stop=True)
                    else:
                        par = j - 8
                        for c in range(NCH):
                            for hh in range(4):
                                o = (c // 2) * 256 + hh * 64
                                mm = pe.matmul(b[rows_of(c % 2), o:o + 64], arT[rows_of(par), hh, c, 0],
                                               bT[rows_of(par), hh, c * CH:(c + 1) * CH], start=True, stop=True)
                    mm.then_inc(inc("rw_products"), 1)
                grid = [(t, g, c2) for t in range(NT) for g in range(HEADS) for c2 in range(2)]

                def each(b0, lhs, rhs, sem):
                    for t, g, c2 in grid:
                        R = rows_of(c2)
                        mm = pe.matmul(bank(b0 + t)[R, g * 64:(g + 1) * 64], lhs[R, t, g], rhs[R, t, g], start=True, stop=True)
                    mm.then_inc(inc(sem), 1)

                for m in range(1, 6):
                    pe.wait_ge(*count("rw_inv", m))
                    each(0, Cs, D_, "rw_W")
                    pe.wait_ge(*count("rw_W_out", m))
                    if m < 5:
                        each(2, DT, Ws, "rw_DW")
                    each(4, Ws, DT, "rw_WD")
                for t, g, c2 in grid:
                    R, h = rows_of(c2), 2 * (g % 4) + g // 4
                    mm = pe.matmul(bank(6 + t)[R, h * 64:(h + 1) * 64], mK[R, t, g, 0:64], v_[R, t, h * 64:(h + 1) * 64],
                                   start=True, stop=True)
                mm.then_inc(inc("rw_xv"), 1)
                for c in range(NCH):
                    R, t = rows_of(c % 2), c // 2
                    pe.wait_ge(*count("rw_state", c + 1))
                    if c >= 1:
                        pe.wait_ge(*count("rw_y", c))
                    else:
                        pe.wait_ge(*count("rw_xv_out", 1))
                        pe.wait_ge(*count("rw_inv", 6))
                    for w, b0, sem in ((0, 0, "rw_x1"), (1, 4, "rw_y1")):
                        for par, hh, g, h in all_heads:
                            mm = pe.matmul(bank(b0 + par)[R, hh * 64:(hh + 1) * 64], arT[rows_of(par), hh, c, w],
                                           state[rows_of(par), hh], start=True, stop=True)
                        mm.then_inc(inc(sem), 1)
                    pe.wait_ge(*count("rw_x", c + 1))
                    for par, hh, g, h in all_heads:
                        mm = pe.matmul(bank(2)[R, h * 64:(h + 1) * 64], DT[R, t, g], x_s[R, h * 64:(h + 1) * 64], start=True, stop=True)
                    mm.then_inc(inc("rw_u"), 1)
                    pe.wait_ge(*count("rw_u_out", c + 1))
                    for par, hh, g, h in all_heads:
                        o, hc = bank(3)[rows_of(par), hh * 64:(hh + 1) * 64], slice(h * 64, (h + 1) * 64)
                        pe.matmul(o, aa[R, t, hc], u_s[R, hc], start=True, stop=False)
                        mm = pe.matmul(o, k_[R, t, hc], v_[R, t, hc], start=False, stop=True)
                    mm.then_inc(inc("rw_s"), 1)
                    for par, hh, g, h in all_heads:
                        o, hc = bank(6)[R, h * 64:(h + 1) * 64], slice(h * 64, (h + 1) * 64)
                        pe.matmul(o, mB[R, t, g, 64:128], u_s[R, hc], start=True, stop=False)
                        mm = pe.matmul(o, mK[R, t, g, 64:128], v_[R, t, hc], start=False, stop=True)
                    mm.then_inc(inc("rw_y2"), 1)
                pe.wait_ge(*count("rw_y_rows", 1))
                for j in range(2):
                    for q in (2 * j, 2 * j + 1):
                        for t in range(NT):
                            mm = pe.transpose(bank(j)[:, (q % 2) * SEQ + t * P:(q % 2) * SEQ + (t + 1) * P],
                                              y_sb[:, t, q * P:(q + 1) * P], ident)
                    mm.then_inc(inc("rw_y_turned"), 1)

            def gpsimd(pool):
                pass

            def vector(dve):
                step = vchain(dve)
                TT, mul, add, sub = dve.tensor_tensor, ALU.mult, ALU.add, ALU.subtract
                two = lambda a: along(a, NT, 1)
                dve.wait_ge(*count("glu_out", 1))
                dve.memset(lora_z[:, :, 0:1], 0.0)
                proj_rkv.vector(dve)
                dve.memset(prev[0:1, 0], 0.0)
                for sem, n in proj_rkv.done:
                    dve.wait_ge(*count(sem, n))
                step(TT(lz, lora_z[:, :, 0:SEQ], lora_z[:, :, 1:SEQ + 1], sub))
                for e in range(2):
                    last = dve.scalar_tensor_tensor(lz[:, e], lz[:, e], vec["mu_lora"][:, e:e + 1], lora_z[:, e, 1:SEQ + 1], mul, add)
                last.then_inc(inc("rw_lora"), 1)
                dve.wait_ge(*count("rw_shifted", 48))
                dve.wait_ge(*count("rw_rows_loaded", 16 * 8))
                step(TT(prev, prev, rkv, sub))
                step(TT(prev, prev, two(mu), mul))
                step(TT(rkv, rkv, prev, add))
                dve.wait_ge(*count("rw_lora_out", 3))
                TT(ld, banks(0, 2).rearrange("p (t c) -> p t c", t=NT), two(rv["w0"]), add).then_inc(inc("rw_pre"), 1)
                TT(aa, banks(2, 2).rearrange("p (t c) -> p t c", t=NT), two(rv["a0"]), add).then_inc(inc("rw_pre"), 1)
                dve.wait_ge(*count("rw_post", 1))
                dve.tensor_scalar(ld, ld, -float(np.exp(-0.5)), None, mul).then_inc(inc("rw_decay"), 1)
                step(TT(kk, k_, two(rv["k_k"]), mul))
                step(TT(e1, kk, kk, mul))
                step(dve.tensor_reduce(ms, flat(e1).rearrange("p (h d) -> p h d", d=HD), AXX, add))
                dve.tensor_scalar(ms, ms, 1e-24, None, ALU.max).then_inc(inc("rw_ms"), 1)
                dve.wait_ge(*count("rw_post", 2))
                step(dve.tensor_scalar(e1, aa, 1.0, None, sub))
                step(TT(e1, e1, two(rv["k_a"]), mul))
                step(dve.tensor_scalar(e1, e1, 1.0, None, add))
                step(TT(k_, k_, e1, mul))
                step(TT(e1, r_, k_, mul))
                step(TT(e1, e1, two(rv["r_k"]), mul))
                dve.tensor_reduce(bonus, flat(e1).rearrange("p (h d) -> p h d", d=HD), AXX, add).then_inc(inc("rw_bonus"), 1)
                dve.wait_ge(*count("rw_sd", 1))
                step(dve.reciprocal(sd, sd))
                kh = flat(kk).rearrange("p (h d) -> p h d", d=HD)
                step(TT(kh, kh, along(sd, HD, 2), mul))
                step(TT(aa, aa, kk, mul))
                dve.wait_ge(*count("rw_exp", 2))
                TT(ld, banks(0, 2).rearrange("p (t c) -> p t c", t=NT), ld, sub).then_inc(inc("rw_cum_before"), 1)
                TT(r_, r_, e1, mul)
                TT(aa, aa, e2, mul)
                TT(k_, k_, e2, mul)
                dve.wait_ge(*count("rw_exp", 4))
                dve.scalar_tensor_tensor(flat(kk), flat(kk), -1.0, flat(ld), mul, mul).then_inc(inc("rw_scaled"), 1)
                for j in range(8):
                    dve.wait_ge(*count("rw_turned", j + 1))
                    which, half = j // 2, j % 2
                    src = bank(3 + j % 4).rearrange("p (q s) -> p q s", q=2)
                    if which < 2:
                        for q in range(2):
                            last = dve.tensor_copy(arT[:, 2 * half + q, :, which], src[:, q].rearrange("p (c s) -> p c s", c=NCH))
                    else:
                        last = dve.tensor_copy((bT, kT)[which - 2][:, 2 * half:2 * half + 2], src)
                    last.then_inc(inc("rw_T"), 1)
                for j in range(10):
                    dve.wait_ge(*count("rw_products", j + 1))
                    b = bank(j % 6)
                    if j < 8:
                        out, t, par = (mB, mK)[j // 4], j // 2 % 2, j % 2
                        ins = TT(out[:, t, 4 * par:4 * par + 4], b.rearrange("p (g s) -> p g s", g=4), along(both, 4, 1), mul)
                    else:
                        par = j - 8
                        for t in range(NT):
                            ins = TT(L[:, t, 4 * par:4 * par + 4], b[:, 256 * t:256 * t + 256].rearrange("p (g s) -> p g s", g=4),
                                     along(after, 4, 1), mul)
                    ins.then_inc(inc("rw_products_out"), 1)
                dve.wait_ge(*count("rw_products_out", 10))
                LT = mB[:, :, :, 0:64].rearrange("p t g s -> p (t g) s")
                m16 = lambda a: along(a, 16, 1)
                TT(flat4(D_), flat4(L), m16(lower[:, 0]), mul)
                step(TT(flat4(DT), LT, m16(upper[:, 0]), mul))
                TT(flat4(D_), flat4(D_), m16(eye), add)
                TT(flat4(DT), flat4(DT), m16(eye), add)
                TT(flat4(Cs), LT, m16(upper[:, 1]), mul).then_inc(inc("rw_inv"), 1)
                for m in range(1, 6):
                    if m < 5:
                        dve.wait_ge(*count("rw_DW", m))
                        dve.wait_ge(*count("rw_WD", m))
                        TT(flat4(Cs), LT, m16(upper[:, m + 1]), mul)
                        TT(D_.rearrange("p t g s -> p (t g s)"), D_.rearrange("p t g s -> p (t g s)"), banks(2, 2), add)
                    else:
                        dve.wait_ge(*count("rw_WD", m))
                    TT(DT.rearrange("p t g s -> p (t g s)"), DT.rearrange("p t g s -> p (t g s)"), banks(4, 2), add)\
                        .then_inc(inc("rw_inv"), 1)
                dve.wait_ge(*count("rw_xv", 1))
                dve.tensor_copy(flat(xv), banks(6, 2)).then_inc(inc("rw_xv_out"), 1)
                dve.wait_ge(*count("rw_xv_out", 1))
                dve.memset(state, 0.0).then_inc(inc("rw_state"), 1)
                for c in range(NCH):
                    R, t = rows_of(c % 2), c // 2
                    by_par = lambda a: a.rearrange("p (q r d) -> p q r d", q=4, r=2)
                    dve.wait_ge(*count("rw_x1", c + 1))
                    for par in range(2):
                        last = TT(by_par(x_s[R])[:, :, par], bank(par)[R, 0:256].rearrange("p (q d) -> p q d", q=4),
                                  by_par(xv[R, t])[:, :, par], add)
                    last.then_inc(inc("rw_x"), 1)
                    dve.wait_ge(*count("rw_s", c + 1))
                    dve.wait_ge(*count("rw_state", c + 1))
                    step(TT(state, state, bank(3)[:, 0:256].rearrange("p (q i) -> p q i", q=4), add))
                    dve.wait_ge(*count("rw_y1", c + 1))
                    TT(state, state, along(pc.rearrange("p (q c) -> p q c", q=4)[:, :, c], CH, 2), mul).then_inc(inc("rw_state"), 1)
                    dve.wait_ge(*count("rw_y2_out", c + 1))
                    for par in range(2):
                        yy = by_par(y_sb[R, t])[:, :, par]
                        last = TT(yy, yy, bank(4 + par)[R, 0:256].rearrange("p (q d) -> p q d", q=4), add)
                    last.then_inc(inc("rw_y"), 1)
                dve.wait_ge(*count("rw_y", NCH))
                yh = flat(y_sb).rearrange("p (h d) -> p h d", d=HD)
                step(dve.tensor_reduce(ms, yh, AXX, add))
                step(dve.tensor_scalar(ms, ms, -1.0 / HD, None, mul))
                step(TT(yh, yh, along(ms, HD, 2), add))
                step(TT(ysq, y_sb, y_sb, mul))
                step(dve.tensor_reduce(ms, flat(ysq).rearrange("p (h d) -> p h d", d=HD), AXX, add))
                dve.tensor_scalar(ms, ms, 1.0 / HD, GN_EPS, mul, add).then_inc(inc("rw_gn_ms"), 1)
                for t in range(NT):
                    last = TT(heads(ysq)[:, t], heads(v_)[:, t], along(bonus[:, 8 * t:8 * t + 8], HD, 2), mul)
                dve.wait_ge(*count("rw_gn_sd", 1))
                step(dve.reciprocal(sd, sd))
                step(TT(yh, yh, along(sd, HD, 2), mul))
                step(TT(y_sb, y_sb, two(rv["gn_w"]), mul))
                step(TT(y_sb, y_sb, two(rv["gn_b"]), add))
                step(TT(y_sb, y_sb, ysq, add))
                dve.wait_ge(*count("rw_gate", 1))
                TT(y_sb, y_sb, gg, mul).then_inc(inc("rw_y_rows"), 1)
                for j in range(2):
                    dve.wait_ge(*count("rw_y_turned", j + 1))
                    dve.tensor_copy(yaT[:, 2 * j:2 * j + 2], bank(j).rearrange("p (q s) -> p q s", q=2)).then_inc(inc("rw_out"), 1)

            cols.release("rkv", *[n for n in list(cols.held) if n.startswith("rw_")])
            return Stage(tensor=tensor, vector=vector, scalar=scalar)

        yaT = cols.take("yaT", 1024).rearrange("p (c s) -> p c s", c=4)
        rwkv7 = rwkv()
        qkv2 = cols.take("qkv2", NT * 3 * HW, top=True).rearrange("p (t c) -> p t c", t=NT)
        jobs = [(U_MOBA + c, "tok", t, 512, KD, qkv2[:, t, 512 * c:512 * (c + 1)]) for c in range(3) for t in range(NT)]
        proj_qkv2 = project("pm", x1T, ("rw_out", 2), jobs)
        ybT = cols.take("ybT", 1024).rearrange("p (c s) -> p c s", c=4)
        attention2 = attention("mb", qkv2, proj_qkv2.done, ybT, const("causal").rearrange("p (t s) -> p t s", t=NT), False)
        cols.release("qkv2")

        gates = cols.take("gates", 3 * KD * SEQ).rearrange("p (c s) -> p c s", c=3 * KD)

        def open_gates(act, tile, src):
            act.activation(gates[:, tile], src[:, 0], ACT.Sigmoid, bias=vec["gate_b"][:, tile:tile + 1])
            return act.activation(gates[:, tile + 1], src[:, 1], ACT.Sigmoid, bias=vec["gate_b"][:, tile + 1:tile + 2])

        proj_gates = project("pt", x1T, ("mb_out", 4),
                             [(U_GATE + c, "T", s, 512, KD, 4 * c + 2 * s) for c in range(6) for s in range(2)],
                             lanes=1, v_copy=open_gates)
        mergedT = cols.take("mergedT", KD * SEQ).rearrange("p (k s) -> p k s", k=KD)

        def merge():
            branches = (yaT, ybT, ycT)

            def tensor(pe):
                for n in range(3):
                    unit_ready(pe, U_UP + n)
                pe.wait_ge(*count("pt_out0", 12))
                for d in range(KD):
                    if d >= 2:
                        pe.wait_ge(*count("mg_out", d - 1))
                    for n, y in enumerate(branches):
                        o = banks(2 * (d % 2), 2)[:, n * SEQ:(n + 1) * SEQ]
                        w = slot(U_UP + n, 4, DM)
                        for k in range(4):
                            mm = pe.matmul(o, w[:, k, d * P:(d + 1) * P], y[:, k], start=(k == 0), stop=(k == 3))
                    mm.then_inc(inc("mg_products"), 1)
                pe.wait_ge(*count("mg_products", KD))
                pe.sem_inc(inc("units_used"), 3)

            def vector(dve):
                step = vchain(dve)
                g3 = gates.rearrange("p (b d) s -> p b d s", b=3)
                dve.wait_ge(*count("pt_out0", 12))
                for d in range(KD):
                    dve.wait_ge(*count("mg_products", d + 1))
                    src = banks(2 * (d % 2), 2)[:, 0:3 * SEQ].rearrange("p (b s) -> p b s", b=3)
                    dve.tensor_tensor(g3[:, :, d], g3[:, :, d], src, ALU.mult).then_inc(inc("mg_out"), 1)
                    dve.wait_ge(*count("mg_out", d + 1))
                    step(dve.tensor_tensor(g3[:, 0, d], g3[:, 0, d], g3[:, 1, d], ALU.add))
                    dve.tensor_tensor(mergedT[:, d], g3[:, 0, d], g3[:, 2, d], ALU.add).then_inc(inc("mg_T"), 1)

            return Stage(tensor=tensor, vector=vector)

        merged = merge()
        cols.release("x1T", "yaT", "ybT", "ycT")
        jobs = [(U_OUT2 + c, "tok", t, 512, KD, x_sb[:, t, 512 * c:512 * (c + 1)]) for c in range(2) for t in range(NT)]
        out_proj2 = project("o2", mergedT, ("mg_T", KD), jobs, lanes=1,
                            v_copy=lambda dve, out, src: dve.scalar_tensor_tensor(out, out, DEEPNORM_ALPHA, src, ALU.mult, ALU.add))
        cols.release("gates", "mergedT")

        ln_rows = {n: cols.take(n, DM, top=True) for n in ("ln1_w", "ln1_b", "ln2_w", "ln2_b")}
        w_router2 = cols.take("w_router2", KD * 36, top=True).rearrange("p (k e) -> p k e", k=KD)

        def layer_norm(tag, ready, w, b):
            mean, ss, sd = tiny(NT), tiny(NT), tiny(NT)
            squares = cols.take(tag + "_squares", DM)

            def vector(dve):
                step = vchain(dve)
                dve.wait_ge(*count(*ready))
                step(dve.tensor_reduce(mean, x_sb, AXX, ALU.add))
                dve.tensor_scalar(mean, mean, -1.0 / DM, None, ALU.mult).then_inc(inc(tag + "_mean"), 1)
                dve.wait_ge(*count(tag + "_ss", NT))
                dve.tensor_scalar(ss, ss, 1.0 / DM, LN_EPS, ALU.mult, ALU.add).then_inc(inc(tag + "_var"), 1)
                dve.wait_ge(*count(tag + "_sd", 1))
                step(dve.reciprocal(sd, sd))
                for t in range(NT):
                    last = dve.tensor_scalar(x_sb[:, t], x_sb[:, t], mean[:, t:t + 1], sd[:, t:t + 1], ALU.add, ALU.mult)
                step(last)
                dve.wait_ge(*count("ln_rows_loaded", 80))
                step(dve.tensor_tensor(x_sb, x_sb, along(ln_rows[w], NT, 1), ALU.mult))
                dve.tensor_tensor(x_sb, x_sb, along(ln_rows[b], NT, 1), ALU.add).then_inc(inc(tag + "_out"), 1)

            def scalar(act):
                act.wait_ge(*count(tag + "_mean", 1))
                for t in range(NT):
                    act.activation(squares, x_sb[:, t], ACT.Square, bias=mean[:, t:t + 1], accum_out=ss[:, t:t + 1])\
                       .then_inc(inc(tag + "_ss"), 1)
                    act.wait_ge(*count(tag + "_ss", t + 1))
                act.wait_ge(*count(tag + "_var", 1))
                act.activation(sd, ss, ACT.Sqrt).then_inc(inc(tag + "_sd"), 1)

            cols.release(tag + "_squares")
            return Stage(vector=vector, scalar=scalar)

        def load_ln_rows(act):
            act.wait_ge(*count("mg_T", KD))
            for n, tile in ln_rows.items():
                act.dma_start(tile, row_source(n, n)).then_inc(inc("ln_rows_loaded"), 16)
            act.dma_start(w_router2, D["w_router_2"].rearrange("(k p) e -> p k e", p=P)).then_inc(inc("ln_rows_loaded"), 16)

        norm3 = layer_norm("l1", ("o2_out0", 4), "ln1_w", "ln1_b")
        x2T = cols.take("x2T", KD * SEQ).rearrange("p (k s) -> p k s", k=KD)
        turn4 = transpose_rows("x2", x_sb, x2T, ("l1_out", 1))

        weight2 = cols.take("weight2", NT * E2).rearrange("p (t e) -> p t e", t=NT)

        def route2():
            lg = cols.take("r2_logits", NT * 36).rearrange("p (t e) -> p t e", t=NT)
            em = cols.take("r2_em", NT * E2).rearrange("p (t e) -> p t e", t=NT)
            er = cols.take("r2_er", NT * E2).rearrange("p (t e) -> p t e", t=NT)
            padded = cols.take("r2_padded", NT * 16).rearrange("p (t e) -> p t e", t=NT)
            rest = cols.take("r2_rest", NT * 16).rearrange("p (t e) -> p t e", t=NT)
            find = cols.take("r2_find", NT * 8).rearrange("p (t e) -> p t e", t=NT)
            best = cols.take("r2_best", NT * 8).rearrange("p (t e) -> p t e", t=NT)
            eg = cols.take("r2_eg", NT * NG).rearrange("p (t e) -> p t e", t=NT)
            gmax, gsum, emax, esum = tiny(NT), tiny(NT), tiny(NT), tiny(NT)
            logits = bank(4, NT * 36).rearrange("p (t e) -> p t e", t=NT)
            LOWEST, TAKEN, OTHER = -3.0e38, -3.3e38, -1e30

            def tensor(pe):
                pe.wait_ge(*count("x2_T", KD // 2))
                pe.wait_ge(*count("ln_rows_loaded", 80))
                for t in range(NT):
                    for k in range(KD):
                        mm = pe.matmul(logits[:, t], x2T[:, k, t * P:(t + 1) * P], w_router2[:, k],
                                       start=(k == 0), stop=(k == KD - 1))
                mm.then_inc(inc("r2_logits"), 1)

            def scalar(act):
                act.wait_ge(*count("r2_gmax", 1))
                for t in range(NT):
                    ins = act.activation(eg[:, t], lg[:, t, 0:NG], ACT.Exp, bias=gmax[:, t:t + 1], accum_out=gsum[:, t:t + 1])
                ins.then_inc(inc("r2_group"), 1)
                act.wait_ge(*count("r2_emax", 1))
                for t in range(NT):
                    ins = act.activation(weight2[:, t], em[:, t], ACT.Exp, bias=emax[:, t:t + 1])
                ins.then_inc(inc("r2_exp"), 1)

            def vector(dve):
                step = vchain(dve)
                dve.memset(padded, LOWEST)
                dve.memset(find, LOWEST)
                dve.wait_ge(*count("r2_logits", 1))
                step(dve.tensor_tensor(lg, logits, along(row["router_b"], NT, 1), ALU.add))
                step(dve.tensor_copy(padded[:, :, 0:NG], lg[:, :, 0:NG]))
                step(dve.tensor_reduce(find[:, :, 0:1], lg[:, :, 0:NG], AXX, ALU.max))
                dve.tensor_reduce(gmax, lg[:, :, 0:NG], AXX, ALU.max, negate=True).then_inc(inc("r2_gmax"), 1)
                for t in range(NT):
                    last = dve.match_replace(rest[:, t], find[:, t], padded[:, t], TAKEN)
                step(last)
                g = rest[:, :, 0:NG]
                step(dve.tensor_tensor(g, g, padded[:, :, 0:NG], ALU.not_equal))
                step(dve.tensor_scalar(g, g, 1.0, -OTHER, ALU.subtract, ALU.mult))
                for t in range(NT):
                    last = dve.tensor_tensor(em[:, t].rearrange("p (g e) -> p g e", g=NG),
                                             lg[:, t, NG:36].rearrange("p (g e) -> p g e", g=NG),
                                             along(rest[:, t, 0:NG], EPG, 2), ALU.add)
                step(last)
                for t in range(NT):
                    last = dve.max(best[:, t], em[:, t])
                step(last)
                dve.tensor_scalar(emax, best[:, :, 0], -1.0, None, ALU.mult).then_inc(inc("r2_emax"), 1)
                step(dve.memset(find, OTHER))
                step(dve.tensor_copy(find[:, :, 0:2], best[:, :, 0:2]))
                for t in range(NT):
                    last = dve.match_replace(er[:, t], find[:, t], em[:, t], TAKEN)
                step(last)
                step(dve.tensor_tensor(er, er, em, ALU.not_equal))
                step(dve.scalar_tensor_tensor(er, em, OTHER / 2, er, ALU.is_gt, ALU.mult))
                dve.wait_ge(*count("r2_exp", 1))
                step(dve.tensor_tensor(weight2, weight2, er, ALU.mult))
                step(dve.tensor_reduce(esum, weight2, AXX, ALU.add))
                dve.wait_ge(*count("r2_group", 1))
                step(dve.tensor_tensor(esum, esum, gsum, ALU.mult))
                step(dve.reciprocal(esum, esum))
                step(dve.tensor_tensor(weight2, weight2, along(esum, E2, 2), ALU.mult))
                dve.wait_ge(*count("x2_T", KD // 2))
                dve.tensor_scalar(x_sb, x_sb, DEEPNORM_ALPHA, None, ALU.mult).then_inc(inc("r2_done"), 1)

            cols.release("r2_logits", "r2_em", "r2_er", "r2_padded", "r2_rest", "r2_find", "r2_best", "r2_eg")
            return Stage(tensor=tensor, vector=vector, scalar=scalar)

        routing2 = route2()

        def experts2():
            QUARTER = SLOTS * UNIT // 4
            buf = [arena[:, b * QUARTER:(b + 1) * QUARTER] for b in range(4)]
            w_gate = [a[:, 0:2048].rearrange("p (k n) -> p k n", k=KD) for a in buf]
            w_up = [a[:, 2048:4096].rearrange("p (k n) -> p k n", k=KD) for a in buf]
            w_down = [a[:, 4096:6144].rearrange("p (k n) -> p k n", k=2) for a in buf]
            hid = [cols.take(f"m2_hid{j}", 512) for j in range(2)]
            wcur = tiny(NT * 4).rearrange("p (t e) -> p t e", t=NT)
            ORDER = [("up", 0), ("up", 1), ("down", 0), ("up", 2), ("down", 1), ("up", 3), ("down", 2), ("down", 3)]

            def load(sp, b, e):
                for tile, name, k in ((w_gate, "expert_w_gate_2", KD), (w_up, "expert_w_up_2", KD), (w_down, "expert_w_down_2", 2)):
                    src = D[name][e] if isinstance(e, int) else D[name][bass.ds(e, 1)].rearrange("o d n -> (o d) n")
                    sp.dma_start(tile[b], src.rearrange("(k p) n -> p k n", k=k)).then_inc(inc(f"m2_loaded{b}"), 16)

            def sync(sp):
                for b in range(4):
                    slots = range(b * QUARTER // UNIT, -(-(b + 1) * QUARTER // UNIT))
                    last = max(u for u in range(U_END - SLOTS, U_END) if u % SLOTS in slots)
                    sp.wait_ge(*count("units_used", last + 1))
                    load(sp, b, b)
                with sp.Fori(1, E2 // 4) as g:
                    for b in range(4):
                        sp.wait_ge(*count("m2_down_done", g * 4 + (b - 3)))
                        load(sp, b, g * 4 + b)

            def tensor(pe):
                pe.wait_ge(*count("x2_T", KD // 2))
                pe.wait_ge(*count("r2_done", 1))
                with pe.Fori(0, E2 // 4) as g:
                    for kind, b in ORDER:
                        p = b % 2
                        if kind == "up":
                            pe.wait_ge(*count(f"m2_loaded{b}", g * 48 + 48))
                            for w, o, sem in ((w_gate[b], bank(2 * p), "m2_gate"), (w_up[b], bank(2 * p + 1), "m2_up")):
                                for f in range(2):
                                    for k in range(KD):
                                        mm = pe.matmul(o[:, f * SEQ:(f + 1) * SEQ], w[:, k, f * P:(f + 1) * P], x2T[:, k],
                                                       start=(k == 0), stop=(k == KD - 1))
                                mm.then_inc(inc(sem), 1)
                        else:
                            pe.wait_ge(*count("m2_hid", g * 4 + (b + 1)))
                            pe.wait_ge(*count("m2_added", g * 16 + (4 * b + 1)))
                            h = hid[p].rearrange("p (f s) -> p f s", f=2)
                            for t in range(NT):
                                for n in range(2):
                                    for f in range(2):
                                        mm = pe.matmul(bank(4 + 2 * t + n), h[:, f, t * P:(t + 1) * P],
                                                       w_down[b][:, f, 512 * n:512 * n + 512], start=(f == 0), stop=(f == 1))
                                    if t * 2 + n < 3:
                                        mm.then_inc(inc("m2_down"), 1)
                            mm.then_inc(inc("m2_down_done"), 1)

            def scalar(act):
                with act.Fori(0, E2 // 4) as g:
                    for b in range(4):
                        act.wait_ge(*count("m2_gate", g * 4 + (b + 1)))
                        act.activation(hid[b % 2], bank(2 * (b % 2)), ACT.Sigmoid).then_inc(inc("m2_sigmoid"), 1)

            def vector(dve):
                dve.sem_inc(inc("m2_added"), 1)
                with dve.Fori(0, E2 // 4) as g:
                    dve.wait_ge(*count("m2_added", g * 16 + 1))
                    dve.tensor_copy(wcur, weight2[:, :, bass.ds(g * 4, 4)]).then_inc(inc("m2_weights"), 1)
                    dve.wait_ge(*count("m2_weights", g + 1))
                    for kind, b in ORDER:
                        p = b % 2
                        if kind == "up":
                            dve.wait_ge(*count("m2_sigmoid", g * 4 + (b + 1)))
                            dve.tensor_tensor(hid[p], hid[p], bank(2 * p), ALU.mult).then_inc(inc("m2_silu"), 1)
                            dve.wait_ge(*count("m2_silu", g * 4 + (b + 1)))
                            dve.wait_ge(*count("m2_up", g * 4 + (b + 1)))
                            dve.tensor_tensor(hid[p], hid[p], bank(2 * p + 1), ALU.mult).then_inc(inc("m2_hid"), 1)
                        else:
                            for j in range(4):
                                if j < 3:
                                    dve.wait_ge(*count("m2_down", g * 12 + (3 * b + j + 1)))
                                else:
                                    dve.wait_ge(*count("m2_down_done", g * 4 + (b + 1)))
                                t, n = j // 2, j % 2
                                part = x_sb[:, t, 512 * n:512 * n + 512]
                                dve.scalar_tensor_tensor(part, bank(4 + j), wcur[:, t, b:b + 1], part, ALU.mult, ALU.add)\
                                    .then_inc(inc("m2_added"), 1)

            cols.release("x2T", "weight2", "m2_hid0", "m2_hid1")
            return Stage(tensor=tensor, vector=vector, scalar=scalar, sync=sync)

        moe2 = experts2()
        norm4 = layer_norm("l2", ("m2_added", 4 * E2 + 1), "ln2_w", "ln2_b")

        def store(sp):
            sp.wait_ge(*count("l2_out", 1))
            sp.dma_start(D["out"].rearrange("(t p) d -> p t d", p=P), x_sb).then_inc(inc("out_stored"), 16)
            sp.wait_ge(*count("out_stored", 16))

        block = ctx.enter_context(nc.Block())

        @block.sync
        def _(sp):
            load_inputs(sp)
            moe1.sync(sp)
            load_block2(sp)
            moe2.sync(sp)
            store(sp)

        @block.tensor
        def _(pe):
            turn1.tensor(pe)
            proj1.tensor(pe)
            attention1.tensor(pe)
            hgrn2.tensor(pe)
            out_proj1.tensor(pe)
            turn2.tensor(pe)
            routing.tensor(pe)
            moe1.tensor(pe)
            turn3.tensor(pe)
            proj_u.tensor(pe)
            ssm_scan.tensor(pe)
            glu_proj.tensor(pe)
            proj_rkv.tensor(pe)
            rwkv7.tensor(pe)
            proj_qkv2.tensor(pe)
            attention2.tensor(pe)
            proj_gates.tensor(pe)
            merged.tensor(pe)
            out_proj2.tensor(pe)
            turn4.tensor(pe)
            routing2.tensor(pe)
            moe2.tensor(pe)

        @block.vector
        def _(dve):
            norm1.vector(dve)
            turn1.vector(dve)
            ssm_par.vector(dve)
            proj1.vector(dve)
            attention1.vector(dve)
            hgrn2.vector(dve)
            out_proj1.vector(dve)
            norm2.vector(dve)
            turn2.vector(dve)
            routing.vector(dve)
            moe1.vector(dve)
            dve.wait_ge(*count("ssm_tables", 1))
            turn3.vector(dve)
            proj_u.vector(dve)
            ssm_scan.vector(dve)
            glu_proj.vector(dve)
            glu.vector(dve)
            rwkv7.vector(dve)
            proj_qkv2.vector(dve)
            attention2.vector(dve)
            merged.vector(dve)
            out_proj2.vector(dve)
            norm3.vector(dve)
            turn4.vector(dve)
            routing2.vector(dve)
            moe2.vector(dve)
            norm4.vector(dve)

        @block.scalar
        def _(act):
            norm1.scalar(act)
            ssm_par.scalar(act)
            proj1.scalar(act)
            attention1.scalar(act)
            hgrn2.scalar(act)
            norm2.scalar(act)
            routing.scalar(act)
            ssm_tab.scalar(act)
            moe1.scalar(act)
            act.wait_ge(*count("ssm_tables", 1))
            proj_u.scalar(act)
            ssm_scan.scalar(act)
            glu_proj.scalar(act)
            glu.scalar(act)
            rwkv7.scalar(act)
            proj_qkv2.scalar(act)
            attention2.scalar(act)
            proj_gates.vector(act)
            load_ln_rows(act)
            norm3.scalar(act)
            routing2.scalar(act)
            moe2.scalar(act)
            norm4.scalar(act)

        @block.gpsimd
        def _(pool):
            ssm_tab.gpsimd(pool)
            ssm_scan.gpsimd(pool)

        return cols


def kernel(**inputs):
    import concourse.bacc as bacc
    from concourse.bass_utils import run_bass_kernel_spmd

    def a(name):
        return np.asarray(inputs[name])

    def column(v, n):
        return np.reshape(v, (n, P)).T

    def twice(v):
        return np.reshape(v, (ST, P)).T

    consts, const_at = shape_constants()
    lb = [column(a(n)[r], 4) for n in ("hgrn_lb_fwd", "hgrn_lb_bwd") for r in (0, 1)]
    vectors = {
        "norm1_w": column(a("norm1_w")[0], 8), "norm2_w": column(a("norm2_w")[0], 8),
        "q_w": np.tile(a("attn_q_norm_w")[0], 2)[:, None], "k_w": np.tile(a("attn_k_norm_w")[0], 2)[:, None],
        "lb": np.concatenate(lb, 1), "mu_lora": column(a("rwkv_mu_2")[0, 1536:], 2),
        "a_re": twice(a("ssm_a_re_2")[0]), "a_im": twice(a("ssm_a_im_2")[0]),
        "log_dt": twice(np.repeat(a("ssm_log_dt_2")[0], HD)), "ssm_d": column(a("ssm_d_2")[0], 4),
        "glu_b": column(a("ssm_glu_b_2")[0], 8), "gate_b": column(a("gate_b_2")[0], 24),
    }
    rows = {
        "out_norm_w": a("hgrn_out_norm_w"), "router_b": np.concatenate([a("router_group_b_2"), a("router_expert_b_2")], 1),
        "mu": a("rwkv_mu_2")[:, :1536], "w0": a("rwkv_w0_2"), "a0": a("rwkv_a0_2"), "k_k": a("rwkv_k_k_2"),
        "k_a": a("rwkv_k_a_2"), "r_k": a("rwkv_r_k_2"), "gn_w": a("rwkv_ln_w_2"), "gn_b": a("rwkv_ln_b_2"),
        "ln1_w": a("ln1_w_2"), "ln1_b": a("ln1_b_2"), "ln2_w": a("ln2_w_2"), "ln2_b": a("ln2_b_2"),
    }

    def block_diagonal(v):
        out = np.zeros((2, HD, ST, 2, 16), np.float32)
        for parity in range(2):
            out[parity, :, :, parity, :] = np.transpose(v[parity::2], (1, 0, 2))
        return out.reshape(P, ST * 32)

    b_re, b_im = a("ssm_b_re_2")[0], a("ssm_b_im_2")[0]
    c_re, c_im = (np.transpose(a(n)[0], (0, 2, 1)) for n in ("ssm_c_re_2", "ssm_c_im_2"))
    arrays = {
        "x": a("x")[0], "consts": consts,
        "vectors": np.concatenate([vectors[n] for n, _ in COLUMN_VECTORS], 1),
        "rows": np.concatenate([np.reshape(rows[n], (1, -1)) for n, _ in ROW_VECTORS], 1),
        "ssm_bc": np.concatenate([block_diagonal(v) for v in (b_re, b_im, c_re, c_im)], 1),
        "lora_wa": np.concatenate([a("rwkv_w2_2")[0], a("rwkv_a2_2")[0]], 0), "lora_g": a("rwkv_g2_2")[0],
        "w_router": np.reshape(a("w_router")[0], (KD, P, E1)),
        "w_router_2": np.concatenate([a("router_group_w_2")[0], a("router_expert_w_2")[0]], 1),
    }
    for name in ("w_in", "w_out", "w_expert_gate", "w_expert_up", "w_expert_down", "w_in_2", "ssm_glu_w_2",
                 "w_up_rwkv_2", "w_up_moba_2", "w_up_ssm_2", "w_out_2", "expert_w_gate_2", "expert_w_up_2",
                 "expert_w_down_2"):
        arrays[name] = a(name)[0]
    arrays = {n: np.ascontiguousarray(v) for n, v in arrays.items()}
    nc = bacc.Bacc("TRN2", target_bir_lowering=False, num_devices=1)
    D = {n: nc.dram_tensor("in_" + n, v.shape, F32, kind="ExternalInput").ap() for n, v in arrays.items()}
    D["out"] = nc.dram_tensor("out", (SEQ, DM), F32, kind="ExternalOutput").ap()
    two_blocks(nc, D, const_at)
    r = run_bass_kernel_spmd(nc, [{"in_" + n: v for n, v in arrays.items()}], core_ids=[0])
    return r.results[0]["out"].reshape(1, SEQ, DM)
```

```python
from contextlib import ExitStack

import numpy as np

import concourse.bass as bass
from concourse import mybir

F32 = mybir.dt.float32
ALU = mybir.AluOpType
ACT = mybir.ActivationFunctionType
AXX = mybir.AxisListType.X

P = 128
SEQ = 256
NT = SEQ // P
DM = 1024
KD = DM // P
HEADS, HD = 8, 64
HW = HEADS * HD
GH = 4
E1, CAP, FF1 = 16, 32, 1024
E2, FF2 = 32, 256
NG, EPG = 4, 8
NSLOT = 2 * SEQ
ROOM = 64
CH = 64
NCH = SEQ // CH
ST = 16
SLOTS, UNIT = 6, 4096
RMS_EPS, LN_EPS, GN_EPS = 1e-6, 1e-5, 64e-5
DEEPNORM_ALPHA = 2 ** 0.25
LOW = 5


def shape_constants():
    parts, at = [], {}

    def put(name, a):
        a = np.asarray(a, np.float32).reshape(P, -1)
        at[name] = (sum(x.shape[1] for x in parts), a.shape[1])
        parts.append(a)

    i = np.arange(P)
    put("ident", np.eye(P))
    q = (np.arange(NT)[None, :, None] * P + i[:, None, None])
    k = np.arange(SEQ)[None, None, :]
    dist = np.abs(q - k)
    put("dist", dist)
    times = (dist <= 64).astype(int) + (dist % 4 == 0) + (dist % 16 == 0)
    put("dilated", np.where(times > 0, np.log(np.maximum(times, 1)), -1e30))
    put("causal", np.where(k <= q, 0.0, -1e30))
    s, t = (i % 32)[:, None], np.arange(32)[None, :]
    put("sibling", np.stack([((s >> l + 1) == (t >> l + 1)) & ((s >> l) != (t >> l)) for l in range(LOW)], 1))
    put("eye32", s == t)
    tri = (i[:, None] <= i[None, :]) & (i[:, None] // CH == i[None, :] // CH)
    put("cumsum", tri)
    put("chunk_sum", i[:, None] // CH == np.arange(2)[None, :])
    r, c = (i % CH)[:, None], np.arange(CH)[None, :]
    put("before_upto", np.concatenate([r < c, r <= c], 1))
    put("after", r > c)
    put("eye64", r == c)
    put("lower", np.stack([((r >> m + 1) == (c >> m + 1)) & ((r >> m) % 2 == 1) & ((c >> m) % 2 == 0)
                           for m in range(6)], 1))
    put("upper", np.stack([((r >> m + 1) == (c >> m + 1)) & ((c >> m) % 2 == 1) & ((r >> m) % 2 == 0)
                           for m in range(6)], 1))
    put("slots", np.broadcast_to(np.arange(1, CAP + 1), (P, CAP)))
    put("numbers", np.broadcast_to(np.arange(1, NSLOT + 1), (P, NSLOT)))
    return np.ascontiguousarray(np.concatenate(parts, 1)), at


COLUMN_VECTORS = [("norm1_w", 8), ("norm2_w", 8), ("q_w", 1), ("k_w", 1), ("lb", 16), ("mu_lora", 2),
                  ("a_re", ST), ("a_im", ST), ("log_dt", ST), ("ssm_d", 4), ("glu_b", 8), ("gate_b", 24)]
ROW_VECTORS = [("out_norm_w", 128), ("router_b", 36), ("mu", 1536), ("w0", HW), ("a0", HW), ("k_k", HW),
               ("k_a", HW), ("r_k", HW), ("gn_w", HW), ("gn_b", HW), ("ln1_w", DM), ("ln1_b", DM),
               ("ln2_w", DM), ("ln2_b", DM)]


SHARED = {
    "b2_turned": ("n1_turned", 4), "pu_product": ("p1_product", 6), "ssm_b_turned": ("p2_product", 10),
    "ssm_driven": ("da_turned", 4), "pr_product": ("da_scores", 8), "ssm_emitted": ("da_probs_turned", 8),
    "pm_product": ("da_weighed", 8), "pg_product": ("hg_level_used", 16), "rw_lora_out": ("hg_o", 2),
    "rw_cum": ("hg_turned", 2), "rw_turned": ("o1_product", 4), "rw_products": ("n2_turned", 4),
    "rw_W": ("r_logits", 1), "rw_DW": ("r_aff_turned", 1), "rw_WD": ("r_slots_turned", 1),
    "rw_xv": ("r_gathered", 8), "rw_x1": ("r_gated_turned", 1), "b2_T": ("n1_ms", 1),
    "pu_out0": ("n1_rows", 2), "ssm_bT": ("n1_T", 4), "ssm_rotated": ("p1_out0", 3),
    "ssm_scanned": ("da_ms", 1), "ssm_y": ("da_rows", 2), "ssm_gelu_inner": ("p2_out0", 5),
    "ssm_gelu": ("da_T", 4), "pg_out0": ("da_biased", 8), "glu_out": ("da_max", 8),
    "rw_lora": ("da_probs", 8), "rw_pre": ("da_out", 4), "rw_decay": ("hg_lb_less_max", 1),
    "rw_ms": ("hg_q_used", 1), "rw_bonus": ("hg_level", 16), "rw_cum_before": ("hg_score", 1),
    "rw_scaled": ("hg_ms", 1), "rw_T": ("hg_rows", 1), "rw_products_out": ("hg_out", 2),
    "rw_inv": ("o1_out0", 4), "rw_xv_out": ("n2_ms", 1), "rw_state": ("n2_rows", 2), "rw_x": ("n2_T", 4),
    "rw_y": ("r_max", 1), "rw_gn_ms": ("r_aff", 1), "rw_y_rows": ("r_slots", 1), "rw_out": ("r_chosen", 1),
    "mb_rows": ("r_gated", 1), "pt_out0": ("r_xin", 8), "pu_out1": ("n1_squares", 2),
    "pr_out0": ("n1_sd", 1), "ssm_gelu_sigmoid": ("p1_out1", 3), "pm_out0": ("da_sd", 1),
    "pg_out1": ("p2_out1", 5), "glu_sigmoid": ("da_exp", 8), "rw_lora_act": ("da_probsT", 8),
    "rw_gate": ("hg_lb_exp", 1), "rw_post": ("hg_sigmoids", 3), "rw_sd": ("hg_k_pairs", 10),
    "rw_exp": ("hg_score_copied", 4), "rw_W_out": ("hg_o_copied", 1), "rw_u_out": ("hg_gate", 1),
    "rw_y2_out": ("hg_sd", 1), "rw_gn_sd": ("n2_squares", 2), "pn_out0": ("n2_sd", 1),
    "pt_out1": ("r_exp", 1), "mb_exp": ("r_gated_T", 1), "x2_turned": ("b2_turned", 4),
    "r2_logits": ("pu_product", 2), "r2_er_turned": ("ssm_b_turned", 2), "r2_before": ("ssm_driven", 8),
    "r2_turned_back": ("pr_product", 7), "r2_gathered": ("ssm_emitted", 8), "m2_in": ("pm_product", 10),
    "m2_turned": ("pg_product", 4), "m2_down": ("rw_lora_out", 3), "m2_combined": ("rw_cum", 1),
    "l1_mean": ("b2_T", 4), "l1_var": ("pu_out0", 1), "l1_out": ("ssm_bT", 1), "x2_T": ("ssm_rotated", 8),
    "r2_gmax": ("ssm_scanned", 8), "r2_emax": ("ssm_y", 4), "r2_chosen": ("ssm_gelu_inner", 1),
    "r2_ranks": ("ssm_gelu", 1), "r2_begin": ("pg_out0", 2), "r2_numbers": ("glu_out", 1),
    "r2_picks": ("rw_lora", 1), "r2_done": ("rw_pre", 2), "m2_equal": ("rw_decay", 1),
    "m2_silu": ("rw_ms", 1), "m2_hid": ("rw_bonus", 1), "m2_y0": ("rw_cum_before", 1),
    "m2_added": ("rw_scaled", 1), "l2_mean": ("rw_T", 8), "l2_var": ("rw_products_out", 10),
    "l2_out": ("rw_inv", 6), "l1_ss": ("pu_out1", 1), "l1_sd": ("pr_out0", 7),
    "r2_group": ("ssm_gelu_sigmoid", 1), "r2_exp": ("pm_out0", 10), "r2_sorted": ("pg_out1", 2),
    "m2_tokens": ("glu_sigmoid", 1), "m2_sigmoid": ("rw_lora_act", 1), "m2_turned_out": ("rw_gate", 1),
    "m2_y1": ("rw_post", 2), "l2_ss": ("rw_sd", 1), "l2_sd": ("rw_exp", 4),
}


class Stage:

    def __init__(self, tensor=None, vector=None, scalar=None, gpsimd=None, sync=None, done=None, held=(),
                 mag=None, v=None, y=None, parts=None):
        self.parts = parts
        self.tensor, self.vector, self.scalar, self.gpsimd, self.sync = tensor, vector, scalar, gpsimd, sync
        self.done, self.held, self.mag, self.v, self.y = done, held, mag, v, y


def in_parts(tensor, vector, scalar, **other):
    def whole(program):
        def run(eng):
            for _ in program(eng):
                pass
        return run

    return Stage(tensor=whole(tensor), vector=whole(vector), scalar=whole(scalar),
                 parts=(tensor, vector, scalar), **other)


def take_turns(eng, order, a, b):
    programs = {"a": a(eng), "b": b(eng)}
    for which in order + "a" * 99 + "b" * 99:
        next(programs[which], None)


def one_after_other(*programs):
    def run(eng):
        for n, program in enumerate(programs):
            if n:
                yield
            yield from program(eng)

    return run


class Columns:

    def __init__(self, tensor, start, end):
        self.tensor, self.free_list, self.held, self.log = tensor, [(start, end)], {}, {}

    def take(self, name, n, top=False):
        order = list(enumerate(self.free_list))
        for j, (a, b) in reversed(order) if top else order:
            if b - a >= n:
                a = b - n if top else a
                self.free_list[j] = (self.free_list[j][0], a) if top else (a + n, b)
                self.held[name] = self.log[name] = (a, a + n)
                return self.tensor[:, a:a + n]
        raise MemoryError(f"{name} {n} {self.free_list} {self.held}")

    def release(self, *names):
        for name in names:
            self.free_list.append(self.held.pop(name))
        merged = []
        for a, b in sorted(self.free_list):
            if merged and merged[-1][1] == a:
                merged[-1] = (merged[-1][0], b)
            elif a < b:
                merged.append((a, b))
        self.free_list = merged


def along(ap, extra, where):
    dims = [list(x) for x in ap.ap]
    dims.insert(where, [0, extra])
    return bass.AP(tensor=ap.tensor, offset=ap.offset, ap=dims)


def two_blocks(nc, D, const_at):
    ctx = ExitStack()
    sems = {}

    def inc(name):
        while name in SHARED:
            name = SHARED[name][0]
        if name not in sems:
            sems[name] = ctx.enter_context(nc.semaphore(name))
        return sems[name]

    def count(name, n):
        base, first = 0, name
        while name in SHARED:
            base += SHARED[name][1]
            name = SHARED[name][0]
        return inc(first), n + base

    with ctx:
        TOTAL = 52800
        arena = ctx.enter_context(nc.sbuf_tensor("arena", [P, TOTAL], F32))
        psum = ctx.enter_context(nc.psum_tensor("psum", [P, 8, 512], F32))
        ring = [arena[:, s * UNIT:(s + 1) * UNIT] for s in range(SLOTS)]
        cols = Columns(arena, SLOTS * UNIT, TOTAL)

        n_const = const_at["numbers"][0]
        const_sb = cols.take("const", n_const)

        def const(name):
            a, n = const_at[name]
            return const_sb[:, a:a + n]

        n_vec = sum(n for _, n in COLUMN_VECTORS)
        vec_sb = cols.take("vec", n_vec)
        vec, a = {}, 0
        for name, n in COLUMN_VECTORS:
            vec[name] = vec_sb[:, a:a + n]
            a += n
        row_at, a = {}, 0
        for name, n in ROW_VECTORS:
            row_at[name] = (a, n)
            a += n

        def row_source(first, last):
            a, b = row_at[first][0], sum(row_at[last])
            return bass.AP(tensor=D["rows"].tensor, offset=a, ap=[[0, P], [1, b - a]])

        rows_a = cols.take("rows_a", 164)
        row = {"out_norm_w": rows_a[:, 0:128], "router_b": rows_a[:, 128:164]}
        w_router = cols.take("w_router", KD * E1)
        small = cols.take("small", 1200)
        small_used = [0]

        def tiny(n):
            small_used[0] += n
            assert small_used[0] <= 1200, small_used
            return small[:, small_used[0] - n:small_used[0]]

        ident = const("ident")
        begin = ctx.enter_context(nc.sbuf_tensor("begin", [1, E2 + 8], mybir.dt.int32))
        x_sb = cols.take("x", NT * DM).rearrange("p (t d) -> p t d", t=NT)

        def bank(b, n=512):
            return psum[:, b, 0:n]

        def banks(b, n):
            return psum[:, b:b + n, :].rearrange("p b n -> p (b n)")

        class Chain:

            def __init__(self, eng, name):
                self.eng, self.name, self.n = eng, name, 0

            def __call__(self, ins):
                self.n += 1
                ins.then_inc(inc(self.name), 1)
                self.eng.wait_ge(*count(self.name, self.n))


        def column_unit(w, c0, n):
            return (w[:, c0:c0 + n].rearrange("(k p) n -> p k n", p=P), w.shape[0] // P, n)

        first_units = [column_unit(D["w_in"], 512 * j, 512) for j in range(8)]
        first_units += [column_unit(D["w_out"], 512 * j, 512) for j in range(2)]
        UNITS_E1 = 6 * E1
        U_E1 = len(first_units)
        U_B2 = U_E1 + UNITS_E1
        B2_SLOTS = 3
        OFF_SSM, OFF_MOBA, OFF_GATE = 3328, 1792, 3840
        b2 = [column_unit(D["w_in_2"], OFF_SSM, 512)]
        b2 += [column_unit(D["w_in_2"], 512 * j, 512) for j in range(3)]
        b2 += [column_unit(D["w_in_2"], 1536, 256), column_unit(D["ssm_glu_w_2"], 0, 1024)]
        b2 += [column_unit(D["w_in_2"], OFF_MOBA + 512 * j, 512) for j in range(3)]
        b2 += [column_unit(D["w_in_2"], OFF_GATE + 512 * j, 512) for j in range(6)]
        b2 += [column_unit(D[w], 0, 1024) for w in ("w_up_rwkv_2", "w_up_moba_2", "w_up_ssm_2")]
        b2 += [column_unit(D["w_out_2"], 512 * j, 512) for j in range(2)]
        U_SSM, U_RWKV, U_LORA, U_GLU, U_MOBA, U_GATE, U_UP, U_OUT2 = (U_B2 + x for x in (0, 1, 4, 5, 6, 9, 15, 18))
        U_END = U_B2 + len(b2)

        def slot_number(u):
            return u % SLOTS if u < U_B2 else (u - U_B2) % B2_SLOTS

        def slot(u, k, n):
            return ring[slot_number(u)][:, 0:k * n].rearrange("p (k n) -> p k n", k=k)

        def unit_ready(eng, u):
            loads = sum(slot_number(v) == slot_number(u) for v in range(u + 1))
            eng.wait_ge(*count(f"slot_loaded{slot_number(u)}", 16 * loads))

        def load_unit(sp, u, unit):
            src, k, n = unit
            before = [v for v in range(u) if slot_number(v) == slot_number(u)]
            if before:
                sp.wait_ge(*count("units_used", before[-1] + 1))
            sp.dma_start(slot(u, k, n), src).then_inc(inc(f"slot_loaded{slot_number(u)}"), 16)

        def load_inputs(sp):
            sp.dma_start(x_sb, D["x"].rearrange("(t p) d -> p t d", p=P)).then_inc(inc("x_loaded"), 16)
            sp.dma_start(const_sb, D["consts"][:, 0:n_const]).then_inc(inc("const_loaded"), 16)
            sp.dma_start(vec_sb, D["vectors"]).then_inc(inc("const_loaded"), 16)
            sp.dma_start(rows_a, row_source("out_norm_w", "router_b")).then_inc(inc("const_loaded"), 16)
            sp.dma_start(w_router.rearrange("p (k e) -> p k e", k=KD), D["w_router"].rearrange("k p e -> p k e"))\
              .then_inc(inc("router_loaded"), 16)
            for u, unit in enumerate(first_units):
                load_unit(sp, u, unit)

        def rms_rows(tag, src, ready, out, scratch):
            ss, sd, rs = tiny(2), tiny(2), tiny(2)

            def scalar(act):
                act.wait_ge(*count(*ready))
                for t in range(NT):
                    act.activation(scratch, src[:, t], ACT.Square, accum_out=ss[:, t:t + 1])\
                       .then_inc(inc(tag + "_squares"), 1)
                    act.wait_ge(*count(tag + "_squares", t + 1))
                act.wait_ge(*count(tag + "_ms", 1))
                act.activation(sd, rs, ACT.Sqrt).then_inc(inc(tag + "_sd"), 1)

            def vector(dve):
                dve.wait_ge(*count(tag + "_squares", NT))
                dve.tensor_scalar(rs, ss, 1.0 / DM, RMS_EPS, ALU.mult, ALU.add).then_inc(inc(tag + "_ms"), 1)
                dve.wait_ge(*count(tag + "_sd", 1))
                dve.wait_ge(*count(*ready))
                vchain(dve)(dve.reciprocal(rs, sd))
                for t in range(NT):
                    dve.tensor_scalar(out[:, t], src[:, t], rs[:, t:t + 1], None, ALU.mult)\
                       .then_inc(inc(tag + "_rows"), 1)

            return Stage(scalar=scalar, vector=vector)

        def transpose_rows(tag, src, out, ready, weight=None):
            def tensor(pe):
                pe.wait_ge(*count("const_loaded", 48))
                pe.wait_ge(*count(*ready))
                for j in range(KD // 2):
                    for k in (2 * j, 2 * j + 1):
                        for t in range(NT):
                            mm = pe.transpose(bank(j)[:, (k % 2) * SEQ + t * P:(k % 2) * SEQ + (t + 1) * P],
                                              src[:, t, k * P:(k + 1) * P], ident)
                    mm.then_inc(inc(tag + "_turned"), 1)

            def vector(dve):
                dve.wait_ge(*count("const_loaded", 48))
                for j in range(KD // 2):
                    dve.wait_ge(*count(tag + "_turned", j + 1))
                    for k in (2 * j, 2 * j + 1):
                        src_ps = bank(j)[:, (k % 2) * SEQ:(k % 2 + 1) * SEQ]
                        if weight is None:
                            ins = dve.tensor_copy(out[:, k], src_ps)
                        else:
                            ins = dve.tensor_scalar(out[:, k], src_ps, weight[:, k:k + 1], None, ALU.mult)
                    ins.then_inc(inc(tag + "_T"), 1)

            return Stage(tensor=tensor, vector=vector)

        the_chain = {}

        def vchain(dve):
            if "v" not in the_chain:
                the_chain["v"] = Chain(dve, "vector_step")
            return the_chain["v"]

        def achain(act):
            if "a" not in the_chain:
                the_chain["a"] = Chain(act, "scalar_step")
            return the_chain["a"]

        def gchain(pool):
            if "g" not in the_chain:
                the_chain["g"] = Chain(pool, "gpsimd_step")
            return the_chain["g"]

        def project(tag, lhs, ready, jobs, lanes=2, v_copy=None, a_copy=None, after=(), places=(0, 1, 2, 3)):
            n_places = len(places)
            v_copy = v_copy or (lambda dve, out, src: dve.tensor_copy(out, src))
            a_copy = a_copy or (lambda act, out, src: act.activation(out, src, ACT.Copy))

            def tensor(pe):
                pe.wait_ge(*count(*ready))
                for sem, n in after:
                    pe.wait_ge(*count(sem, n))
                finished = 0
                for j, (u, kind, sub, n, kt, out) in enumerate(jobs):
                    w = slot(u, kt, n)
                    unit_ready(pe, u)
                    if j >= n_places:
                        pe.wait_ge(*count(f"{tag}_out{(j - n_places) % lanes}", (j - n_places) // lanes + 1))
                    b = bank(places[j % n_places])
                    blocks = [(b[:, 0:n], None)] if kind == "tok" else \
                        [(b[:, e * SEQ:(e + 1) * SEQ], (2 * sub + e) * P) for e in range(2)]
                    for o, c in blocks:
                        for k in range(kt):
                            if kind == "tok":
                                mm = pe.matmul(o, lhs[:, k, sub * P:(sub + 1) * P], w[:, k, :],
                                               start=(k == 0), stop=(k == kt - 1))
                            else:
                                mm = pe.matmul(o, w[:, k, c:c + P], lhs[:, k, :],
                                               start=(k == 0), stop=(k == kt - 1))
                            if finished:
                                mm.then_inc(inc("units_used"), 1)
                                finished = 0
                            if kind == "tok" and k == kt // 2 - 1 or kind == "T" and k == kt - 1 and c // P % 2 == 0:
                                yield
                    mm.then_inc(inc(tag + "_product"), 1)
                    finished = j + 1 == len(jobs) or jobs[j + 1][0] != u
                    if j + 1 < len(jobs):
                        yield
                pe.wait_ge(*count(tag + "_product", len(jobs)))
                pe.sem_inc(inc("units_used"), 1)

            def copies(eng, lane, copy):
                for j, (u, kind, sub, n, kt, out) in enumerate(jobs):
                    if j % lanes == lane:
                        eng.wait_ge(*count(tag + "_product", j + 1))
                        b = bank(places[j % n_places])
                        src = b[:, 0:n] if kind == "tok" else b.rearrange("p (e s) -> p e s", e=2)
                        copy(eng, out, src).then_inc(inc(f"{tag}_out{lane}"), 1)
                        yield

            return in_parts(tensor, lambda dve: copies(dve, 0, v_copy), lambda act: copies(act, 1, a_copy),
                         done=[(f"{tag}_out{n}", (len(jobs) + lanes - 1 - n) // lanes) for n in range(lanes)])

        hT = cols.take("hT", KD * SEQ).rearrange("p (k s) -> p k s", k=KD)
        xn = cols.take("xn", NT * DM).rearrange("p (t d) -> p t d", t=NT)
        scratch = cols.take("scratch", DM)
        norm1 = rms_rows("n1", x_sb, ("x_loaded", 16), xn, scratch)
        turn1 = transpose_rows("n1", xn, hT, ("n1_rows", NT), vec["norm1_w"])
        qkv = cols.take("qkv", NT * 3 * HW).rearrange("p (t c) -> p t c", t=NT)
        hgT = cols.take("hgT", 3 * GH * SEQ).rearrange("p (c s) -> p c s", s=SEQ)
        ig = cols.take("ig", NT * 2 * HW).rearrange("p (t c) -> p t c", t=NT)
        jobs = [(u, "tok", t, 512, KD, qkv[:, t, 512 * u:512 * u + 512]) for u in range(3) for t in range(NT)]
        proj1 = project("p1", hT, ("n1_T", KD // 2), jobs)
        jobs = [(u, "T", s, 512, KD, hgT[:, 4 * (u - 3) + 2 * s:4 * (u - 3) + 2 * s + 2]) for u in range(3, 6) for s in range(2)]
        jobs += [(u, "tok", t, 512, KD, ig[:, t, 512 * (u - 6):512 * (u - 5)]) for u in range(6, 8) for t in range(NT)]
        proj2 = project("p2", hT, ("n1_T", KD // 2), jobs, after=proj1.done)
        cols.release("xn", "scratch")
        mixT = cols.take("mixT", KD * SEQ).rearrange("p (k s) -> p k s", k=KD)

        def attention(tag, src, inputs_done, out, mask, norm):
            qkT = cols.take(tag + "qkT", 8 * SEQ).rearrange("p (c s) -> p c s", s=SEQ)
            sc = [cols.take(f"{tag}sc{j}", 512).rearrange("p (t s) -> p t s", t=NT) for j in range(2)]
            pT = [cols.take(f"{tag}pT{j}", 512).rearrange("p (t s) -> p t s", t=NT) for j in range(2)]
            den, rden, nmax = tiny(2 * HEADS), tiny(2 * HEADS), tiny(2 * HEADS)
            qk = src[:, :, 0:2 * HW]
            if norm:
                sq = cols.take(tag + "sq", NT * 2 * HW)
                ms, sd = tiny(32), tiny(32)

            def prepare(dve):
                step = vchain(dve)
                for sem, n in inputs_done:
                    dve.wait_ge(*count(sem, n))
                if norm:
                    sqv = sq.rearrange("p (t c) -> p t c", t=NT)
                    step(dve.tensor_tensor(sqv, qk, qk, ALU.mult))
                    step(dve.tensor_reduce(ms, sq.rearrange("p (h d) -> p h d", d=HD), AXX, ALU.add))
                    dve.tensor_scalar(ms, ms, 1.0 / HD, RMS_EPS, ALU.mult, ALU.add).then_inc(inc(tag + "_ms"), 1)
                    dve.wait_ge(*count(tag + "_sd", 1))
                    step(dve.reciprocal(sd, sd))
                    for t in range(NT):
                        v = qk[:, t].rearrange("p (h d) -> p h d", d=HD)
                        last = dve.tensor_tensor(v, v, along(sd[:, 16 * t:16 * t + 16], HD, 2), ALU.mult)
                        last.then_inc(inc(tag + "_rows"), 1)
                else:
                    dve.sem_inc(inc(tag + "_rows"), NT)
                yield
                for j in range(4):
                    dve.wait_ge(*count(tag + "_turned", j + 1))
                    o, i = qkT[:, 2 * j:2 * j + 2], bank(4 + j).rearrange("p (e s) -> p e s", e=2)
                    if norm:
                        w = vec["q_w"] if j < 2 else vec["k_w"]
                        ins = dve.tensor_scalar(o, i, w, HD ** -0.5 if j < 2 else 1.0, ALU.mult, ALU.mult)
                    else:
                        ins = dve.tensor_scalar(o, i, HD ** -0.5 if j < 2 else 1.0, None, ALU.mult)
                    ins.then_inc(inc(tag + "_T"), 1)
                yield

            def products(pe):
                pe.wait_ge(*count(tag + "_rows", NT))
                for sem, n in inputs_done:
                    pe.wait_ge(*count(sem, n))
                for j in range(4):
                    for c in (2 * j, 2 * j + 1):
                        for t in range(NT):
                            mm = pe.transpose(bank(4 + j)[:, (c % 2) * SEQ + t * P:(c % 2) * SEQ + (t + 1) * P],
                                              src[:, t, c * P:(c + 1) * P], ident)
                    mm.then_inc(inc(tag + "_turned"), 1)
                yield
                pe.wait_ge(*count(tag + "_T", 4))

                def scores(h):
                    if h >= 2:
                        pe.wait_ge(*count(tag + "_biased", h - 1))
                    r = slice(64 * (h % 2), 64 * (h % 2) + 64)
                    for t in range(NT):
                        mm = pe.matmul(bank(4 + h % 2)[:, t * SEQ:(t + 1) * SEQ],
                                       qkT[r, h // 2, t * P:(t + 1) * P], qkT[r, 4 + h // 2, :],
                                       start=True, stop=True)
                    mm.then_inc(inc(tag + "_scores"), 1)

                def turn(h):
                    pe.wait_ge(*count(tag + "_probs", h + 1))
                    if h >= 1:
                        pe.wait_ge(*count(tag + "_probsT", h))
                    for t in range(NT):
                        for k in range(NT):
                            mm = pe.transpose(bank(6)[:, k * SEQ + t * P:k * SEQ + (t + 1) * P],
                                              sc[h % 2][:, t, k * P:(k + 1) * P], ident)
                    mm.then_inc(inc(tag + "_probs_turned"), 1)

                def weigh(h):
                    pe.wait_ge(*count(tag + "_probsT", h + 1))
                    if h % 2 == 0 and h >= 4:
                        pe.wait_ge(*count(tag + "_out", h // 2 - 1))
                    o = bank(7)[64 * (h % 2):64 * (h % 2) + 64, (h // 2 % 2) * SEQ:(h // 2 % 2 + 1) * SEQ]
                    for k in range(NT):
                        mm = pe.matmul(o, src[:, k, 2 * HW + h * HD:2 * HW + (h + 1) * HD], pT[h % 2][:, k],
                                       start=(k == 0), stop=(k == NT - 1))
                    mm.then_inc(inc(tag + "_weighed"), 1)

                scores(0)
                scores(1)
                yield
                for h in range(HEADS):
                    turn(h)
                    yield
                    weigh(h)
                    if h + 2 < HEADS:
                        scores(h + 2)
                    yield

            def softmax(dve):
                step = vchain(dve)

                def bias(h):
                    dve.wait_ge(*count(tag + "_scores", h + 1))
                    if h >= 2:
                        dve.wait_ge(*count(tag + "_probs_turned", h - 1))
                    s = sc[h % 2]
                    slope = 2.0 ** -(h + 1)
                    dve.scalar_tensor_tensor(s, dist, -slope, bank(4 + h % 2).rearrange("p (t s) -> p t s", t=NT),
                                             ALU.mult, ALU.add).then_inc(inc(tag + "_biased"), 1)
                    dve.wait_ge(*count(tag + "_biased", h + 1))
                    step(dve.tensor_tensor(s, s, mask, ALU.add))
                    dve.tensor_reduce(nmax[:, 2 * h:2 * h + 2], s, AXX, ALU.max, negate=True)\
                       .then_inc(inc(tag + "_max"), 1)

                def divide(h):
                    dve.wait_ge(*count(tag + "_exp", h + 1))
                    step(dve.reciprocal(rden[:, 2 * h:2 * h + 2], den[:, 2 * h:2 * h + 2]))
                    dve.tensor_tensor(sc[h % 2], sc[h % 2], along(rden[:, 2 * h:2 * h + 2], SEQ, 2), ALU.mult)\
                       .then_inc(inc(tag + "_probs"), 1)

                bias(0)
                for h in range(HEADS):
                    divide(h)
                    if h + 1 < HEADS:
                        bias(h + 1)
                    if h % 2:
                        dve.wait_ge(*count(tag + "_weighed", h + 1))
                        dve.tensor_copy(out[:, h // 2], bank(7)[:, (h // 2 % 2) * SEQ:(h // 2 % 2 + 1) * SEQ])\
                           .then_inc(inc(tag + "_out"), 1)
                    yield

            def exps(act):
                if norm:
                    act.wait_ge(*count(tag + "_ms", 1))
                    act.activation(sd, ms, ACT.Sqrt).then_inc(inc(tag + "_sd"), 1)
                yield

                def turned(h):
                    act.wait_ge(*count(tag + "_probs_turned", h + 1))
                    if h >= 2:
                        act.wait_ge(*count(tag + "_weighed", h - 1))
                    act.activation(pT[h % 2].rearrange("p t s -> p (t s)"), bank(6), ACT.Copy)\
                       .then_inc(inc(tag + "_probsT"), 1)

                for h in range(HEADS):
                    if h >= 1:
                        turned(h - 1)
                    act.wait_ge(*count(tag + "_max", h + 1))
                    for t in range(NT):
                        ins = act.activation(sc[h % 2][:, t], sc[h % 2][:, t], ACT.Exp,
                                             bias=nmax[:, 2 * h + t:2 * h + t + 1],
                                             accum_out=den[:, 2 * h + t:2 * h + t + 1])
                    ins.then_inc(inc(tag + "_exp"), 1)
                    yield
                turned(HEADS - 1)

            cols.release(tag + "qkT", tag + "sc0", tag + "sc1", tag + "pT0", tag + "pT1")
            if norm:
                cols.release(tag + "sq")

            def vector(dve):
                yield from prepare(dve)
                yield from softmax(dve)

            return in_parts(products, vector, exps)

        dist = const("dist").rearrange("p (t s) -> p t s", t=NT)
        attention1 = attention("da", qkv, proj1.done, mixT[:, 0:4], const("dilated").rearrange("p (t s) -> p t s", t=NT), True)

        def hgrn():
            cols.release("qkv", "hT")
            names = []

            def take(name, n):
                names.append("hg_" + name)
                return cols.take("hg_" + name, n)

            q2 = take("q2", 2048).rearrange("p (d s) -> p d s", d=2)
            k2 = take("k2", 2048).rearrange("p (d s) -> p d s", d=2)
            totals = [take(f"total{l}", 2048 >> l).rearrange("p (d s) -> p d s", d=2) for l in range(8)]
            qs = take("qs", 1024)
            kd = take("kd", 1024)
            low = take("low", LOW * 256)
            near = take("near", 256)
            o_sb = take("o", 1024).rearrange("p (t c) -> p t c", t=NT)
            sig = take("sig", 1024)
            score = hgT[:, 4:12].rearrange("p c s -> p (c s)").rearrange("p (h s t) -> p h s t", h=GH, s=NT)
            far, sig_q, e_lb, lb_sum = tiny(8), None, tiny(16), tiny(8)
            lb, rest = tiny(8), tiny(8)
            ms, sd = tiny(8), tiny(8)
            q_raw, f_raw = hgT[:, 0:4].rearrange("p c s -> p (c s)"), hgT[:, 4:12].rearrange("p c s -> p (c s)")
            k_pairs = hgT[:, 4:8].rearrange("p c s -> p (c s)")
            lbv = vec["lb"].rearrange("p (d r k) -> p d r k", d=2, r=2)
            e_view = e_lb.rearrange("p (d r k) -> p d r k", d=2, r=2)
            score_ps = banks(4, 4).rearrange("p (h s t) -> p h s t", h=GH, s=NT)
            eye, siblings = const("eye32"), const("sibling").rearrange("p (l t) -> p l t", l=LOW)
            g_in = ig[:, :, HW:2 * HW]

            def halves(l):
                return [(half, 2 * l + half + 1) for half in range(2)]

            def pair(ap2, n, t0, size):
                dims = [list(ap2.ap[0])]
                if size // (2 * n) > 1:
                    dims.append([2 * n, size // (2 * n)])
                dims.append([n + 1024, 2])
                if n > 1:
                    dims.append([1, n])
                return bass.AP(tensor=ap2.tensor, offset=ap2.offset + t0, ap=dims)

            def scalar(act):
                for sem, n in proj2.done:
                    act.wait_ge(*count(sem, n))
                act.wait_ge(*count("hg_lb_less_max", 1))
                act.activation(e_lb, e_lb, ACT.Exp).then_inc(inc("hg_lb_exp"), 1)
                act.activation(sig, q_raw, ACT.Sigmoid).then_inc(inc("hg_sigmoids"), 1)
                act.activation(totals[0].rearrange("p d s -> p (d s)"), f_raw, ACT.Sigmoid).then_inc(inc("hg_sigmoids"), 1)
                act.activation(k2.rearrange("p d s -> p (d s)"), f_raw, ACT.Sigmoid, scale=-1.0).then_inc(inc("hg_sigmoids"), 1)
                for l in range(LOW):
                    for half, n in halves(l):
                        act.wait_ge(*count("hg_level", n))
                        act.activation(k_pairs[:, 512 * half:512 * half + 512], pair(k2, 1 << l, 512 * half, 512), ACT.Copy)\
                           .then_inc(inc("hg_k_pairs"), 1)
                act.wait_ge(*count("hg_level_used", 16))
                for h in range(GH):
                    act.activation(score[:, h], score_ps[:, h], ACT.Copy).then_inc(inc("hg_score_copied"), 1)
                act.wait_ge(*count("hg_o", NT))
                act.activation(o_sb, banks(0, 2).rearrange("p (t c) -> p t c", t=NT), ACT.Copy).then_inc(inc("hg_o_copied"), 1)
                act.wait_ge(*count("hg_q_used", 1))
                act.activation(sig.rearrange("p (t c) -> p t c", t=NT), g_in, ACT.Sigmoid).then_inc(inc("hg_gate"), 1)
                act.wait_ge(*count("hg_ms", 1))
                act.activation(sd, ms, ACT.Sqrt).then_inc(inc("hg_sd"), 1)

            def vector(dve):
                step = vchain(dve)
                fv = far.rearrange("p (d k) -> p d k", d=2)
                step(dve.tensor_tensor(fv, lbv[:, :, 0], lbv[:, :, 1], ALU.max))
                dve.tensor_tensor(e_view[:, :, 0], lbv[:, :, 0], fv, ALU.subtract)
                dve.tensor_tensor(e_view[:, :, 1], lbv[:, :, 1], fv, ALU.subtract).then_inc(inc("hg_lb_less_max"), 1)
                dve.wait_ge(*count("hg_lb_exp", 1))
                sv = lb_sum.rearrange("p (d k) -> p d k", d=2)
                step(dve.tensor_tensor(sv, e_view[:, :, 0], e_view[:, :, 1], ALU.add))
                step(dve.reciprocal(lb_sum, lb_sum))
                dve.tensor_tensor(lb.rearrange("p (d k) -> p d k", d=2), e_view[:, :, 0], sv, ALU.mult)
                step(dve.tensor_tensor(rest.rearrange("p (d k) -> p d k", d=2), e_view[:, :, 1], sv, ALU.mult))
                dve.wait_ge(*count("hg_sigmoids", 3))
                for sem, n in proj2.done:
                    dve.wait_ge(*count(sem, n))
                for j in range(8):
                    g = totals[0][:, j // 4, (j % 4) * SEQ:(j % 4 + 1) * SEQ]
                    k = k2[:, j // 4, (j % 4) * SEQ:(j % 4 + 1) * SEQ]
                    dve.tensor_scalar(g, g, rest[:, j:j + 1], lb[:, j:j + 1], ALU.mult, ALU.add)
                    last = dve.tensor_scalar(k, k, rest[:, j:j + 1], None, ALU.mult)
                step(last)
                step(dve.tensor_tensor(qs, q_raw, sig, ALU.mult))
                dve.tensor_tensor(kd, k2[:, 0], k2[:, 1], ALU.add).then_inc(inc("hg_q_used"), 1)
                for half in range(2):
                    r = slice(512 * half, 512 * half + 512)
                    dve.tensor_tensor(q2[:, 0, r], qs[:, r], totals[0][:, 1, r], ALU.mult)
                    dve.tensor_tensor(q2[:, 1, r], qs[:, r], totals[0][:, 0, r], ALU.mult).then_inc(inc("hg_level"), 1)
                for l in range(7):
                    n = 1 << l
                    for half, number in halves(l):
                        dve.wait_ge(*count("hg_level", number))
                        part = slice(half * (512 >> l), (half + 1) * (512 >> l))
                        twice = slice(half * (256 >> l), (half + 1) * (256 >> l))
                        t_f, t_b = (totals[l][:, d, part].rearrange("p (j u) -> p j u", u=2) for d in range(2))
                        dve.tensor_tensor(totals[l + 1][:, 0, twice], t_f[:, :, 0], t_f[:, :, 1], ALU.mult)
                        dve.tensor_tensor(totals[l + 1][:, 1, twice], t_b[:, :, 0], t_b[:, :, 1], ALU.mult)
                        dve.wait_ge(*count("hg_level_used", number))
                        for arr, lower, upper in ((q2, t_b[:, :, 1], t_f[:, :, 0]), (k2, t_f[:, :, 1], t_b[:, :, 0])):
                            for u, other in ((0, lower), (1, upper)):
                                v = arr[:, u, 512 * half:512 * half + 512].rearrange("p (j u i) -> p j u i", u=2, i=n)[:, :, u]
                                last = dve.tensor_tensor(v, v, along(other, n, 2), ALU.mult)
                        last.then_inc(inc("hg_level"), 1)
                lowv = low.rearrange("p (l e t) -> p l e t", l=LOW, e=8)
                step(dve.tensor_tensor(lowv, banks(0, 3)[:, 0:LOW * 256].rearrange("p (l e t) -> p l e t", l=LOW, e=8),
                                       along(siblings, 8, 2), ALU.mult))
                step(dve.tensor_reduce(near, low.rearrange("p (l e) -> p e l", l=LOW), AXX, ALU.add))
                dve.wait_ge(*count("hg_score_copied", GH))
                nearv = near.rearrange("p (h s t) -> p h s t", h=GH, s=NT)
                spots = [(slice(32 * b, 32 * b + 32), s, s * P + 32 * b) for b in range(4) for s in range(NT)]
                for r, s, c in spots:
                    last = dve.tensor_tensor(score[r, :, s, c:c + 32], score[r, :, s, c:c + 32], along(eye[r], GH, 1), ALU.mult)
                step(last)
                for r, s, c in spots:
                    last = dve.tensor_tensor(score[r, :, s, c:c + 32], score[r, :, s, c:c + 32], nearv[r, :, s], ALU.add)
                last.then_inc(inc("hg_score"), 1)
                dve.wait_ge(*count("hg_o_copied", 1))
                o_heads = o_sb.rearrange("p t (h v) -> p (t h) v", v=P)
                sq = score.rearrange("p h s t -> p (h s t)")[:, 0:1024]
                step(dve.tensor_tensor(sq.rearrange("p (t c) -> p t c", t=NT), o_sb, o_sb, ALU.mult))
                step(dve.tensor_reduce(ms, sq.rearrange("p (h v) -> p h v", v=P), AXX, ALU.add))
                dve.tensor_scalar(ms, ms, 1.0 / P, RMS_EPS, ALU.mult, ALU.add).then_inc(inc("hg_ms"), 1)
                dve.wait_ge(*count("hg_sd", 1))
                step(dve.reciprocal(sd, sd))
                step(dve.tensor_tensor(o_heads, o_heads, along(sd, P, 2), ALU.mult))
                step(dve.tensor_tensor(o_heads, o_heads, along(row["out_norm_w"], 8, 1), ALU.mult))
                step(dve.tensor_tensor(o_sb, o_sb, g_in, ALU.mult))
                dve.wait_ge(*count("hg_gate", 1))
                dve.tensor_tensor(o_sb, o_sb, sig.rearrange("p (t c) -> p t c", t=NT), ALU.mult).then_inc(inc("hg_rows"), 1)
                for j in range(2):
                    dve.wait_ge(*count("hg_turned", j + 1))
                    dve.tensor_copy(mixT[:, 4 + 2 * j:6 + 2 * j], bank(2 + j).rearrange("p (e s) -> p e s", e=2))\
                       .then_inc(inc("hg_out"), 1)

            def tensor(pe):
                pe.wait_ge(*count("da_out", 4))
                for l in range(8):
                    n = 1 << l
                    for half, number in halves(l):
                        pe.wait_ge(*count("hg_level", number))
                        if l < LOW:
                            pe.wait_ge(*count("hg_k_pairs", number))
                        for h in (2 * half, 2 * half + 1):
                            if l < LOW:
                                for s in range(NT):
                                    for b in range(4):
                                        t0 = h * SEQ + s * P + 32 * b
                                        r = slice(32 * b, 32 * b + 32)
                                        c = l * 256 + h * 64 + s * 32
                                        mm = pe.matmul(banks(0, 3)[r, c:c + 32], k_pairs[:, t0:t0 + 32], pair(q2, n, t0, 32),
                                                       start=True, stop=True)
                                        if l == 0:
                                            mm = pe.matmul(score_ps[r, h, s, s * P + 32 * b:s * P + 32 * b + 32],
                                                           kd[:, t0:t0 + 32], qs[:, t0:t0 + 32], start=True, stop=True)
                            else:
                                for j in range(SEQ // (2 * n)):
                                    a, z = 2 * j * n, (2 * j + 1) * n
                                    for s0, t0, copy in ((a, z, 0), (z, a, 1)):
                                        mm = pe.matmul(score_ps[s0 % P:s0 % P + n, h, s0 // P, t0:t0 + n],
                                                       k2[:, copy, h * SEQ + s0:h * SEQ + s0 + n],
                                                       q2[:, 1 - copy, h * SEQ + t0:h * SEQ + t0 + n], start=True, stop=True)
                        mm.then_inc(inc("hg_level_used"), 1)
                pe.wait_ge(*count("hg_score", 1))
                for t in range(NT):
                    for h in range(GH):
                        for s in range(NT):
                            mm = pe.matmul(bank(t)[:, h * P:(h + 1) * P], score[:, h, s, t * P:(t + 1) * P],
                                           ig[:, s, h * P:(h + 1) * P], start=(s == 0), stop=(s == NT - 1))
                    mm.then_inc(inc("hg_o"), 1)
                pe.wait_ge(*count("hg_rows", 1))
                for j in range(2):
                    for c in (2 * j, 2 * j + 1):
                        for t in range(NT):
                            mm = pe.transpose(bank(2 + j)[:, (c % 2) * SEQ + t * P:(c % 2) * SEQ + (t + 1) * P],
                                              o_sb[:, t, c * P:(c + 1) * P], ident)
                    mm.then_inc(inc("hg_turned"), 1)

            cols.release("hgT", "ig", *names)
            return Stage(tensor=tensor, vector=vector, scalar=scalar)

        hgrn2 = hgrn()

        jobs = [(8 + c, "tok", t, 512, KD, x_sb[:, t, 512 * c:512 * (c + 1)]) for c in range(2) for t in range(NT)]
        out_proj1 = project("o1", mixT, ("hg_out", 2), jobs, lanes=1,
                            v_copy=lambda dve, out, src: dve.tensor_tensor(out, out, src, ALU.add))
        cols.release("mixT")
        h2 = cols.take("h2", NT * DM, top=True).rearrange("p (t d) -> p t d", t=NT)
        scratch2 = cols.take("scratch2", DM, top=True)
        norm2 = rms_rows("n2", x_sb, ("o1_out0", 4), h2, scratch2)
        h2T = cols.take("h2T", KD * SEQ, top=True).rearrange("p (k s) -> p k s", k=KD)
        turn2 = transpose_rows("n2", h2, h2T, ("n2_rows", NT), vec["norm2_w"])
        chosen = cols.take("chosen", NT * E1 * CAP, top=True)
        gated = cols.take("gated", NT * E1 * CAP, top=True)
        gated_T = cols.take("gated_T", 4 * SEQ).rearrange("p (g s) -> p g s", g=4)
        xin = cols.take("xin", (E1 + 1) * KD * CAP).rearrange("p (e k c) -> p e k c", e=E1 + 1, k=KD)

        def route():
            aff = tiny(NT * E1).rearrange("p (t e) -> p t e", t=NT)
            nmax, total = tiny(NT), tiny(NT)
            work, best, picked = cols.take("r_work", SEQ), tiny(8), cols.take("r_picked", SEQ)
            place, ones_row = cols.take("r_count", SEQ), cols.take("r_ones", SEQ)
            slot_of = tiny(NT * E1)
            logits = bank(4, NT * E1).rearrange("p (t e) -> p t e", t=NT)
            c3 = chosen.rearrange("p (a c) -> p a c", c=CAP)
            g3 = gated.rearrange("p (a c) -> p a c", c=CAP)
            by_tile = chosen.rearrange("p (t c) -> p t c", t=NT)
            gated_by_tile = gated.rearrange("p (t c) -> p t c", t=NT)

            def tensor(pe):
                pe.wait_ge(*count("router_loaded", 16))
                pe.wait_ge(*count("n2_T", KD // 2))
                wr = w_router.rearrange("p (k e) -> p k e", k=KD)
                for t in range(NT):
                    for k in range(KD):
                        mm = pe.matmul(logits[:, t], h2T[:, k, t * P:(t + 1) * P], wr[:, k],
                                       start=(k == 0), stop=(k == KD - 1))
                mm.then_inc(inc("r_logits"), 1)
                pe.wait_ge(*count("r_aff", 1))
                for t in range(NT):
                    mm = pe.transpose(bank(5)[0:E1, t * P:(t + 1) * P], aff[:, t], ident)
                mm.then_inc(inc("r_aff_turned"), 1)
                pe.wait_ge(*count("r_slots", 1))
                for t in range(NT):
                    mm = pe.transpose(bank(6)[:, t * E1:(t + 1) * E1], place[0:E1, t * P:(t + 1) * P], ident[0:E1, 0:E1])
                mm.then_inc(inc("r_slots_turned"), 1)
                pe.wait_ge(*count("r_chosen", 1))
                for k in range(KD):
                    if k >= 2:
                        pe.wait_ge(*count("r_xin", k - 1))
                    for t in range(NT):
                        mm = pe.matmul(bank(2 + k % 2), h2[:, t, k * P:(k + 1) * P], by_tile[:, t],
                                       start=(t == 0), stop=(t == NT - 1))
                    mm.then_inc(inc("r_gathered"), 1)
                pe.wait_ge(*count("r_gated", 1))
                for g in range(4):
                    for t in range(NT):
                        mm = pe.transpose(bank(g // 2)[:, (g % 2) * SEQ + t * P:(g % 2) * SEQ + (t + 1) * P],
                                          gated_by_tile[:, t, g * P:(g + 1) * P], ident)
                mm.then_inc(inc("r_gated_turned"), 1)

            def scalar(act):
                act.wait_ge(*count("r_max", 1))
                for t in range(NT):
                    ins = act.activation(aff[:, t], logits[:, t], ACT.Exp, bias=nmax[:, t:t + 1],
                                         accum_out=total[:, t:t + 1])
                ins.then_inc(inc("r_exp"), 1)
                act.wait_ge(*count("r_gated_turned", 1))
                act.activation(gated_T.rearrange("p g s -> p (g s)"), banks(0, 2), ACT.Copy).then_inc(inc("r_gated_T"), 1)

            def vector(dve):
                step = vchain(dve)
                dve.memset(xin[:, E1], 0.0)
                dve.memset(ones_row, 1.0)
                dve.wait_ge(*count("r_logits", 1))
                dve.tensor_reduce(nmax, logits, AXX, ALU.max, negate=True).then_inc(inc("r_max"), 1)
                dve.wait_ge(*count("r_exp", 1))
                step(dve.reciprocal(total, total))
                dve.tensor_tensor(aff, aff, along(total, E1, 2), ALU.mult).then_inc(inc("r_aff"), 1)
                dve.wait_ge(*count("r_aff_turned", 1))
                w = work[0:E1]
                step(dve.tensor_copy(w, bank(5)[0:E1, 0:SEQ]))
                for _ in range(CAP // 8):
                    step(dve.max(best[0:E1], w))
                    step(dve.match_replace(w, best[0:E1], w, -1.0))
                step(dve.tensor_scalar(picked[0:E1], w, -0.5, None, ALU.is_lt))
                step(dve.tensor_tensor_scan(place[0:E1], ones_row[0:E1], picked[0:E1], 0.0, ALU.mult, ALU.add))
                dve.tensor_tensor(place[0:E1], place[0:E1], picked[0:E1], ALU.mult).then_inc(inc("r_slots"), 1)
                dve.wait_ge(*count("r_slots_turned", 1))
                step(dve.tensor_copy(slot_of, bank(6)[:, 0:NT * E1]))
                dve.tensor_tensor(c3, along(slot_of, CAP, 2), along(const("slots"), NT * E1, 1), ALU.is_equal)\
                   .then_inc(inc("r_chosen"), 1)
                dve.wait_ge(*count("r_chosen", 1))
                dve.tensor_tensor(g3, c3, along(aff.rearrange("p t e -> p (t e)"), CAP, 2), ALU.mult)\
                   .then_inc(inc("r_gated"), 1)
                for k in range(KD):
                    dve.wait_ge(*count("r_gathered", k + 1))
                    dve.tensor_scalar(xin[:, 0:E1, k], bank(2 + k % 2).rearrange("p (e c) -> p e c", c=CAP),
                                      vec["norm2_w"][:, k:k + 1], None, ALU.mult).then_inc(inc("r_xin"), 1)

            cols.release("r_work", "r_picked", "r_count", "r_ones")
            return Stage(tensor=tensor, vector=vector, scalar=scalar)

        routing = route()

        def experts1():
            xcur = cols.take("e1_x", KD * CAP).rearrange("p (k c) -> p k c", k=KD)
            gcur = cols.take("e1_g", SEQ)
            hid = cols.take("e1_hid", 512)
            hid_T = cols.take("e1_hid_T", 256)
            y_sb = cols.take("e1_y", DM)
            hid_T4 = hid_T.rearrange("p (c n m) -> p c n m", c=4, n=2)
            gate_ps, up_ps, turned_ps, y_ps = bank(0)[0:64], bank(1)[0:64], bank(2), banks(3, 2)
            weights = [("w_expert_gate", 0), ("w_expert_gate", 1), ("w_expert_up", 0), ("w_expert_up", 1),
                       ("w_expert_down", 0), ("w_expert_down", 1)]

            def ready(eng, e4, j, g):
                u = U_E1 + 6 * e4 + j
                eng.wait_ge(*count(f"slot_loaded{u % SLOTS}", g * 64 + 16 * (u // SLOTS + 1)))

            def w_slot(e4, j):
                return slot(U_E1 + 6 * e4 + j, KD, 512)

            def sync(sp):
                with sp.Fori(0, E1 // 4) as g:
                    for e4 in range(4):
                        for j, (name, half) in enumerate(weights):
                            u = U_E1 + 6 * e4 + j
                            sp.wait_ge(*count("units_used", g * 24 + (u - SLOTS + 1)))
                            src = D[name][bass.ds(g * 4 + e4, 1), :, 512 * half:512 * half + 512]
                            sp.dma_start(w_slot(e4, j), src.rearrange("o (k p) n -> p (o k) n", p=P))\
                              .then_inc(inc(f"slot_loaded{u % SLOTS}"), 16)

            def tensor(pe):
                pe.wait_ge(*count("r_xin", KD))
                pe.wait_ge(*count("r_gated_T", 1))
                pe.sem_inc(inc("e1_combined"), 1)
                with pe.Fori(0, E1 // 4) as g:
                    for e4 in range(4):
                        pe.wait_ge(*count("e1_x", g * 4 + (e4 + 1)))
                        for which, (ps, sem) in enumerate(((gate_ps, "e1_gate"), (up_ps, "e1_up"))):
                            for n in range(2):
                                ready(pe, e4, 2 * which + n, g)
                            for k in range(KD):
                                for n in range(2):
                                    mm = pe.matmul(ps[32 * n:32 * n + 32], xcur[:, k], w_slot(e4, 2 * which + n)[:, k],
                                                   start=(k == 0), stop=(k == KD - 1))
                                    if k == 0 and n == 0 and (which or e4):
                                        mm.then_inc(inc("units_used"), 1)
                                    if k == KD - 1 and n == 0:
                                        mm.then_inc(inc("units_used"), 1)
                            mm.then_inc(inc(sem), 1)
                        pe.wait_ge(*count("e1_hid", g * 4 + (e4 + 1)))
                        for c in range(4):
                            mm = pe.matmul(turned_ps[:, 64 * c:64 * c + 64], hid[0:64, P * c:P * c + P], ident[0:64, 0:64],
                                           start=True, stop=True)
                            if c == 0:
                                mm.then_inc(inc("units_used"), 1)
                        mm.then_inc(inc("e1_turned"), 1)
                        pe.wait_ge(*count("e1_hid_T", g * 4 + (e4 + 1)))
                        for n in range(2):
                            ready(pe, e4, 4 + n, g)
                            for k in range(KD):
                                mm = pe.matmul(y_ps[32 * e4:32 * e4 + 32, 512 * n:512 * n + 512],
                                               hid_T4[:, k % 4, k // 4], w_slot(e4, 4 + n)[:, k],
                                               start=(k == 0), stop=(k == KD - 1))
                            mm.then_inc(inc("units_used" if n == 0 else "e1_down"), 1)
                    pe.wait_ge(*count("e1_y", g + 1))
                    pe.wait_ge(*count("e1_gated", g + 1))
                    for j in range(4):
                        if j < 2:
                            pe.wait_ge(*count("e1_added", g * 4 + 1))
                        else:
                            pe.wait_ge(*count("e1_added", g * 4 + j))
                        if j == 0:
                            pe.sem_inc(inc("units_used"), 1)
                        pe.matmul(bank(5 + j % 2), gcur[:, (j // 2) * P:(j // 2 + 1) * P],
                                  y_sb[:, 512 * (j % 2):512 * (j % 2) + 512], start=True, stop=True)\
                          .then_inc(inc("e1_combined"), 1)

            def scalar(act):
                with act.Fori(0, E1 // 4) as g:
                    for e4 in range(4):
                        act.wait_ge(*count("e1_gate", g * 4 + (e4 + 1)))
                        act.activation(hid[0:64], gate_ps, ACT.Sigmoid).then_inc(inc("e1_sigmoid"), 1)
                        act.wait_ge(*count("e1_turned", g * 4 + (e4 + 1)))
                        act.activation(hid_T, turned_ps[:, 0:256], ACT.Copy).then_inc(inc("e1_hid_T"), 1)
                    act.wait_ge(*count("e1_down", g * 4 + 4))
                    act.activation(y_sb, y_ps, ACT.Copy).then_inc(inc("e1_y"), 1)

            def vector(dve):
                xin_e = xin.rearrange("p e k c -> p e (k c)")
                flat = xcur.rearrange("p k c -> p (k c)")
                dve.wait_ge(*count("r_xin", KD))
                dve.tensor_copy(flat, xin_e[:, 0]).then_inc(inc("e1_x"), 1)
                dve.wait_ge(*count("r_gated_T", 1))
                dve.sem_inc(inc("e1_added"), 1)
                with dve.Fori(0, E1 // 4) as g:
                    dve.wait_ge(*count("e1_combined", g * 4 + 1))
                    dve.tensor_copy(gcur, gated_T[:, bass.ds(g, 1), :].rearrange("p o s -> p (o s)")).then_inc(inc("e1_gated"), 1)
                    for e4 in range(4):
                        dve.wait_ge(*count("e1_sigmoid", g * 4 + (e4 + 1)))
                        dve.tensor_tensor(hid[0:64], hid[0:64], gate_ps, ALU.mult).then_inc(inc("e1_silu"), 1)
                        dve.wait_ge(*count("e1_silu", g * 4 + (e4 + 1)))
                        dve.wait_ge(*count("e1_up", g * 4 + (e4 + 1)))
                        dve.tensor_tensor(hid[0:64], hid[0:64], up_ps, ALU.mult).then_inc(inc("e1_hid"), 1)
                        dve.tensor_copy(flat, xin_e[:, bass.ds(g * 4 + (e4 + 1), 1)].rearrange("p o s -> p (o s)"))\
                           .then_inc(inc("e1_x"), 1)
                    for j in range(4):
                        dve.wait_ge(*count("e1_combined", g * 4 + (j + 2)))
                        part = x_sb[:, j // 2, 512 * (j % 2):512 * (j % 2) + 512]
                        dve.tensor_tensor(part, part, bank(5 + j % 2), ALU.add).then_inc(inc("e1_added"), 1)

            return Stage(tensor=tensor, vector=vector, scalar=scalar, sync=sync,
                         held=("e1_x", "e1_g", "e1_hid", "e1_hid_T", "e1_y", "gated_T", "xin"))

        moe1 = experts1()
        cols.release("h2", "h2T", "scratch2", "chosen", "gated")
        def ssm_setup():
            names = ("dt", "x", "y", "p", "em1", "mag", "half", "turns", "s", "c", "sin", "cosm1", "cos", "lre1",
                     "lim", "den", "t0", "t1", "cre", "cim", "en_c", "en_s", "sq_c", "sq_s")
            v = {n: tiny(ST) for n in names}
            a_re, a_im = vec["a_re"], vec["a_im"]
            two_pi = 2 * np.pi
            hi = float(np.float32(6.28125))
            lo = float(two_pi - hi)
            magic = float(1.5 * 2 ** 23)

            def scalar(act):
                act.wait_ge(*count("const_loaded", 48))
                act.activation(v["dt"], vec["log_dt"], ACT.Exp).then_inc(inc("ssm_dt"), 1)
                act.wait_ge(*count("ssm_half", 1))
                act.activation(v["s"], v["half"], ACT.Sin)
                act.activation(v["c"], v["t0"], ACT.Sin).then_inc(inc("ssm_sines"), 1)

            def vector(dve):
                step = vchain(dve)
                dve.wait_ge(*count("const_loaded", 48))
                dve.wait_ge(*count("ssm_dt", 1))
                step(dve.tensor_tensor(v["x"], a_re, v["dt"], ALU.mult))
                step(dve.tensor_scalar(v["x"], v["x"], 88.0, -100.0, ALU.min, ALU.max))
                step(dve.tensor_scalar(v["y"], v["x"], 1.0 / 128, None, ALU.mult))
                step(dve.tensor_scalar(v["p"], v["y"], 1.0 / 8, 1.0, ALU.mult, ALU.add))
                for n in range(7, 1, -1):
                    step(dve.tensor_tensor(v["p"], v["p"], v["y"], ALU.mult))
                    step(dve.tensor_scalar(v["p"], v["p"], 1.0 / n, 1.0, ALU.mult, ALU.add))
                step(dve.tensor_tensor(v["em1"], v["p"], v["y"], ALU.mult))
                for _ in range(7):
                    step(dve.scalar_tensor_tensor(v["em1"], v["em1"], 2.0, v["em1"], ALU.add, ALU.mult))
                step(dve.tensor_scalar(v["mag"], v["em1"], 1.0, None, ALU.add))
                step(dve.tensor_tensor(v["y"], a_im, v["dt"], ALU.mult))
                step(dve.tensor_scalar(v["turns"], v["y"], 1 / two_pi, magic, ALU.mult, ALU.add))
                step(dve.tensor_scalar(v["turns"], v["turns"], magic, None, ALU.subtract))
                step(dve.scalar_tensor_tensor(v["y"], v["turns"], -hi, v["y"], ALU.mult, ALU.add))
                step(dve.scalar_tensor_tensor(v["y"], v["turns"], -lo, v["y"], ALU.mult, ALU.add))
                step(dve.tensor_scalar(v["half"], v["y"], 0.5, 1.5707963, ALU.mult, ALU.min))
                step(dve.tensor_scalar(v["half"], v["half"], -1.5707963, None, ALU.max))
                step(dve.tensor_scalar(v["t1"], v["half"], -1.0, None, ALU.mult))
                step(dve.tensor_tensor(v["t1"], v["t1"], v["half"], ALU.max))
                dve.tensor_scalar(v["t0"], v["t1"], -1.0, float(np.pi / 2), ALU.mult, ALU.add).then_inc(inc("ssm_half"), 1)
                dve.wait_ge(*count("ssm_sines", 1))
                dve.scalar_tensor_tensor(v["sin"], v["s"], 2.0, v["c"], ALU.mult, ALU.mult)
                step(dve.scalar_tensor_tensor(v["cosm1"], v["s"], -2.0, v["s"], ALU.mult, ALU.mult))
                step(dve.tensor_scalar(v["cos"], v["cosm1"], 1.0, None, ALU.add))
                step(dve.tensor_tensor(v["lre1"], v["em1"], v["cos"], ALU.mult))
                step(dve.tensor_tensor(v["lre1"], v["lre1"], v["cosm1"], ALU.add))
                step(dve.tensor_tensor(v["lim"], v["mag"], v["sin"], ALU.mult))
                step(dve.tensor_tensor(v["den"], a_re, a_re, ALU.mult))
                step(dve.tensor_tensor(v["t1"], a_im, a_im, ALU.mult))
                step(dve.tensor_tensor(v["den"], v["den"], v["t1"], ALU.add))
                step(dve.reciprocal(v["den"], v["den"]))
                step(dve.tensor_tensor(v["cre"], v["lre1"], a_re, ALU.mult))
                step(dve.tensor_tensor(v["t1"], v["lim"], a_im, ALU.mult))
                step(dve.tensor_tensor(v["cre"], v["cre"], v["t1"], ALU.add))
                step(dve.tensor_tensor(v["cre"], v["cre"], v["den"], ALU.mult))
                step(dve.tensor_tensor(v["cim"], v["lim"], a_re, ALU.mult))
                step(dve.tensor_tensor(v["t1"], v["lre1"], a_im, ALU.mult))
                step(dve.tensor_tensor(v["cim"], v["cim"], v["t1"], ALU.subtract))
                dve.tensor_tensor(v["cim"], v["cim"], v["den"], ALU.mult).then_inc(inc("ssm_params"), 1)

            return Stage(vector=vector, scalar=scalar, mag=v["mag"], v=v)

        ssm_par = ssm_setup()

        def ssm_tables():
            v = ssm_par.v
            cos3, sin3 = ssm_cos, ssm_sin

            def scalar(act):
                act.wait_ge(*count("r_xin", KD))
                act.wait_ge(*count("r_gated_turned", 1))
                act.dma_start(bc_sb, D["ssm_bc"]).then_inc(inc("ssm_bc_loaded"), 16)

            def gpsimd(pool):
                step = gchain(pool)
                pool.wait_ge(*count("ssm_params", 1))
                pool.wait_ge(*count("r_xin", KD))
                pool.wait_ge(*count("r_gated_turned", 1))
                pool.wait_ge(*count("ssm_bc_loaded", 16))
                mul = lambda o, a, b: step(pool.tensor_tensor(o, a, b, ALU.mult))
                b_re, b_im, c_re, c_im = (bc_sb[:, 512 * j:512 * j + 512] for j in range(4))
                r3 = lambda a: a.rearrange("p (s c) -> p s c", s=ST)
                t3 = ssm_tmp[:, 0:512]
                cre, cim = (along(v[n], 32, 2) for n in ("cre", "cim"))
                mul(r3(bb_re), r3(b_re), cre)
                mul(r3(t3), r3(b_im), cim)
                step(pool.tensor_tensor(bb_re, bb_re, t3, ALU.subtract))
                mul(r3(bb_im), r3(b_im), cre)
                mul(r3(t3), r3(b_re), cim)
                step(pool.tensor_tensor(bb_im, bb_im, t3, ALU.add))
                step(pool.tensor_scalar(b_re, c_re, -1.0, None, ALU.mult))
                step(pool.tensor_scalar(b_im, c_im, -1.0, None, ALU.mult))
                step(pool.memset(cos3[:, :, 0:1], 1.0))
                step(pool.memset(sin3[:, :, 0:1], 0.0))
                step(pool.tensor_copy(v["en_c"], v["cos"]))
                step(pool.tensor_copy(v["en_s"], v["sin"]))
                for m in range(8):
                    n = 1 << m
                    for a in range(0, n, 64):
                        w = min(n, 64)
                        ec, es = along(v["en_c"], w, 2), along(v["en_s"], w, 2)
                        c0, s0 = cos3[:, :, a:a + w], sin3[:, :, a:a + w]
                        c1, s1 = cos3[:, :, n + a:n + a + w], sin3[:, :, n + a:n + a + w]
                        tmp = ssm_tmp[:, 0:ST * w].rearrange("p (s c) -> p s c", s=ST)
                        mul(c1, c0, ec)
                        mul(tmp, s0, es)
                        step(pool.tensor_tensor(c1, c1, tmp, ALU.subtract))
                        mul(s1, s0, ec)
                        mul(tmp, c0, es)
                        step(pool.tensor_tensor(s1, s1, tmp, ALU.add))
                    mul(v["sq_c"], v["en_c"], v["en_c"])
                    mul(v["sq_s"], v["en_s"], v["en_s"])
                    mul(v["en_s"], v["en_s"], v["en_c"])
                    step(pool.tensor_tensor(v["en_c"], v["sq_c"], v["sq_s"], ALU.subtract))
                    step(pool.tensor_tensor(v["en_s"], v["en_s"], v["en_s"], ALU.add))
                pool.sem_inc(inc("ssm_tables"), 1)

            return Stage(gpsimd=gpsimd, scalar=scalar)

        bc_sb = cols.take("bc", 2048, top=True)
        bb = cols.take("bb", 1024, top=True)
        bb_re, bb_im = bb[:, 0:512], bb[:, 512:1024]
        ssm_cos = cols.take("ssm_cos", ST * SEQ, top=True).rearrange("p (s c) -> p s c", s=ST)
        ssm_sin = cols.take("ssm_sin", ST * SEQ, top=True).rearrange("p (s c) -> p s c", s=ST)
        ssm_tmp = cols.take("ssm_tmp", 1024, top=True)
        ssm_tab = ssm_tables()
        cols.release(*moe1.held, "ssm_tmp")

        def load_block2(sp):
            for n, unit in enumerate(b2):
                load_unit(sp, U_B2 + n, unit)

        x1T = cols.take("x1T", KD * SEQ).rearrange("p (k s) -> p k s", k=KD)
        turn3 = transpose_rows("b2", x_sb, x1T, ("e1_added", E1 + 1))
        uT = cols.take("uT", 4 * SEQ, top=True).rearrange("p (c s) -> p c s", c=4)
        proj_u = project("pu", x1T, ("b2_T", KD // 2),
                         [(U_SSM, "T", s, 512, KD, uT[:, 2 * s:2 * s + 2]) for s in range(2)])

        half_ring = arena[:, B2_SLOTS * UNIT:SLOTS * UNIT]
        rkv = half_ring[:, 0:3072].rearrange("p (t c) -> p t c", t=NT)
        lora_z = cols.take("lora_z", 2 * (SEQ + 1)).rearrange("p (e s) -> p e s", e=2)
        jobs = [(U_RWKV + c, "tok", t, 512, KD, rkv[:, t, 512 * c:512 * (c + 1)]) for c in range(3) for t in range(NT)]
        jobs += [(U_LORA, "T", 0, 256, KD, lora_z[:, :, 1:SEQ + 1])]
        by_scalar = dict(lanes=1, v_copy=lambda act, out, src: act.activation(out, src, ACT.Copy))
        proj_rkv = project("pr", x1T, ("b2_T", KD // 2), jobs, places=(6, 7), **by_scalar)

        def ssm():
            bT = cols.take("bT", 1024, top=True).rearrange("p (r q s) -> p r q s", r=2, q=4)
            xs = [cols.take(f"ssm_x{j}", 1024, top=True).rearrange("p (r s) -> p r s", r=2) for j in range(2)]
            ts = cols.take("ssm_t", 1024, top=True).rearrange("p (r s) -> p r s", r=2)
            pr = cols.take("ssm_p", 2048, top=True).rearrange("p (r s) -> p r s", r=4)
            yT = bb.rearrange("p (c s) -> p c s", c=4)
            c_re, nc_re, nc_im = bc_sb[:, 1024:1536], bc_sb[:, 0:512], bc_sb[:, 512:1024]
            flat_cos, flat_sin = (a.rearrange("p s c -> p (s c)") for a in (ssm_cos, ssm_sin))
            mag = ssm_par.mag
            HB = ST // 2

            def tensor(pe):
                pe.wait_ge(*count("ssm_tables", 1))
                pe.wait_ge(*count("pu_out0", 1))
                pe.wait_ge(*count("pu_out1", 1))
                for r, src in enumerate((bb_re, bb_im)):
                    for q in range(4):
                        mm = pe.transpose(bank(r)[:, q * P:(q + 1) * P], src[:, q * P:(q + 1) * P], ident)
                    mm.then_inc(inc("ssm_b_turned"), 1)
                pe.wait_ge(*count("ssm_bT", 1))

                def drive(s):
                    if s >= 2:
                        pe.wait_ge(*count("ssm_rotated", s - 1))
                    for r in range(2):
                        for i in range(2):
                            tile = 2 * s + i
                            rows = slice(32 * (tile % 4), 32 * (tile % 4) + 32)
                            mm = pe.matmul(bank(2 * (s % 2) + i)[:, r * SEQ:(r + 1) * SEQ], bT[rows, r, tile // 4],
                                           uT[rows, tile // 4], start=True, stop=True)
                    mm.then_inc(inc("ssm_driven"), 1)

                def emit(s):
                    pe.wait_ge(*count("ssm_products", s + 1))
                    q = s // 2
                    if s % 2 == 0 and q >= 2:
                        pe.wait_ge(*count("ssm_y", q - 1))
                    for i in range(2):
                        tile = 2 * s + i
                        o = bank(4 + q % 2)[32 * (tile % 4):32 * (tile % 4) + 32, 0:SEQ]
                        for n, c in enumerate((c_re, nc_re, nc_im, nc_im)):
                            mm = pe.matmul(o, c[:, 32 * tile:32 * tile + 32], pr[:, n, i * SEQ:(i + 1) * SEQ],
                                           start=(n == 0), stop=(n == 3))
                    mm.then_inc(inc("ssm_emitted"), 1)

                drive(0)
                yield
                for s in range(HB):
                    if s + 1 < HB:
                        drive(s + 1)
                    yield
                    emit(s)
                    yield

            def vector(dve):
                step = vchain(dve)
                dve.wait_ge(*count("ssm_tables", 1))
                dve.memset(lora_z[:, :, 0:1], 0.0)
                dve.wait_ge(*count("ssm_b_turned", 2))
                dve.tensor_copy(bT.rearrange("p r q s -> p (r q s)"), banks(0, 2)).then_inc(inc("ssm_bT"), 1)

                def finish(q):
                    dve.wait_ge(*count("ssm_emitted", 2 * q + 2))
                    dve.scalar_tensor_tensor(yT[:, q], uT[:, q], vec["ssm_d"][:, q:q + 1], bank(4 + q % 2)[:, 0:SEQ],
                                             ALU.mult, ALU.add).then_inc(inc("ssm_y"), 1)

                for s in range(HB):
                    c, sn = flat_cos[:, 512 * s:512 * s + 512], flat_sin[:, 512 * s:512 * s + 512]
                    driven = banks(2 * (s % 2), 2).rearrange("p (i r s) -> p i r s", i=2, r=2)
                    re, im, x = driven[:, :, 0], driven[:, :, 1], xs[s % 2].rearrange("p r (i s) -> p r i s", i=2)
                    c, sn = (a.rearrange("p (i s) -> p i s", i=2) for a in (c, sn))
                    ts_ = ts.rearrange("p r (i s) -> p r i s", i=2)
                    dve.wait_ge(*count("ssm_driven", s + 1))
                    if s >= 2:
                        dve.wait_ge(*count("ssm_products", s - 1))
                    dve.tensor_tensor(x[:, 0], re, c, ALU.mult)
                    dve.tensor_tensor(ts_[:, 0], im, sn, ALU.mult)
                    dve.tensor_tensor(x[:, 1], im, c, ALU.mult)
                    dve.tensor_tensor(ts_[:, 1], re, sn, ALU.mult).then_inc(inc("ssm_rotated"), 1)
                    dve.wait_ge(*count("ssm_rotated", s + 1))
                    dve.tensor_tensor(x[:, 0], x[:, 0], ts_[:, 0], ALU.add)
                    step(dve.tensor_tensor(x[:, 1], x[:, 1], ts_[:, 1], ALU.subtract))
                    for r in range(2):
                        for i in range(2):
                            tile = 2 * s + i
                            part = x[:, r, i]
                            last = dve.tensor_tensor_scan(part, mag[:, tile:tile + 1].broadcast_to([P, SEQ]), part,
                                                          0.0, ALU.mult, ALU.add)
                    last.then_inc(inc("ssm_scanned"), 1)
                    if s % 2 and s >= 3:
                        finish(s // 2 - 1)
                finish(3)
                y = yT.rearrange("p c s -> p (c s)")
                inner = ts.rearrange("p r s -> p (r s)")
                dve.wait_ge(*count("ssm_y", 4))
                step(dve.tensor_tensor(inner, y, y, ALU.mult))
                step(dve.tensor_scalar(inner, inner, 0.044715, 1.0, ALU.mult, ALU.add))
                dve.tensor_tensor(inner, inner, y, ALU.mult).then_inc(inc("ssm_gelu_inner"), 1)
                dve.wait_ge(*count("ssm_gelu_sigmoid", 1))
                dve.tensor_tensor(y, y, inner, ALU.mult).then_inc(inc("ssm_gelu"), 1)

            def scalar(act):
                inner = ts.rearrange("p r s -> p (r s)")
                act.wait_ge(*count("ssm_gelu_inner", 1))
                act.activation(inner, inner, ACT.Sigmoid, scale=float(2 * np.sqrt(2 / np.pi))).then_inc(inc("ssm_gelu_sigmoid"), 1)

            def gpsimd(pool):
                for s in range(HB):
                    c, sn = flat_cos[:, 512 * s:512 * s + 512], flat_sin[:, 512 * s:512 * s + 512]
                    x = xs[s % 2]
                    pool.wait_ge(*count("ssm_scanned", s + 1))
                    if s >= 1:
                        pool.wait_ge(*count("ssm_emitted", s))
                    pool.tensor_tensor(pr[:, 0], x[:, 0], c, ALU.mult)
                    pool.tensor_tensor(pr[:, 1], x[:, 1], sn, ALU.mult)
                    pool.tensor_tensor(pr[:, 2], x[:, 0], sn, ALU.mult)
                    pool.tensor_tensor(pr[:, 3], x[:, 1], c, ALU.mult).then_inc(inc("ssm_products"), 1)

            cols.release("bc", "ssm_cos", "ssm_sin", "ssm_x0", "ssm_x1", "ssm_t", "ssm_p", "bT", "uT")
            return Stage(vector=vector, scalar=scalar, gpsimd=gpsimd, y=yT, parts=(tensor, None, None))

        ssm_scan = ssm()
        zg = cols.take("zg", 2048, top=True).rearrange("p (c s) -> p c s", c=8)
        glu_proj = project("pg", ssm_scan.y, ("ssm_gelu", 1),
                           [(U_GLU, "T", s, 1024, 4, zg[:, 2 * s:2 * s + 2]) for s in range(4)])
        ycT = cols.take("ycT", 1024).rearrange("p (c s) -> p c s", c=4)

        def glu_gate():
            def scalar(act):
                for sem, n in glu_proj.done:
                    act.wait_ge(*count(sem, n))
                for c in range(4):
                    ins = act.activation(zg[:, 4 + c], zg[:, 4 + c], ACT.Sigmoid, bias=vec["glu_b"][:, 4 + c:5 + c])
                ins.then_inc(inc("glu_sigmoid"), 1)

            def vector(dve):
                for sem, n in glu_proj.done:
                    dve.wait_ge(*count(sem, n))
                dve.wait_ge(*count("glu_sigmoid", 1))
                for c in range(4):
                    ins = dve.scalar_tensor_tensor(ycT[:, c], zg[:, c], vec["glu_b"][:, c:c + 1], zg[:, 4 + c],
                                                   ALU.add, ALU.mult)
                ins.then_inc(inc("glu_out"), 1)

            return Stage(vector=vector, scalar=scalar)

        glu = glu_gate()
        cols.release("bb", "zg")
        qkv2 = half_ring[:, 3072:6144].rearrange("p (t c) -> p t c", t=NT)
        jobs = [(U_MOBA + c, "tok", t, 512, KD, qkv2[:, t, 512 * c:512 * (c + 1)]) for c in range(3) for t in range(NT)]
        gates = half_ring[:, 6144:12288].rearrange("p (c s) -> p c s", c=3 * KD)
        gate_jobs = [(U_GATE + c, "T", s, 512, KD, gates[:, 4 * c + 2 * s:4 * c + 2 * s + 2]) for c in range(6) for s in range(2)]
        jobs += gate_jobs[0:4]
        proj_qkv2 = project("pm", x1T, ("b2_T", KD // 2), jobs, after=proj_rkv.done, places=(7,), **by_scalar)

        proj_gates_tail = project("pn", x1T, ("b2_T", KD // 2), gate_jobs[4:6], after=[("rw_xv_out", 1)], places=(7,), **by_scalar)

        def rwkv():
            take = lambda n, w, top=False: cols.take("rw_" + n, w, top)
            tok = lambda n, top=False: take(n, 1024, top).rearrange("p (t c) -> p t c", t=NT)
            rv = {n: take(n, HW) for n in ("gn_w", "gn_b")}
            gg, aa, kk = tok("g"), tok("a"), tok("kk")
            prev = take("prev", 3072, True).rearrange("p (t c) -> p t c", t=NT)
            mu = take("mu", 1536, True)
            rv |= {n: take(n, HW, True) for n in ("w0", "a0", "k_k", "k_a", "r_k")}
            wa, wg = take("wa", HW, True), take("wg", HW, True)
            lz = take("lz", 2 * SEQ, True).rearrange("p (e s) -> p e s", e=2)
            cols.release("rw_prev")
            ld, e1 = tok("ld", True), tok("e1", True)
            flat = lambda a: a.rearrange("p t c -> p (t c)")
            heads = lambda a: a.rearrange("p t (h d) -> p t h d", d=HD)
            r_, k_, v_ = (rkv[:, :, 512 * j:512 * j + 512] for j in range(3))
            ms, sd, bonus, pc = tiny(16), tiny(16), tiny(16), tiny(16)
            cols.release("rw_mu", "rw_w0", "rw_a0", "rw_wa", "rw_wg", "rw_lz", "lora_z")
            e2 = tok("e2", True)
            cols.release("rw_ld", "rw_e1", "rw_e2", "rw_k_k", "rw_k_a", "rw_r_k")
            arT = take("arT", 2048).rearrange("p (q c w s) -> p q c w s", q=4, c=NCH, w=2)
            bT, kT = (take(n, 1024).rearrange("p (q s) -> p q s", q=4) for n in ("bT", "kT"))
            mB, mK = (take(n, 2048).rearrange("p (t g s) -> p t g s", t=NT, g=HEADS) for n in ("mB", "mK"))
            cols.release("rw_kk")
            L = take("L", 1024).rearrange("p (t g s) -> p t g s", t=NT, g=HEADS)
            cols.release("rw_bT", "rw_kT")
            D_, DT, Ws, Cs = (take(n, 1024).rearrange("p (t g s) -> p t g s", t=NT, g=HEADS) for n in ("D", "DT", "W", "C"))
            cols.release("rw_D", "rw_W", "rw_C", "rw_L")
            xv = tok("xv")
            x_s, u_s = take("x", HW), take("u", HW)
            state = take("state", 256).rearrange("p (q i) -> p q i", q=4)
            y_sb = tok("y")
            ysq = xv
            flat4 = lambda a: a.rearrange("p t g s -> p (t g) s")
            both, after, eye = const("before_upto"), const("after"), const("eye64")
            lower = const("lower").rearrange("p (m s) -> p m s", m=6)
            upper = const("upper").rearrange("p (m s) -> p m s", m=6)
            all_heads = [(h % 2, h // 2, (h % 2) * 4 + h // 2, h) for h in range(HEADS)]

            def rows_of(par):
                return slice(64 * par, 64 * par + 64)

            def scalar(act):
                act.wait_ge(*count("glu_out", 1))
                for n, tile in [("mu", mu)] + [(n, rv[n]) for n in ("w0", "a0", "k_k", "k_a", "r_k", "gn_w", "gn_b")]:
                    act.dma_start(tile, row_source(n, n)).then_inc(inc("rw_rows_loaded"), 16)
                act.dma_start(wa, D["lora_wa"]).then_inc(inc("rw_lora_loaded"), 16)
                act.dma_start(wg, D["lora_g"]).then_inc(inc("rw_lora_loaded"), 16)
                for sem, n in proj_rkv.done:
                    act.wait_ge(*count(sem, n))
                for t in range(NT):
                    act.dma_start(prev[1:P, t], rkv[0:P - 1, t]).then_inc(inc("rw_shifted"), 16)
                act.dma_start(prev[0:1, 1], rkv[P - 1:P, 0]).then_inc(inc("rw_shifted"), 16)
                yield
                act.wait_ge(*count("rw_lora", 1))
                act.activation(lz[0:64, 0], lz[0:64, 0], ACT.Tanh)
                act.activation(lz[:, 1], lz[:, 1], ACT.Sigmoid).then_inc(inc("rw_lora_act"), 1)
                yield
                act.wait_ge(*count("rw_lora_out", 3))
                act.activation(flat(gg), banks(4, 2), ACT.Copy).then_inc(inc("rw_gate"), 1)
                for n, a in enumerate((ld, aa)):
                    act.wait_ge(*count("rw_pre", n + 1))
                    act.activation(flat(a), flat(a), ACT.Sigmoid).then_inc(inc("rw_post"), 1)
                yield
                act.wait_ge(*count("rw_ms", 1))
                act.activation(sd, ms, ACT.Sqrt).then_inc(inc("rw_sd"), 1)
                yield
                act.wait_ge(*count("rw_cum", 1))
                act.wait_ge(*count("rw_bonus", 1))
                act.activation(flat(e1), banks(0, 2), ACT.Exp).then_inc(inc("rw_exp"), 1)
                act.activation(flat(e2), banks(0, 2), ACT.Exp, scale=-1.0).then_inc(inc("rw_exp"), 1)
                act.activation(pc, bank(2)[:, 0:16], ACT.Exp).then_inc(inc("rw_exp"), 1)
                act.wait_ge(*count("rw_cum_before", 1))
                act.activation(flat(ld), flat(ld), ACT.Exp).then_inc(inc("rw_exp"), 1)
                yield
                for m in range(1, 6):
                    act.wait_ge(*count("rw_W", m))
                    act.activation(Ws.rearrange("p t g s -> p (t g s)"), banks(0, 2), ACT.Copy).then_inc(inc("rw_W_out"), 1)
                    yield
                for c in range(NCH):
                    R, t = rows_of(c % 2), c // 2
                    act.wait_ge(*count("rw_u", c + 1))
                    act.activation(u_s[R], bank(2)[R], ACT.Copy).then_inc(inc("rw_u_out"), 1)
                    act.wait_ge(*count("rw_y2", c + 1))
                    act.activation(y_sb[R, t], bank(6)[R], ACT.Copy).then_inc(inc("rw_y2_out"), 1)
                for n in range(2):
                    act.wait_ge(*count("rw_gn_ms", 1))
                act.activation(sd, ms, ACT.Sqrt).then_inc(inc("rw_gn_sd"), 1)

            def tensor(pe):
                pe.wait_ge(*count("rw_lora_act", 1))
                pe.wait_ge(*count("rw_lora_loaded", 32))
                for n, (lhs, rhs) in enumerate(((lz[0:64, 0], wa[0:64]), (lz[64:128, 0], wa[64:128]), (lz[:, 1], wg))):
                    for t in range(NT):
                        mm = pe.matmul(bank(2 * n + t), lhs[:, t * P:(t + 1) * P], rhs, start=True, stop=True)
                    mm.then_inc(inc("rw_lora_out"), 1)
                yield
                pe.wait_ge(*count("rw_decay", 1))
                for t in range(NT):
                    pe.matmul(bank(t), const("cumsum"), ld[:, t], start=True, stop=True)
                    for q in range(4):
                        mm = pe.matmul(bank(2)[:, 4 * q + 2 * t:4 * q + 2 * t + 2], ld[:, t, q * P:(q + 1) * P],
                                       const("chunk_sum"), start=True, stop=True)
                mm.then_inc(inc("rw_cum"), 1)
                yield
                pe.wait_ge(*count("rw_scaled", 1))
                for j in range(8):
                    src, half = (kk, r_, aa, k_)[j // 2], j % 2
                    if j >= 4:
                        pe.wait_ge(*count("rw_T", j - 3))
                    for q in (2 * half, 2 * half + 1):
                        for t in range(NT):
                            mm = pe.transpose(bank(3 + j % 4)[:, (q % 2) * SEQ + t * P:(q % 2) * SEQ + (t + 1) * P],
                                              src[:, t, q * P:(q + 1) * P], ident)
                    mm.then_inc(inc("rw_turned"), 1)
                pe.wait_ge(*count("rw_T", 8))
                for j in range(10):
                    if j >= 6:
                        pe.wait_ge(*count("rw_products_out", j - 5))
                    b = bank(j % 6)
                    if j < 8:
                        src, t, par = (bT, kT)[j // 4], j // 2 % 2, j % 2
                        for hh in range(4):
                            for c2 in range(2):
                                c = 2 * t + c2
                                mm = pe.matmul(b[rows_of(c2), hh * P:(hh + 1) * P], src[rows_of(par), hh, c * CH:(c + 1) * CH],
                                               arT[rows_of(par), hh, c].rearrange("p w s -> p (w s)"), start=True, stop=True)
                    else:
                        par = j - 8
                        for c in range(NCH):
                            for hh in range(4):
                                o = (c // 2) * 256 + hh * 64
                                mm = pe.matmul(b[rows_of(c % 2), o:o + 64], arT[rows_of(par), hh, c, 0],
                                               bT[rows_of(par), hh, c * CH:(c + 1) * CH], start=True, stop=True)
                    mm.then_inc(inc("rw_products"), 1)
                yield
                grid = [(t, g, c2) for t in range(NT) for g in range(HEADS) for c2 in range(2)]

                def each(b0, lhs, rhs, sem):
                    for t, g, c2 in grid:
                        R = rows_of(c2)
                        mm = pe.matmul(bank(b0 + t)[R, g * 64:(g + 1) * 64], lhs[R, t, g], rhs[R, t, g], start=True, stop=True)
                    mm.then_inc(inc(sem), 1)

                for m in range(1, 6):
                    pe.wait_ge(*count("rw_inv", m))
                    each(0, Cs, D_, "rw_W")
                    pe.wait_ge(*count("rw_W_out", m))
                    if m < 5:
                        each(2, DT, Ws, "rw_DW")
                    each(4, Ws, DT, "rw_WD")
                    yield
                for sem, n in proj_qkv2.done:
                    pe.wait_ge(*count(sem, n))
                for t, g, c2 in grid:
                    R, h = rows_of(c2), 2 * (g % 4) + g // 4
                    mm = pe.matmul(bank(6 + t)[R, h * 64:(h + 1) * 64], mK[R, t, g, 0:64], v_[R, t, h * 64:(h + 1) * 64],
                                   start=True, stop=True)
                mm.then_inc(inc("rw_xv"), 1)
                for c in range(NCH):
                    R, t = rows_of(c % 2), c // 2
                    pe.wait_ge(*count("rw_state", c + 1))
                    if c >= 1:
                        pe.wait_ge(*count("rw_y", c))
                    else:
                        pe.wait_ge(*count("rw_xv_out", 1))
                        pe.wait_ge(*count("rw_inv", 6))
                    for w, b0, sem in ((0, 0, "rw_x1"), (1, 4, "rw_y1")):
                        for par, hh, g, h in all_heads:
                            mm = pe.matmul(bank(b0 + par)[R, hh * 64:(hh + 1) * 64], arT[rows_of(par), hh, c, w],
                                           state[rows_of(par), hh], start=True, stop=True)
                        mm.then_inc(inc(sem), 1)
                    pe.wait_ge(*count("rw_x", c + 1))
                    for par, hh, g, h in all_heads:
                        mm = pe.matmul(bank(2)[R, h * 64:(h + 1) * 64], DT[R, t, g], x_s[R, h * 64:(h + 1) * 64], start=True, stop=True)
                    mm.then_inc(inc("rw_u"), 1)
                    pe.wait_ge(*count("rw_u_out", c + 1))
                    for par, hh, g, h in all_heads:
                        o, hc = bank(3)[rows_of(par), hh * 64:(hh + 1) * 64], slice(h * 64, (h + 1) * 64)
                        pe.matmul(o, aa[R, t, hc], u_s[R, hc], start=True, stop=False)
                        mm = pe.matmul(o, k_[R, t, hc], v_[R, t, hc], start=False, stop=True)
                    mm.then_inc(inc("rw_s"), 1)
                    for par, hh, g, h in all_heads:
                        o, hc = bank(6)[R, h * 64:(h + 1) * 64], slice(h * 64, (h + 1) * 64)
                        pe.matmul(o, mB[R, t, g, 64:128], u_s[R, hc], start=True, stop=False)
                        mm = pe.matmul(o, mK[R, t, g, 64:128], v_[R, t, hc], start=False, stop=True)
                    mm.then_inc(inc("rw_y2"), 1)
                yield
                pe.wait_ge(*count("rw_y_rows", 1))
                for j in range(2):
                    for q in (2 * j, 2 * j + 1):
                        for t in range(NT):
                            mm = pe.transpose(bank(j)[:, (q % 2) * SEQ + t * P:(q % 2) * SEQ + (t + 1) * P],
                                              y_sb[:, t, q * P:(q + 1) * P], ident)
                    mm.then_inc(inc("rw_y_turned"), 1)

            def gpsimd(pool):
                pass

            def vector(dve):
                step = vchain(dve)
                TT, mul, add, sub = dve.tensor_tensor, ALU.mult, ALU.add, ALU.subtract
                two = lambda a: along(a, NT, 1)
                dve.wait_ge(*count("glu_out", 1))
                dve.memset(prev[0:1, 0], 0.0)
                for sem, n in proj_rkv.done:
                    dve.wait_ge(*count(sem, n))
                step(TT(lz, lora_z[:, :, 0:SEQ], lora_z[:, :, 1:SEQ + 1], sub))
                for e in range(2):
                    last = dve.scalar_tensor_tensor(lz[:, e], lz[:, e], vec["mu_lora"][:, e:e + 1], lora_z[:, e, 1:SEQ + 1], mul, add)
                last.then_inc(inc("rw_lora"), 1)
                dve.wait_ge(*count("rw_shifted", 48))
                dve.wait_ge(*count("rw_rows_loaded", 16 * 8))
                step(TT(prev, prev, rkv, sub))
                step(TT(prev, prev, two(mu), mul))
                step(TT(rkv, rkv, prev, add))
                dve.wait_ge(*count("rw_lora_out", 3))
                TT(ld, banks(0, 2).rearrange("p (t c) -> p t c", t=NT), two(rv["w0"]), add).then_inc(inc("rw_pre"), 1)
                TT(aa, banks(2, 2).rearrange("p (t c) -> p t c", t=NT), two(rv["a0"]), add).then_inc(inc("rw_pre"), 1)
                dve.wait_ge(*count("rw_post", 1))
                dve.tensor_scalar(ld, ld, -float(np.exp(-0.5)), None, mul).then_inc(inc("rw_decay"), 1)
                step(TT(kk, k_, two(rv["k_k"]), mul))
                step(TT(e1, kk, kk, mul))
                step(dve.tensor_reduce(ms, flat(e1).rearrange("p (h d) -> p h d", d=HD), AXX, add))
                dve.tensor_scalar(ms, ms, 1e-24, None, ALU.max).then_inc(inc("rw_ms"), 1)
                dve.wait_ge(*count("rw_post", 2))
                step(dve.tensor_scalar(e1, aa, 1.0, None, sub))
                step(TT(e1, e1, two(rv["k_a"]), mul))
                step(dve.tensor_scalar(e1, e1, 1.0, None, add))
                step(TT(k_, k_, e1, mul))
                step(TT(e1, r_, k_, mul))
                step(TT(e1, e1, two(rv["r_k"]), mul))
                dve.tensor_reduce(bonus, flat(e1).rearrange("p (h d) -> p h d", d=HD), AXX, add).then_inc(inc("rw_bonus"), 1)
                dve.wait_ge(*count("rw_sd", 1))
                step(dve.reciprocal(sd, sd))
                kh = flat(kk).rearrange("p (h d) -> p h d", d=HD)
                step(TT(kh, kh, along(sd, HD, 2), mul))
                step(TT(aa, aa, kk, mul))
                dve.wait_ge(*count("rw_exp", 2))
                TT(ld, banks(0, 2).rearrange("p (t c) -> p t c", t=NT), ld, sub).then_inc(inc("rw_cum_before"), 1)
                TT(r_, r_, e1, mul)
                TT(aa, aa, e2, mul)
                TT(k_, k_, e2, mul)
                dve.wait_ge(*count("rw_exp", 4))
                dve.scalar_tensor_tensor(flat(kk), flat(kk), -1.0, flat(ld), mul, mul).then_inc(inc("rw_scaled"), 1)
                for j in range(8):
                    dve.wait_ge(*count("rw_turned", j + 1))
                    which, half = j // 2, j % 2
                    src = bank(3 + j % 4).rearrange("p (q s) -> p q s", q=2)
                    if which < 2:
                        for q in range(2):
                            last = dve.tensor_copy(arT[:, 2 * half + q, :, which], src[:, q].rearrange("p (c s) -> p c s", c=NCH))
                    else:
                        last = dve.tensor_copy((bT, kT)[which - 2][:, 2 * half:2 * half + 2], src)
                    last.then_inc(inc("rw_T"), 1)
                for j in range(10):
                    dve.wait_ge(*count("rw_products", j + 1))
                    b = bank(j % 6)
                    if j < 8:
                        out, t, par = (mB, mK)[j // 4], j // 2 % 2, j % 2
                        ins = TT(out[:, t, 4 * par:4 * par + 4], b.rearrange("p (g s) -> p g s", g=4), along(both, 4, 1), mul)
                    else:
                        par = j - 8
                        for t in range(NT):
                            ins = TT(L[:, t, 4 * par:4 * par + 4], b[:, 256 * t:256 * t + 256].rearrange("p (g s) -> p g s", g=4),
                                     along(after, 4, 1), mul)
                    ins.then_inc(inc("rw_products_out"), 1)
                dve.wait_ge(*count("rw_products_out", 10))
                LT = mB[:, :, :, 0:64].rearrange("p t g s -> p (t g) s")
                m16 = lambda a: along(a, 16, 1)
                TT(flat4(D_), flat4(L), m16(lower[:, 0]), mul)
                step(TT(flat4(DT), LT, m16(upper[:, 0]), mul))
                TT(flat4(D_), flat4(D_), m16(eye), add)
                TT(flat4(DT), flat4(DT), m16(eye), add)
                TT(flat4(Cs), LT, m16(upper[:, 1]), mul).then_inc(inc("rw_inv"), 1)
                for m in range(1, 6):
                    if m < 5:
                        dve.wait_ge(*count("rw_DW", m))
                        dve.wait_ge(*count("rw_WD", m))
                        TT(flat4(Cs), LT, m16(upper[:, m + 1]), mul)
                        TT(D_.rearrange("p t g s -> p (t g s)"), D_.rearrange("p t g s -> p (t g s)"), banks(2, 2), add)
                    else:
                        dve.wait_ge(*count("rw_WD", m))
                    TT(DT.rearrange("p t g s -> p (t g s)"), DT.rearrange("p t g s -> p (t g s)"), banks(4, 2), add)\
                        .then_inc(inc("rw_inv"), 1)
                dve.wait_ge(*count("rw_xv", 1))
                dve.tensor_copy(flat(xv), banks(6, 2)).then_inc(inc("rw_xv_out"), 1)
                dve.wait_ge(*count("rw_xv_out", 1))
                dve.memset(state, 0.0).then_inc(inc("rw_state"), 1)
                for c in range(NCH):
                    R, t = rows_of(c % 2), c // 2
                    by_par = lambda a: a.rearrange("p (q r d) -> p q r d", q=4, r=2)
                    dve.wait_ge(*count("rw_x1", c + 1))
                    for par in range(2):
                        last = TT(by_par(x_s[R])[:, :, par], bank(par)[R, 0:256].rearrange("p (q d) -> p q d", q=4),
                                  by_par(xv[R, t])[:, :, par], add)
                    last.then_inc(inc("rw_x"), 1)
                    dve.wait_ge(*count("rw_s", c + 1))
                    dve.wait_ge(*count("rw_state", c + 1))
                    step(TT(state, state, bank(3)[:, 0:256].rearrange("p (q i) -> p q i", q=4), add))
                    dve.wait_ge(*count("rw_y1", c + 1))
                    TT(state, state, along(pc.rearrange("p (q c) -> p q c", q=4)[:, :, c], CH, 2), mul).then_inc(inc("rw_state"), 1)
                    dve.wait_ge(*count("rw_y2_out", c + 1))
                    for par in range(2):
                        yy = by_par(y_sb[R, t])[:, :, par]
                        last = TT(yy, yy, bank(4 + par)[R, 0:256].rearrange("p (q d) -> p q d", q=4), add)
                    last.then_inc(inc("rw_y"), 1)
                dve.wait_ge(*count("rw_y", NCH))
                yh = flat(y_sb).rearrange("p (h d) -> p h d", d=HD)
                step(dve.tensor_reduce(ms, yh, AXX, add))
                step(dve.tensor_scalar(ms, ms, -1.0 / HD, None, mul))
                step(TT(yh, yh, along(ms, HD, 2), add))
                step(TT(ysq, y_sb, y_sb, mul))
                step(dve.tensor_reduce(ms, flat(ysq).rearrange("p (h d) -> p h d", d=HD), AXX, add))
                dve.tensor_scalar(ms, ms, 1.0 / HD, GN_EPS, mul, add).then_inc(inc("rw_gn_ms"), 1)
                for t in range(NT):
                    last = TT(heads(ysq)[:, t], heads(v_)[:, t], along(bonus[:, 8 * t:8 * t + 8], HD, 2), mul)
                dve.wait_ge(*count("rw_gn_sd", 1))
                step(dve.reciprocal(sd, sd))
                step(TT(yh, yh, along(sd, HD, 2), mul))
                step(TT(y_sb, y_sb, two(rv["gn_w"]), mul))
                step(TT(y_sb, y_sb, two(rv["gn_b"]), add))
                step(TT(y_sb, y_sb, ysq, add))
                dve.wait_ge(*count("rw_gate", 1))
                TT(y_sb, y_sb, gg, mul).then_inc(inc("rw_y_rows"), 1)
                for j in range(2):
                    dve.wait_ge(*count("rw_y_turned", j + 1))
                    dve.tensor_copy(yaT[:, 2 * j:2 * j + 2], bank(j).rearrange("p (q s) -> p q s", q=2)).then_inc(inc("rw_out"), 1)

            cols.release(*[n for n in list(cols.held) if n.startswith("rw_")])
            return Stage(vector=vector, parts=(tensor, None, scalar))

        yaT = cols.take("yaT", 1024).rearrange("p (c s) -> p c s", c=4)
        rwkv7 = rwkv()
        ybT = cols.take("ybT", 1024).rearrange("p (c s) -> p c s", c=4)
        attention2 = attention("mb", qkv2, proj_qkv2.done, ybT, const("causal").rearrange("p (t s) -> p t s", t=NT), False)

        proj_gates = project("pt", x1T, ("rw_out", 2), gate_jobs[6:],
                             after=proj_qkv2.done + proj_gates_tail.done)
        mergedT = cols.take("mergedT", KD * SEQ).rearrange("p (k s) -> p k s", k=KD)

        def merge():
            branches = (yaT, ybT, ycT)

            def tensor(pe):
                for n in range(3):
                    unit_ready(pe, U_UP + n)
                for sem, n in proj_gates.done + [("mb_out", 4)]:
                    pe.wait_ge(*count(sem, n))
                for d in range(KD):
                    if d >= 2:
                        pe.wait_ge(*count("mg_out", d - 1))
                    for n, y in enumerate(branches):
                        o = banks(2 * (d % 2), 2)[:, n * SEQ:(n + 1) * SEQ]
                        w = slot(U_UP + n, 4, DM)
                        for k in range(4):
                            mm = pe.matmul(o, w[:, k, d * P:(d + 1) * P], y[:, k], start=(k == 0), stop=(k == 3))
                    mm.then_inc(inc("mg_products"), 1)
                pe.wait_ge(*count("mg_products", KD))
                pe.sem_inc(inc("units_used"), 3)

            def scalar(act):
                for sem, n in proj_gates.done + proj_gates_tail.done + proj_qkv2.done:
                    act.wait_ge(*count(sem, n))
                for d in range(KD):
                    for tile in (d, KD + d, 2 * KD + d):
                        ins = act.activation(gates[:, tile], gates[:, tile], ACT.Sigmoid, bias=vec["gate_b"][:, tile:tile + 1])
                    ins.then_inc(inc("mg_gates"), 1)

            def vector(dve):
                step = vchain(dve)
                g3 = gates.rearrange("p (b d) s -> p b d s", b=3)
                for d in range(KD):
                    dve.wait_ge(*count("mg_gates", d + 1))
                    dve.wait_ge(*count("mg_products", d + 1))
                    src = banks(2 * (d % 2), 2)[:, 0:3 * SEQ].rearrange("p (b s) -> p b s", b=3)
                    dve.tensor_tensor(g3[:, :, d], g3[:, :, d], src, ALU.mult).then_inc(inc("mg_out"), 1)
                    dve.wait_ge(*count("mg_out", d + 1))
                    step(dve.tensor_tensor(g3[:, 0, d], g3[:, 0, d], g3[:, 1, d], ALU.add))
                    dve.tensor_tensor(mergedT[:, d], g3[:, 0, d], g3[:, 2, d], ALU.add).then_inc(inc("mg_T"), 1)

            return Stage(tensor=tensor, vector=vector, scalar=scalar)

        merged = merge()
        cols.release("x1T", "yaT", "ybT", "ycT")
        jobs = [(U_OUT2 + c, "tok", t, 512, KD, x_sb[:, t, 512 * c:512 * (c + 1)]) for c in range(2) for t in range(NT)]
        out_proj2 = project("o2", mergedT, ("mg_T", KD), jobs, lanes=1,
                            v_copy=lambda dve, out, src: dve.scalar_tensor_tensor(out, out, DEEPNORM_ALPHA, src, ALU.mult, ALU.add))
        cols.release("mergedT")

        ln_rows = {n: cols.take(n, DM, top=True) for n in ("ln2_w", "ln2_b")}
        iota = cols.take("numbers", NSLOT, top=True)
        w_router2 = cols.take("w_router2", KD * 36, top=True).rearrange("p (k e) -> p k e", k=KD)
        ln_rows |= {n: cols.take(n, DM, top=True) for n in ("ln1_w", "ln1_b")}

        def layer_norm(tag, ready, w, b):
            mean, ss, sd = tiny(NT), tiny(NT), tiny(NT)
            squares = cols.take(tag + "_squares", DM)

            def vector(dve):
                step = vchain(dve)
                dve.wait_ge(*count(*ready))
                step(dve.tensor_reduce(mean, x_sb, AXX, ALU.add))
                dve.tensor_scalar(mean, mean, -1.0 / DM, None, ALU.mult).then_inc(inc(tag + "_mean"), 1)
                dve.wait_ge(*count(tag + "_ss", NT))
                dve.tensor_scalar(ss, ss, 1.0 / DM, LN_EPS, ALU.mult, ALU.add).then_inc(inc(tag + "_var"), 1)
                dve.wait_ge(*count(tag + "_sd", 1))
                step(dve.reciprocal(sd, sd))
                for t in range(NT):
                    last = dve.tensor_scalar(x_sb[:, t], x_sb[:, t], mean[:, t:t + 1], sd[:, t:t + 1], ALU.add, ALU.mult)
                step(last)
                dve.wait_ge(*count("ln_rows_loaded", 96))
                step(dve.tensor_tensor(x_sb, x_sb, along(ln_rows[w], NT, 1), ALU.mult))
                dve.tensor_tensor(x_sb, x_sb, along(ln_rows[b], NT, 1), ALU.add).then_inc(inc(tag + "_out"), 1)

            def scalar(act):
                act.wait_ge(*count(tag + "_mean", 1))
                for t in range(NT):
                    act.activation(squares, x_sb[:, t], ACT.Square, bias=mean[:, t:t + 1], accum_out=ss[:, t:t + 1])\
                       .then_inc(inc(tag + "_ss"), 1)
                    act.wait_ge(*count(tag + "_ss", t + 1))
                act.wait_ge(*count(tag + "_var", 1))
                act.activation(sd, ss, ACT.Sqrt).then_inc(inc(tag + "_sd"), 1)

            cols.release(tag + "_squares")
            return Stage(vector=vector, scalar=scalar)

        def load_ln_rows(act):
            act.wait_ge(*count("mg_T", KD))
            for n, tile in ln_rows.items():
                act.dma_start(tile, row_source(n, n)).then_inc(inc("ln_rows_loaded"), 16)
            act.dma_start(iota, D["consts"][:, n_const:]).then_inc(inc("ln_rows_loaded"), 16)
            act.dma_start(w_router2, D["w_router_2"].rearrange("(k p) e -> p k e", p=P)).then_inc(inc("ln_rows_loaded"), 16)

        norm3 = layer_norm("l1", ("o2_out0", 4), "ln1_w", "ln1_b")
        x2T = cols.take("x2T", KD * SEQ).rearrange("p (k s) -> p k s", k=KD)
        turn4 = transpose_rows("x2", x_sb, x2T, ("l1_out", 1))

        weight2 = cols.take("weight2", NT * E2).rearrange("p (t e) -> p t e", t=NT)
        sorted_T = cols.take("sorted_T", KD * (NSLOT + SEQ)).rearrange("p (k c) -> p k c", k=KD)
        picks = cols.take("picks", NT * NSLOT).rearrange("p (t c) -> p t c", t=NT)
        rank2 = cols.take("rank2", NT * E2).rearrange("p (t e) -> p t e", t=NT)
        zero = cols.take("zero", P)

        def route2():
            lg = cols.take("r2_logits", NT * 36).rearrange("p (t e) -> p t e", t=NT)
            em = cols.take("r2_em", NT * E2).rearrange("p (t e) -> p t e", t=NT)
            er = cols.take("r2_er", NT * E2).rearrange("p (t e) -> p t e", t=NT)
            er_T, rank, ones_row = cols.take("r2_er_T", SEQ), cols.take("r2_rank", SEQ), cols.take("r2_ones", SEQ)
            place = cols.take("r2_place", NT * E2).rearrange("p (t e) -> p t e", t=NT)
            first = tiny(1)
            number = cols.take("r2_number", NT * 8).rearrange("p (t e) -> p t e", t=NT)
            local = cols.take("r2_local", SEQ)
            padded = cols.take("r2_padded", NT * 16).rearrange("p (t e) -> p t e", t=NT)
            rest = cols.take("r2_rest", NT * 16).rearrange("p (t e) -> p t e", t=NT)
            find = cols.take("r2_find", NT * 8).rearrange("p (t e) -> p t e", t=NT)
            best = cols.take("r2_best", NT * 8).rearrange("p (t e) -> p t e", t=NT)
            eg = cols.take("r2_eg", NT * NG).rearrange("p (t e) -> p t e", t=NT)
            gmax, gsum, emax, esum = tiny(NT), tiny(NT), tiny(NT), tiny(NT)
            logits = bank(4, NT * 36).rearrange("p (t e) -> p t e", t=NT)
            LOWEST, TAKEN, OTHER = -3.0e38, -3.3e38, -1e30

            def tensor(pe):
                pe.wait_ge(*count("x2_T", KD // 2))
                pe.wait_ge(*count("ln_rows_loaded", 96))
                for t in range(NT):
                    for k in range(KD):
                        mm = pe.matmul(logits[:, t], x2T[:, k, t * P:(t + 1) * P], w_router2[:, k],
                                       start=(k == 0), stop=(k == KD - 1))
                mm.then_inc(inc("r2_logits"), 1)
                pe.wait_ge(*count("r2_chosen", 1))
                for t in range(NT):
                    mm = pe.transpose(bank(5)[0:E2, t * P:(t + 1) * P], er[:, t], ident)
                mm.then_inc(inc("r2_er_turned"), 1)
                pe.wait_ge(*count("r2_ranks", 1))
                how_many = rank[0:E2, SEQ - 1:SEQ]
                before = const("before_upto")[0:E2, 0:E2]
                pe.matmul(bank(6)[0:E2, 0:1], before, how_many, start=True, stop=True)
                pe.matmul(bank(6)[0:1, 32:32 + E2], how_many, before, start=True, stop=True)
                pe.matmul(bank(6)[0:1, 64:64 + E2], how_many, ident[0:E2, 0:E2], start=True, stop=True)\
                  .then_inc(inc("r2_before"), 1)
                pe.wait_ge(*count("r2_numbers", 1))
                for j, of in enumerate((ones_row, local)):
                    for t in range(NT):
                        mm = pe.transpose(bank(7)[:, (2 * j + t) * E2:(2 * j + t + 1) * E2], of[0:E2, t * P:(t + 1) * P],
                                          ident[0:E2, 0:E2])
                mm.then_inc(inc("r2_turned_back"), 1)
                pe.wait_ge(*count("r2_picks", 1))
                for k in range(KD):
                    if k >= 4:
                        pe.wait_ge(*count("r2_sorted", k - 3))
                    for t in range(NT):
                        mm = pe.matmul(bank(k % 4), x_sb[:, t, k * P:(k + 1) * P], picks[:, t],
                                       start=(t == 0), stop=(t == NT - 1))
                    mm.then_inc(inc("r2_gathered"), 1)

            def scalar(act):
                act.wait_ge(*count("r2_gmax", 1))
                for t in range(NT):
                    ins = act.activation(eg[:, t], lg[:, t, 0:NG], ACT.Exp, bias=gmax[:, t:t + 1], accum_out=gsum[:, t:t + 1])
                ins.then_inc(inc("r2_group"), 1)
                act.wait_ge(*count("r2_emax", 1))
                for t in range(NT):
                    ins = act.activation(weight2[:, t], em[:, t], ACT.Exp, bias=emax[:, t:t + 1])
                ins.then_inc(inc("r2_exp"), 1)
                for k in range(KD):
                    act.wait_ge(*count("r2_gathered", k + 1))
                    act.activation(sorted_T[:, k, 0:NSLOT], bank(k % 4), ACT.Copy).then_inc(inc("r2_sorted"), 1)

            def vector(dve):
                step = vchain(dve)
                dve.memset(ones_row, 1.0)
                dve.memset(begin[:, E2 + 1:], 0)
                dve.memset(sorted_T[:, :, NSLOT:], 0.0).then_inc(inc("r2_tail"), 1)
                dve.memset(padded, LOWEST)
                dve.memset(find, LOWEST)
                dve.wait_ge(*count("r2_logits", 1))
                step(dve.tensor_tensor(lg, logits, along(row["router_b"], NT, 1), ALU.add))
                step(dve.tensor_copy(padded[:, :, 0:NG], lg[:, :, 0:NG]))
                step(dve.tensor_reduce(find[:, :, 0:1], lg[:, :, 0:NG], AXX, ALU.max))
                dve.tensor_reduce(gmax, lg[:, :, 0:NG], AXX, ALU.max, negate=True).then_inc(inc("r2_gmax"), 1)
                for t in range(NT):
                    last = dve.match_replace(rest[:, t], find[:, t], padded[:, t], TAKEN)
                step(last)
                g = rest[:, :, 0:NG]
                step(dve.tensor_tensor(g, g, padded[:, :, 0:NG], ALU.not_equal))
                step(dve.tensor_scalar(g, g, 1.0, -OTHER, ALU.subtract, ALU.mult))
                for t in range(NT):
                    last = dve.tensor_tensor(em[:, t].rearrange("p (g e) -> p g e", g=NG),
                                             lg[:, t, NG:36].rearrange("p (g e) -> p g e", g=NG),
                                             along(rest[:, t, 0:NG], EPG, 2), ALU.add)
                step(last)
                for t in range(NT):
                    last = dve.max(best[:, t], em[:, t])
                step(last)
                dve.tensor_scalar(emax, best[:, :, 0], -1.0, None, ALU.mult).then_inc(inc("r2_emax"), 1)
                step(dve.memset(find, OTHER))
                step(dve.tensor_copy(find[:, :, 0:2], best[:, :, 0:2]))
                for t in range(NT):
                    last = dve.match_replace(er[:, t], find[:, t], em[:, t], TAKEN)
                step(last)
                step(dve.tensor_tensor(er, er, em, ALU.not_equal))
                dve.scalar_tensor_tensor(er, em, OTHER / 2, er, ALU.is_gt, ALU.mult).then_inc(inc("r2_chosen"), 1)
                dve.wait_ge(*count("r2_chosen", 1))
                dve.wait_ge(*count("r2_exp", 1))
                step(dve.tensor_tensor(weight2, weight2, er, ALU.mult))
                step(dve.tensor_reduce(esum, weight2, AXX, ALU.add))
                dve.wait_ge(*count("r2_group", 1))
                step(dve.tensor_tensor(esum, esum, gsum, ALU.mult))
                step(dve.reciprocal(esum, esum))
                step(dve.tensor_tensor(weight2, weight2, along(esum, E2, 2), ALU.mult))
                dve.wait_ge(*count("r2_er_turned", 1))
                step(dve.tensor_copy(er_T[0:E2], bank(5)[0:E2, 0:SEQ]))
                dve.tensor_tensor_scan(rank[0:E2], ones_row[0:E2], er_T[0:E2], 0.0, ALU.mult, ALU.add)\
                   .then_inc(inc("r2_ranks"), 1)
                dve.wait_ge(*count("r2_before", 1))
                step(dve.tensor_copy(first[0:E2], bank(6)[0:E2, 0:1]))
                dve.tensor_copy(begin[:, 0:E2], bank(6)[0:1, 32:32 + E2])
                dve.tensor_reduce(begin[:, E2:E2 + 1], bank(6)[0:1, 64:64 + E2], AXX, ALU.max).then_inc(inc("r2_begin"), 1)
                dve.tensor_tensor(local[0:E2], rank[0:E2], er_T[0:E2], ALU.mult)
                dve.scalar_tensor_tensor(ones_row[0:E2], rank[0:E2], first[0:E2], er_T[0:E2], ALU.add, ALU.mult)\
                   .then_inc(inc("r2_numbers"), 1)
                dve.wait_ge(*count("r2_turned_back", 1))
                step(dve.tensor_copy(place, bank(7)[:, 0:NT * E2].rearrange("p (t e) -> p t e", t=NT)))
                dve.tensor_copy(rank2, bank(7)[:, NT * E2:2 * NT * E2].rearrange("p (t e) -> p t e", t=NT))
                for t in range(NT):
                    last = dve.max(number[:, t], place[:, t])
                step(last)
                for t in range(NT):
                    last = dve.tensor_scalar(picks[:, t], iota, number[:, t, 0:1], None, ALU.is_equal)
                step(last)
                for t in range(NT):
                    last = dve.scalar_tensor_tensor(picks[:, t], iota, number[:, t, 1:2], picks[:, t], ALU.is_equal, ALU.add)
                last.then_inc(inc("r2_picks"), 1)
                step(dve.memset(zero, 0.0))
                dve.sem_inc(inc("r2_done"), 1)

            cols.release("r2_logits", "r2_em", "r2_er", "r2_padded", "r2_rest", "r2_find", "r2_best", "r2_eg",
                         "r2_er_T", "r2_rank", "r2_ones", "r2_place", "r2_number", "r2_local")
            return Stage(tensor=tensor, vector=vector, scalar=scalar)

        routing2 = route2()
        cols.release("x2T", "picks", "ln1_w", "ln1_b")

        def experts2():
            QUARTER = SLOTS * UNIT // 4
            PAIRS = E2 // 2
            buf = [arena[:, b * QUARTER:(b + 1) * QUARTER] for b in range(4)]
            w_in = [a[:, 0:4096].rearrange("p (k n) -> p k n", k=KD) for a in buf]
            w_down = [a[:, 4096:6144].rearrange("p (k n) -> p k n", k=2) for a in buf]
            tokens = [cols.take(f"m2_tokens{j}", KD * 2 * ROOM).rearrange("p (k c) -> p k c", k=KD) for j in range(2)]
            hid = [cols.take(f"m2_hid{j}", FF2) for j in range(2)]
            picked = [cols.take(f"m2_picked{j}", NT * 2 * ROOM) for j in range(2)]
            turned = [cols.take(f"m2_turned{j}", 512) for j in range(2)]
            y_sb = cols.take("m2_y", DM)
            in_ps, turned_ps, y_ps = bank(4), bank(5), banks(6, 2)

            def load(sp, q, pair):
                for b, e in ((2 * q, 2 * pair), (2 * q + 1, 2 * pair + 1)):
                    for j, name in enumerate(("expert_w_gate_2", "expert_w_up_2")):
                        src = D[name][bass.ds(e, 1)].rearrange("o d n -> (o d) n")
                        sp.dma_start(w_in[b][:, :, FF2 * j:FF2 * (j + 1)], src.rearrange("(k p) n -> p k n", p=P))\
                          .then_inc(inc(f"m2_in_loaded{q}"), 16)

            def load_down(sp, q, pair):
                for b, e in ((2 * q, 2 * pair), (2 * q + 1, 2 * pair + 1)):
                    src = D["expert_w_down_2"][bass.ds(e, 1)].rearrange("o d n -> (o d) n")
                    sp.dma_start(w_down[b], src.rearrange("(k p) n -> p k n", p=P)).then_inc(inc(f"m2_down_loaded{q}"), 16)

            def either(eng, loop):
                eng.wait_ge(*count("r2_begin", 1))
                fullest = eng.value_load(begin[:, E2:E2 + 1], min_val=0, max_val=SEQ)
                with eng.If(fullest <= ROOM):
                    loop(1)
                with eng.Else():
                    loop(SEQ // ROOM)
                eng.end_ifs()

            def rounds(eng, subs, body):
                with eng.Fori(0, PAIRS // 2 - 1) as g:
                    body(g, False)
                body(PAIRS // 2 - 1, True)

            def place_of(g, u, subs):
                return g * 2 + u // subs, u % subs, u // subs % 2

            def sync(sp):
                sp.wait_ge(*count("mg_T", KD))
                load(sp, 1, 1)
                load_down(sp, 1, 1)
                sp.wait_ge(*count("units_used", U_END))
                load(sp, 0, 0)
                load_down(sp, 0, 0)

                def loop(subs):
                    with sp.Fori(1, PAIRS // 2) as g:
                        for q in range(2):
                            sp.wait_ge(*count("m2_in", g * (2 * subs) + (q - 1) * subs))
                            load(sp, q, g * 2 + q)
                            sp.wait_ge(*count("m2_down", g * (2 * subs) + (q - 1) * subs))
                            load_down(sp, q, g * 2 + q)

                either(sp, loop)

            def tensor(pe):
                pe.wait_ge(*count("r2_done", 1))
                pe.wait_ge(*count("r2_sorted", KD))
                for j in range(4):
                    pe.matmul(bank(j), zero, x_sb[:, 0, 0:512], start=True, stop=False)

                def loop(subs):
                    R = 2 * subs

                    def products_in(g, u, ks):
                        pair, sub, q = place_of(g, u, subs)
                        if ks[0] == 0:
                            pe.wait_ge(*count(f"m2_in_loaded{q}", (g + u // R) * 64 + 64))
                            pe.wait_ge(*count("m2_tokens", g * R + (u + 1)))
                        for k in ks:
                            for h in range(2):
                                mm = pe.matmul(in_ps[ROOM * h:ROOM * (h + 1)], tokens[u % 2][:, k, ROOM * h:ROOM * (h + 1)],
                                               w_in[2 * q + h][:, k], start=(k == 0), stop=(k == KD - 1))
                        if ks[-1] == KD - 1:
                            mm.then_inc(inc("m2_in"), 1)

                    def body(g, last):
                        for u in range(R):
                            follows = not (last and u == R - 1)
                            pair, sub, q = place_of(g, u, subs)
                            pe.wait_ge(*count("m2_hid", g * R + (u + 1)))
                            for f in range(2):
                                pe.transpose(turned_ps[:, f * P:(f + 1) * P], hid[u % 2][:, f * P:(f + 1) * P], ident)
                            for t in range(NT):
                                mm = pe.transpose(turned_ps[:, (2 + t) * P:(3 + t) * P], picked[u % 2][:, t * P:(t + 1) * P], ident)
                            mm.then_inc(inc("m2_turned"), 1)
                            if follows:
                                products_in(g, u + 1, range(0, 4))
                            pe.wait_ge(*count(f"m2_down_loaded{q}", g * 32 + 32))
                            pe.wait_ge(*count("m2_turned_out", g * R + (u + 1)))
                            for n in range(2):
                                for f in range(2):
                                    for h in range(2):
                                        mm = pe.matmul(y_ps[ROOM * h:ROOM * (h + 1), 512 * n:512 * (n + 1)],
                                                       turned[u % 2][:, f * P + ROOM * h:f * P + ROOM * (h + 1)],
                                                       w_down[2 * q + h][:, f, 512 * n:512 * (n + 1)],
                                                       start=(f == 0), stop=(f == 1))
                            mm.then_inc(inc("m2_down"), 1)
                            if follows:
                                products_in(g, u + 1, range(4, KD))
                            pe.wait_ge(*count("m2_y0", g * R + (u + 1)))
                            pe.wait_ge(*count("m2_y1", g * R + (u + 1)))
                            for t in range(NT):
                                for n in range(2):
                                    mm = pe.matmul(bank(2 * t + n), turned[u % 2][:, (2 + t) * P:(3 + t) * P],
                                                   y_sb[:, 512 * n:512 * (n + 1)], start=False, stop=not follows)
                            mm.then_inc(inc("m2_combined"), 1)

                    products_in(0, 0, range(KD))
                    rounds(pe, subs, body)

                either(pe, loop)

            def scalar(act):
                act.wait_ge(*count("r2_sorted", KD))
                act.wait_ge(*count("r2_tail", 1))
                act.wait_ge(*count("r2_done", 1))

                def loop(subs):
                    R = 2 * subs

                    def take_tokens(g, u):
                        pair, sub, q = place_of(g, u, subs)
                        for h in range(2):
                            at = act.value_load(begin[:, bass.ds(pair * 2 + h, 1)], min_val=0, max_val=NSLOT)
                            ins = act.activation(tokens[u % 2][:, :, ROOM * h:ROOM * (h + 1)],
                                                 sorted_T[:, :, bass.ds(at + ROOM * sub, ROOM)], ACT.Copy)
                        ins.then_inc(inc("m2_tokens"), 1)

                    def sigmoid(g, u):
                        act.wait_ge(*count("m2_in", g * R + (u + 1)))
                        act.activation(hid[u % 2], in_ps[:, 0:FF2], ACT.Sigmoid).then_inc(inc("m2_sigmoid"), 1)

                    def body(g, last):
                        for u in range(R):
                            act.wait_ge(*count("m2_turned", g * R + (u + 1)))
                            act.activation(turned[u % 2], turned_ps, ACT.Copy).then_inc(inc("m2_turned_out"), 1)
                            if not (last and u >= R - 2):
                                take_tokens(g, u + 2)
                            act.wait_ge(*count("m2_down", g * R + (u + 1)))
                            act.activation(y_sb[:, 512:1024], y_ps[:, 512:1024], ACT.Copy).then_inc(inc("m2_y1"), 1)
                            if not (last and u == R - 1):
                                sigmoid(g, u + 1)

                    take_tokens(0, 0)
                    take_tokens(0, 1)
                    sigmoid(0, 0)
                    rounds(act, subs, body)

                either(act, loop)

            def vector(dve):
                def loop(subs):
                    R = 2 * subs
                    step = vchain(dve)

                    def pick(g, u):
                        pair, sub, q = place_of(g, u, subs)
                        o = picked[u % 2].rearrange("p (t h c) -> p t h c", t=NT, h=2)
                        ranks, w = rank2[:, :, bass.ds(pair * 2, 2)], weight2[:, :, bass.ds(pair * 2, 2)]
                        numbers = iota[:, ROOM * sub:ROOM * (sub + 1)]
                        dve.tensor_tensor(o, along(ranks, ROOM, 3), along(along(numbers, 2, 1), NT, 1), ALU.is_equal)\
                           .then_inc(inc("m2_equal"), 1)
                        dve.wait_ge(*count("m2_equal", g * R + (u + 1)))
                        dve.tensor_tensor(o, o, along(w, ROOM, 3), ALU.mult)

                    def multiply(g, u):
                        dve.wait_ge(*count("m2_sigmoid", g * R + (u + 1)))
                        dve.tensor_tensor(hid[u % 2], hid[u % 2], in_ps[:, 0:FF2], ALU.mult).then_inc(inc("m2_silu"), 1)
                        dve.wait_ge(*count("m2_silu", g * R + (u + 1)))
                        dve.tensor_tensor(hid[u % 2], hid[u % 2], in_ps[:, FF2:2 * FF2], ALU.mult).then_inc(inc("m2_hid"), 1)

                    def body(g, last):
                        for u in range(R):
                            dve.wait_ge(*count("m2_turned", g * R + (u + 1)))
                            if not (last and u == R - 1):
                                pick(g, u + 1)
                            dve.wait_ge(*count("m2_down", g * R + (u + 1)))
                            dve.tensor_copy(y_sb[:, 0:512], y_ps[:, 0:512]).then_inc(inc("m2_y0"), 1)
                            if not (last and u == R - 1):
                                multiply(g, u + 1)

                    pick(0, 0)
                    multiply(0, 0)
                    rounds(dve, subs, body)
                    dve.wait_ge(*count("m2_combined", PAIRS * subs))

                dve.wait_ge(*count("r2_done", 1))
                dve.wait_ge(*count("r2_gathered", KD))
                either(dve, loop)
                xf = x_sb.rearrange("p t d -> p (t d)")
                dve.scalar_tensor_tensor(xf, xf, DEEPNORM_ALPHA, banks(0, 4), ALU.mult, ALU.add).then_inc(inc("m2_added"), 1)

            cols.release("m2_y")
            return Stage(tensor=tensor, vector=vector, scalar=scalar, sync=sync)

        moe2 = experts2()
        norm4 = layer_norm("l2", ("m2_added", 1), "ln2_w", "ln2_b")

        def store(sp):
            sp.wait_ge(*count("l2_out", 1))
            sp.dma_start(D["out"].rearrange("(t p) d -> p t d", p=P), x_sb).then_inc(inc("out_stored"), 16)
            sp.wait_ge(*count("out_stored", 16))

        block = ctx.enter_context(nc.Block())

        ORDER1 = ("aaaab" + "ab" * 17, "babba" + "bba" * 4, "babb" + "abb" * 5)
        ORDER2 = ("aaaab" + "ab" * 17, "babba" + "bba" * 4, "babb" + "abb" * 5)

        @block.sync
        def _(sp):
            load_inputs(sp)
            moe1.sync(sp)
            load_block2(sp)
            moe2.sync(sp)
            store(sp)

        @block.tensor
        def _(pe):
            turn1.tensor(pe)
            proj1.tensor(pe)
            take_turns(pe, ORDER1[0], proj2.parts[0], attention1.parts[0])
            hgrn2.tensor(pe)
            out_proj1.tensor(pe)
            turn2.tensor(pe)
            routing.tensor(pe)
            moe1.tensor(pe)
            turn3.tensor(pe)
            proj_u.tensor(pe)
            take_turns(pe, "b" + "ab" * 16, proj_rkv.parts[0], ssm_scan.parts[0])
            beside_rwkv = one_after_other(proj_qkv2.parts[0], proj_gates_tail.parts[0])(pe)
            next(beside_rwkv)
            next(beside_rwkv)
            glu_proj.tensor(pe)
            take_turns(pe, "aaaaabaaabaaaabaabaabababb" + "baaaa", lambda pe: beside_rwkv, rwkv7.parts[0])
            take_turns(pe, ORDER2[0], proj_gates.parts[0], attention2.parts[0])
            merged.tensor(pe)
            out_proj2.tensor(pe)
            turn4.tensor(pe)
            routing2.tensor(pe)
            moe2.tensor(pe)

        @block.vector
        def _(dve):
            norm1.vector(dve)
            turn1.vector(dve)
            ssm_par.vector(dve)
            proj1.vector(dve)
            take_turns(dve, ORDER1[1], proj2.parts[1], attention1.parts[1])
            hgrn2.vector(dve)
            out_proj1.vector(dve)
            norm2.vector(dve)
            turn2.vector(dve)
            routing.vector(dve)
            moe1.vector(dve)
            dve.wait_ge(*count("ssm_tables", 1))
            turn3.vector(dve)
            proj_u.vector(dve)
            ssm_scan.vector(dve)
            glu_proj.vector(dve)
            glu.vector(dve)
            rwkv7.vector(dve)
            take_turns(dve, ORDER2[1], proj_gates.parts[1], attention2.parts[1])
            merged.vector(dve)
            out_proj2.vector(dve)
            norm3.vector(dve)
            turn4.vector(dve)
            routing2.vector(dve)
            moe2.vector(dve)
            norm4.vector(dve)

        @block.scalar
        def _(act):
            norm1.scalar(act)
            ssm_par.scalar(act)
            proj1.scalar(act)
            take_turns(act, ORDER1[2], proj2.parts[2], attention1.parts[2])
            hgrn2.scalar(act)
            norm2.scalar(act)
            routing.scalar(act)
            ssm_tab.scalar(act)
            moe1.scalar(act)
            act.wait_ge(*count("ssm_tables", 1))
            proj_u.scalar(act)
            proj_rkv.vector(act)
            ssm_scan.scalar(act)
            copies_beside = proj_qkv2.parts[1](act)
            next(copies_beside)
            glu_proj.scalar(act)
            glu.scalar(act)
            take_turns(act, "baabbabaabaababbabb", lambda act: copies_beside, rwkv7.parts[2])
            proj_gates_tail.vector(act)
            take_turns(act, ORDER2[2], proj_gates.parts[2], attention2.parts[2])
            merged.scalar(act)
            load_ln_rows(act)
            norm3.scalar(act)
            routing2.scalar(act)
            moe2.scalar(act)
            norm4.scalar(act)

        @block.gpsimd
        def _(pool):
            ssm_tab.gpsimd(pool)
            ssm_scan.gpsimd(pool)

        return cols


def kernel(**inputs):
    import concourse.bacc as bacc
    from concourse.bass_utils import run_bass_kernel_spmd

    def a(name):
        return np.asarray(inputs[name])

    def column(v, n):
        return np.reshape(v, (n, P)).T

    def twice(v):
        return np.reshape(v, (ST, P)).T

    consts, const_at = shape_constants()
    lb = [column(a(n)[r], 4) for n in ("hgrn_lb_fwd", "hgrn_lb_bwd") for r in (0, 1)]
    vectors = {
        "norm1_w": column(a("norm1_w")[0], 8), "norm2_w": column(a("norm2_w")[0], 8),
        "q_w": np.tile(a("attn_q_norm_w")[0], 2)[:, None], "k_w": np.tile(a("attn_k_norm_w")[0], 2)[:, None],
        "lb": np.concatenate(lb, 1), "mu_lora": column(a("rwkv_mu_2")[0, 1536:], 2),
        "a_re": twice(a("ssm_a_re_2")[0]), "a_im": twice(a("ssm_a_im_2")[0]),
        "log_dt": twice(np.repeat(a("ssm_log_dt_2")[0], HD)), "ssm_d": column(a("ssm_d_2")[0], 4),
        "glu_b": column(a("ssm_glu_b_2")[0], 8), "gate_b": column(a("gate_b_2")[0], 24),
    }
    rows = {
        "out_norm_w": a("hgrn_out_norm_w"), "router_b": np.concatenate([a("router_group_b_2"), a("router_expert_b_2")], 1),
        "mu": a("rwkv_mu_2")[:, :1536], "w0": a("rwkv_w0_2"), "a0": a("rwkv_a0_2"), "k_k": a("rwkv_k_k_2"),
        "k_a": a("rwkv_k_a_2"), "r_k": a("rwkv_r_k_2"), "gn_w": a("rwkv_ln_w_2"), "gn_b": a("rwkv_ln_b_2"),
        "ln1_w": a("ln1_w_2"), "ln1_b": a("ln1_b_2"), "ln2_w": a("ln2_w_2"), "ln2_b": a("ln2_b_2"),
    }

    def block_diagonal(v):
        out = np.zeros((2, HD, ST, 2, 16), np.float32)
        for parity in range(2):
            out[parity, :, :, parity, :] = np.transpose(v[parity::2], (1, 0, 2))
        return out.reshape(P, ST * 32)

    b_re, b_im = a("ssm_b_re_2")[0], a("ssm_b_im_2")[0]
    c_re, c_im = (np.transpose(a(n)[0], (0, 2, 1)) for n in ("ssm_c_re_2", "ssm_c_im_2"))
    arrays = {
        "x": a("x")[0], "consts": consts,
        "vectors": np.concatenate([vectors[n] for n, _ in COLUMN_VECTORS], 1),
        "rows": np.concatenate([np.reshape(rows[n], (1, -1)) for n, _ in ROW_VECTORS], 1),
        "ssm_bc": np.concatenate([block_diagonal(v) for v in (b_re, b_im, c_re, c_im)], 1),
        "lora_wa": np.concatenate([a("rwkv_w2_2")[0], a("rwkv_a2_2")[0]], 0), "lora_g": a("rwkv_g2_2")[0],
        "w_router": np.reshape(a("w_router")[0], (KD, P, E1)),
        "w_router_2": np.concatenate([a("router_group_w_2")[0], a("router_expert_w_2")[0]], 1),
    }
    for name in ("w_in", "w_out", "w_expert_gate", "w_expert_up", "w_expert_down", "w_in_2", "ssm_glu_w_2",
                 "w_up_rwkv_2", "w_up_moba_2", "w_up_ssm_2", "w_out_2", "expert_w_gate_2", "expert_w_up_2",
                 "expert_w_down_2"):
        arrays[name] = a(name)[0]
    arrays = {n: np.ascontiguousarray(v) for n, v in arrays.items()}
    nc = bacc.Bacc("TRN2", target_bir_lowering=False, num_devices=1)
    D = {n: nc.dram_tensor("in_" + n, v.shape, F32, kind="ExternalInput").ap() for n, v in arrays.items()}
    D["out"] = nc.dram_tensor("out", (SEQ, DM), F32, kind="ExternalOutput").ap()
    two_blocks(nc, D, const_at)
    r = run_bass_kernel_spmd(nc, [{"in_" + n: v for n, v in arrays.items()}], core_ids=[0])
    return r.results[0]["out"].reshape(1, SEQ, DM)
```
